# Optimizing a Trainium2 kernel written in Bass

```python
import math
import jax, jax.numpy as jnp
from jax import lax
import numpy as np

D_MODEL = 1024
BATCH = 1
SEQ = 256
DEPTH = 1

N_META = 16
D_MIX = 2 * D_MODEL
SSD_HEAD_DIM = 64
SSD_HEADS = 24
D_SSD = SSD_HEADS * SSD_HEAD_DIM
SSD_GROUPS = 4
SSD_STATE = 128
SSD_CONV = 4
SSD_CHUNK = 128
D_XBC = D_SSD + 2 * SSD_GROUPS * SSD_STATE
D_SC = D_MIX - D_SSD
SC_CONV = 3
D_IN = D_SSD + D_XBC + SSD_HEADS + 3 * D_SC
PEER_HEADS = 8
PEER_KEYS = 128
PEER_EXPERTS = PEER_KEYS * PEER_KEYS
PEER_TOPK = 16
PEER_QDIM = 256
PEER_HALF = PEER_QDIM // 2
PEER_BLOCK = 512
EPS = 1e-6


def rmsnorm(x, g):
    xf = x.astype(jnp.float32)
    xf = xf * lax.rsqrt(jnp.mean(xf * xf, axis=-1, keepdims=True) + EPS)
    return (xf * g.astype(jnp.float32)).astype(x.dtype)

def causal_dwconv(x, w):
    width, ch = w.shape
    return lax.conv_general_dilated(
        x, w[:, None, :].astype(x.dtype), window_strides=(1,), padding=[(width - 1, 0)],
        dimension_numbers=('NWC', 'WIO', 'NWC'), feature_group_count=ch)

def segsum(a):
    t = a.shape[-1]
    ar = jnp.broadcast_to(a[..., None], a.shape + (t,))
    ar = jnp.where(jnp.tril(jnp.ones((t, t), bool), -1), ar, 0.0)
    cs = jnp.cumsum(ar, axis=-2)
    return jnp.where(jnp.tril(jnp.ones((t, t), bool), 0), cs, -jnp.inf)

def ssd_scan(x, dt, A, Bm, Cm):
    b, l, h, p = x.shape
    g, n = Bm.shape[2], Bm.shape[3]
    r, q = h // g, SSD_CHUNK
    c = l // q
    xc = x.reshape(b, c, q, g, r, p)
    Bc = Bm.reshape(b, c, q, g, n)
    Cc = Cm.reshape(b, c, q, g, n)
    dtc = dt.reshape(b, c, q, g, r)
    a = (dtc * A.reshape(g, r)).transpose(0, 3, 4, 1, 2)
    x_dt = xc * dtc[..., None]
    a_cs = jnp.cumsum(a, axis=-1)
    decay_in = jnp.exp(segsum(a))
    cb = jnp.einsum('bclgn,bcsgn->bgcls', Cc, Bc)
    y_diag = jnp.einsum('bgcls,bgrcls,bcsgrp->bclgrp', cb, decay_in, x_dt)
    decay_states = jnp.exp(a_cs[..., -1:] - a_cs)
    states = jnp.einsum('bcsgn,bgrcs,bcsgrp->bcgrpn', Bc, decay_states, x_dt)
    states = jnp.concatenate([jnp.zeros_like(states[:, :1]), states], axis=1)
    chunk_a = jnp.pad(a_cs[..., -1], ((0, 0), (0, 0), (0, 0), (1, 0)))
    decay_chunk = jnp.exp(segsum(chunk_a))
    new_states = jnp.einsum('bgrzc,bcgrpn->bzgrpn', decay_chunk, states)
    prev_states = new_states[:, :-1]
    y_off = jnp.einsum('bclgn,bcgrpn,bgrcl->bclgrp', Cc, prev_states, jnp.exp(a_cs))
    return (y_diag + y_off).reshape(b, l, h, p)

def hybrid_mixer(n, w_in, conv_ssd_w, conv_ssd_b, dt_bias, a_log, d_skip, ssd_norm_w,
                 conv_sc_w, w_out):
    bsz, L, _ = n.shape
    proj = n @ w_in.astype(n.dtype)
    s1 = D_SSD
    s2 = s1 + D_XBC
    s3 = s2 + SSD_HEADS
    s4 = s3 + D_SC
    s5 = s4 + D_SC
    z, xbc, dt_raw, sc_b, sc_c, sc_x = jnp.split(proj, [s1, s2, s3, s4, s5], axis=-1)

    xbc = jax.nn.silu(causal_dwconv(xbc, conv_ssd_w) + conv_ssd_b.astype(n.dtype))
    xs, Bm, Cm = jnp.split(xbc, [D_SSD, D_SSD + SSD_GROUPS * SSD_STATE], axis=-1)
    xs_h = xs.reshape(bsz, L, SSD_HEADS, SSD_HEAD_DIM)
    dt = jax.nn.softplus(dt_raw.astype(jnp.float32) + dt_bias.astype(jnp.float32))
    A = -jnp.exp(a_log.astype(jnp.float32))
    pad_len = SSD_CHUNK - N_META

    def lpad(t):
        return jnp.pad(t, ((0, 0), (pad_len, 0)) + ((0, 0),) * (t.ndim - 2))

    y = ssd_scan(lpad(xs_h.astype(jnp.float32)), lpad(dt), A,
                 lpad(Bm.reshape(bsz, L, SSD_GROUPS, SSD_STATE).astype(jnp.float32)),
                 lpad(Cm.reshape(bsz, L, SSD_GROUPS, SSD_STATE).astype(jnp.float32)))
    y = y[:, pad_len:] + d_skip.astype(jnp.float32)[:, None] * xs_h.astype(jnp.float32)
    y = y.reshape(bsz, L, D_SSD) * jax.nn.silu(z.astype(jnp.float32))
    y_ssd = rmsnorm(y.reshape(bsz, L, SSD_GROUPS, D_SSD // SSD_GROUPS),
                    ssd_norm_w.reshape(SSD_GROUPS, D_SSD // SSD_GROUPS))
    y_ssd = y_ssd.reshape(bsz, L, D_SSD).astype(n.dtype)

    y_sc = sc_b * causal_dwconv(sc_c * sc_x, conv_sc_w)

    return jnp.concatenate([y_ssd, y_sc], axis=-1) @ w_out.astype(n.dtype)

def peer_ffn(n, w_q, sub_keys, expert_u, expert_v):
    bsz, L, d = n.shape
    t = n.reshape(-1, d)
    T = t.shape[0]
    q = (t @ w_q.astype(n.dtype)).reshape(T, PEER_HEADS, 2, PEER_HALF)
    s = jnp.einsum('thsd,hskd->thsk', q, sub_keys.astype(n.dtype)).astype(jnp.float32)
    v_half, i_half = lax.top_k(s, PEER_TOPK)
    cand = (v_half[:, :, 0, :, None] + v_half[:, :, 1, None, :]).reshape(T, PEER_HEADS, PEER_TOPK * PEER_TOPK)
    best, pos = lax.top_k(cand, PEER_TOPK)
    i1 = jnp.take_along_axis(i_half[:, :, 0], pos // PEER_TOPK, axis=-1)
    i2 = jnp.take_along_axis(i_half[:, :, 1], pos % PEER_TOPK, axis=-1)
    experts = (i1 * PEER_KEYS + i2).reshape(T, PEER_HEADS * PEER_TOPK)
    gates = jax.nn.softmax(best, axis=-1).reshape(T, PEER_HEADS * PEER_TOPK).astype(n.dtype)

    nb = -(-T // PEER_BLOCK)
    padT = nb * PEER_BLOCK - T
    tp = jnp.pad(t, ((0, padT), (0, 0))).reshape(nb, PEER_BLOCK, d)
    ep = jnp.pad(experts, ((0, padT), (0, 0))).reshape(nb, PEER_BLOCK, -1)
    gp = jnp.pad(gates, ((0, padT), (0, 0))).reshape(nb, PEER_BLOCK, -1)

    def block(args):
        xb, eb, gb = args
        u = expert_u[eb].astype(xb.dtype)
        act = jax.nn.gelu(jnp.einsum('td,tkd->tk', xb, u), approximate=False) * gb
        return jnp.einsum('tk,tkd->td', act, expert_v[eb].astype(xb.dtype))

    out = lax.map(block, (tp, ep, gp))
    return out.reshape(-1, d)[:T].reshape(bsz, L, d)

def first_inputs(seed: int = 0) -> dict:
    key = jax.random.key(seed)
    ks = jax.random.split(key, 20)

    def nrm(k, shape, scale):
        return jax.random.normal(k, shape, jnp.float32) * scale

    x = nrm(ks[0], (BATCH, SEQ, D_MODEL), 1.0)
    meta_tokens = nrm(ks[1], (N_META, D_MODEL), 1.0)
    g_mix = 1.0 + nrm(ks[2], (DEPTH, D_MODEL), 0.05)
    w_in = nrm(ks[3], (DEPTH, D_MODEL, D_IN), D_MODEL ** -0.5)
    conv_ssd_w = nrm(ks[4], (DEPTH, SSD_CONV, D_XBC), SSD_CONV ** -0.5)
    conv_ssd_b = nrm(ks[5], (DEPTH, D_XBC), 0.02)
    dt0 = jnp.exp(jax.random.uniform(ks[6], (DEPTH, SSD_HEADS), jnp.float32,
                                     minval=math.log(1e-3), maxval=math.log(1e-1)))
    dt_bias = dt0 + jnp.log(-jnp.expm1(-dt0))
    a_log = jnp.log(jax.random.uniform(ks[7], (DEPTH, SSD_HEADS), jnp.float32, minval=1.0, maxval=16.0))
    d_skip = 1.0 + nrm(ks[8], (DEPTH, SSD_HEADS), 0.05)
    ssd_norm_w = 1.0 + nrm(ks[9], (DEPTH, D_SSD), 0.05)
    conv_sc_w = nrm(ks[10], (DEPTH, SC_CONV, D_SC), SC_CONV ** -0.5)
    w_out = nrm(ks[11], (DEPTH, D_MIX, D_MODEL), D_MIX ** -0.5)
    g_ffn = 1.0 + nrm(ks[12], (DEPTH, D_MODEL), 0.05)
    w_q = nrm(ks[13], (DEPTH, D_MODEL, PEER_HEADS * PEER_QDIM), D_MODEL ** -0.5)
    sub_keys = nrm(ks[14], (DEPTH, PEER_HEADS, 2, PEER_KEYS, PEER_HALF), PEER_HALF ** -0.5)
    expert_u = nrm(ks[15], (DEPTH, PEER_EXPERTS, D_MODEL), D_MODEL ** -0.5)
    expert_v = nrm(ks[16], (DEPTH, PEER_EXPERTS, D_MODEL), PEER_HEADS ** -0.5)
    g_final = 1.0 + nrm(ks[17], (D_MODEL,), 0.05)
    return {"x": x, "meta_tokens": meta_tokens, "g_mix": g_mix, "w_in": w_in,
            "conv_ssd_w": conv_ssd_w, "conv_ssd_b": conv_ssd_b, "dt_bias": dt_bias,
            "a_log": a_log, "d_skip": d_skip, "ssd_norm_w": ssd_norm_w,
            "conv_sc_w": conv_sc_w, "w_out": w_out, "g_ffn": g_ffn, "w_q": w_q,
            "sub_keys": sub_keys, "expert_u": expert_u, "expert_v": expert_v,
            "g_final": g_final}

def first_block(x, meta_tokens, g_mix, w_in, conv_ssd_w, conv_ssd_b, dt_bias, a_log, d_skip,
              ssd_norm_w, conv_sc_w, w_out, g_ffn, w_q, sub_keys, expert_u, expert_v, g_final):
    bsz = x.shape[0]
    meta = jnp.broadcast_to(meta_tokens[None].astype(x.dtype), (bsz, N_META, D_MODEL))
    h = jnp.concatenate([meta, x], axis=1)
    for l in range(DEPTH):
        h = h + hybrid_mixer(rmsnorm(h, g_mix[l]), w_in[l], conv_ssd_w[l], conv_ssd_b[l],
                             dt_bias[l], a_log[l], d_skip[l], ssd_norm_w[l], conv_sc_w[l], w_out[l])
        h = h + peer_ffn(rmsnorm(h, g_ffn[l]), w_q[l], sub_keys[l], expert_u[l], expert_v[l])
    h = rmsnorm(h, g_final)
    return h[:, N_META:]


DEPTH_2 = 2

N_A_LAYERS = DEPTH_2 // 2
N_B_LAYERS = DEPTH_2 - N_A_LAYERS
HG_EXPAND = 128
HG_HEADS = D_MODEL // HG_EXPAND
HG_DV = D_MODEL // HG_HEADS
HG_CHUNK = 32
ATT_HEAD_DIM = 64
ATT_Q_HEADS = D_MODEL // ATT_HEAD_DIM
ATT_KV_HEADS = 2
ATT_GROUP = ATT_Q_HEADS // ATT_KV_HEADS
WINDOW = 128
D_FF = 2816
CONV_WIDTH = 3


F32 = jnp.float32

def rms_norm(x, g):
    xf = x.astype(F32)
    xf = xf * lax.rsqrt(jnp.mean(xf * xf, axis=-1, keepdims=True) + EPS)
    return (xf * g.astype(F32)).astype(x.dtype)

def alibi_slopes(n_heads):
    return jnp.asarray(2.0 ** (-8.0 * np.arange(1, n_heads + 1) / n_heads), F32)

def hgrn2_chunked(q, k, v, logf):
    b_, s_, h_, dk = q.shape
    dv = v.shape[-1]
    n_chunks = s_ // HG_CHUNK

    def to_chunks(t):
        return t.reshape(b_, n_chunks, HG_CHUNK, h_, t.shape[-1]).transpose(1, 0, 3, 2, 4)

    qc, kc, vc, gc = to_chunks(q), to_chunks(k), to_chunks(v), to_chunks(logf)
    causal = jnp.tril(jnp.ones((HG_CHUNK, HG_CHUNK), bool))[:, :, None]

    def step(state, inp):
        qb, kb, vb, gb = inp
        cum = jnp.cumsum(gb, axis=2)
        o_inter = jnp.einsum('bhtk,bhkv->bhtv', qb * jnp.exp(cum), state)
        rel = cum[:, :, :, None, :] - cum[:, :, None, :, :]
        decay = jnp.exp(jnp.where(causal, rel, -jnp.inf))
        scores = jnp.einsum('bhtk,bhsk,bhtsk->bhts', qb, kb, decay)
        o_intra = jnp.einsum('bhts,bhsv->bhtv', scores, vb)
        last = cum[:, :, -1:, :]
        new_state = (jnp.exp(last[:, :, 0, :])[..., None] * state
                     + jnp.einsum('bhsk,bhsv->bhkv', kb * jnp.exp(last - cum), vb))
        return new_state, o_inter + o_intra

    s0 = jnp.zeros((b_, h_, dk, dv), F32)
    _, o = lax.scan(step, s0, (qc, kc, vc, gc))
    return o.transpose(1, 0, 3, 2, 4).reshape(b_, s_, h_, dv)

def hgrn2_mixer(x, w_in, lower_bound, out_norm, w_out):
    b_, s_, _ = x.shape
    q, f, i, g = jnp.split(x @ w_in, 4, axis=-1)
    q = jax.nn.silu(q.astype(F32)) * HG_EXPAND ** -0.5
    forget = lower_bound + (1.0 - lower_bound) * jax.nn.sigmoid(f.astype(F32))
    logf = jnp.log(forget)
    k = 1.0 - forget
    heads = lambda t: t.reshape(b_, s_, HG_HEADS, -1)
    o = hgrn2_chunked(heads(q), heads(k), heads(i.astype(F32)), heads(logf))
    o = rms_norm(o, out_norm) * jax.nn.silu(heads(g.astype(F32)))
    return o.reshape(b_, s_, D_MODEL).astype(x.dtype) @ w_out

def shared_kv(h, kv_norm, w_kv):
    b_, s_, _ = h.shape
    k, v = jnp.split(rms_norm(h, kv_norm) @ w_kv, 2, axis=-1)
    return (k.reshape(b_, s_, ATT_KV_HEADS, ATT_HEAD_DIM),
            v.reshape(b_, s_, ATT_KV_HEADS, ATT_HEAD_DIM))

def swa_sink_attention(x, k, v, w_q, sinks, w_o):
    b_, s_, _ = x.shape
    nb = s_ // WINDOW
    q = (x @ w_q).reshape(b_, nb, WINDOW, ATT_KV_HEADS, ATT_GROUP, ATT_HEAD_DIM)

    def band(t):
        tb = t.reshape(b_, nb, WINDOW, ATT_KV_HEADS, ATT_HEAD_DIM)
        prev = jnp.pad(tb[:, :-1], ((0, 0), (1, 0), (0, 0), (0, 0), (0, 0)))
        return jnp.concatenate([prev, tb], axis=2)

    kb, vb = band(k), band(v)
    scores = jnp.einsum('bnqkgd,bnskd->bnkgqs', q.astype(F32), kb.astype(F32)) * ATT_HEAD_DIM ** -0.5
    q_idx = jnp.arange(WINDOW)[:, None] + WINDOW
    k_idx = jnp.arange(2 * WINDOW)[None, :]
    dist = q_idx - k_idx
    key_abs = (jnp.arange(nb) * WINDOW)[:, None] + jnp.arange(2 * WINDOW)[None, :] - WINDOW
    valid = ((dist >= 0) & (dist < WINDOW))[None] & (key_abs >= 0)[:, None, :]
    slopes = alibi_slopes(ATT_Q_HEADS).reshape(ATT_KV_HEADS, ATT_GROUP)
    scores = scores - slopes[:, :, None, None] * dist.astype(F32)
    scores = jnp.where(valid[None, :, None, None], scores, -jnp.inf)
    sink = sinks.astype(F32).reshape(ATT_KV_HEADS, ATT_GROUP)[None, None, :, :, None, None]
    m = jnp.maximum(jnp.max(scores, axis=-1, keepdims=True), sink)
    e = jnp.exp(scores - m)
    probs = e / (jnp.sum(e, axis=-1, keepdims=True) + jnp.exp(sink - m))
    out = jnp.einsum('bnkgqs,bnskd->bnqkgd', probs, vb.astype(F32))
    return out.reshape(b_, s_, ATT_Q_HEADS * ATT_HEAD_DIM).astype(x.dtype) @ w_o

def conv_ffn(x, w_up, conv_w, conv_b, w_down):
    s_ = x.shape[1]
    gate, val = jnp.split(x @ w_up, 2, axis=-1)
    gp = jnp.pad(gate, ((0, 0), (CONV_WIDTH - 1, 0), (0, 0)))
    conv = conv_b
    for j in range(CONV_WIDTH):
        conv = conv + conv_w[j] * gp[:, j:j + s_]
    return (jax.nn.silu(conv) * val) @ w_down

def second_inputs(seed: int = 0) -> dict:
    key = jax.random.key(seed)
    ks = jax.random.split(key, 18)
    D = D_MODEL
    HQD = ATT_Q_HEADS * ATT_HEAD_DIM
    KVD = ATT_KV_HEADS * ATT_HEAD_DIM

    def w(k, shape, fan_in):
        return jax.random.normal(k, shape, F32) * fan_in ** -0.5

    def gain(k, shape):
        return 1.0 + 0.02 * jax.random.normal(k, shape, F32)

    return {
        'x': jax.random.normal(ks[0], (BATCH, SEQ, D), F32),
        'hg_norm': gain(ks[1], (N_A_LAYERS, D)),
        'hg_w_in': w(ks[2], (N_A_LAYERS, D, 4 * D), D),
        'hg_lb_logits': 0.1 * jax.random.normal(ks[3], (N_A_LAYERS + 1, D), F32),
        'hg_out_norm': gain(ks[4], (N_A_LAYERS, HG_DV)),
        'hg_w_out': w(ks[5], (N_A_LAYERS, D, D), D),
        'kv_norm': gain(ks[6], (D,)),
        'w_kv': w(ks[7], (D, 2 * KVD), D),
        'attn_norm': gain(ks[8], (N_B_LAYERS, D)),
        'attn_w_q': w(ks[9], (N_B_LAYERS, D, HQD), D),
        'attn_sinks': 0.5 * jax.random.normal(ks[10], (N_B_LAYERS, ATT_Q_HEADS), F32),
        'attn_w_o': w(ks[11], (N_B_LAYERS, HQD, D), HQD),
        'ffn_norm': gain(ks[12], (DEPTH_2, D)),
        'ffn_w_up': w(ks[13], (DEPTH_2, D, 2 * D_FF), D),
        'ffn_conv_w': w(ks[14], (DEPTH_2, CONV_WIDTH, D_FF), CONV_WIDTH),
        'ffn_conv_b': 0.02 * jax.random.normal(ks[15], (DEPTH_2, D_FF), F32),
        'ffn_w_down': w(ks[16], (DEPTH_2, D_FF, D), D_FF),
        'final_norm': gain(ks[17], (D,)),
    }

def second_block(x, hg_norm, hg_w_in, hg_lb_logits, hg_out_norm, hg_w_out, kv_norm, w_kv,
              attn_norm, attn_w_q, attn_sinks, attn_w_o, ffn_norm, ffn_w_up, ffn_conv_w,
              ffn_conv_b, ffn_w_down, final_norm):
    lower_bounds = jnp.cumsum(jax.nn.softmax(hg_lb_logits.astype(F32), axis=0), axis=0)
    h = x
    k_sh, v_sh = None, None
    for layer in range(DEPTH_2):
        if layer < N_A_LAYERS:
            a = layer
            h = h + hgrn2_mixer(rms_norm(h, hg_norm[a]), hg_w_in[a], lower_bounds[a],
                                hg_out_norm[a], hg_w_out[a])
        else:
            bi = layer - N_A_LAYERS
            if bi == 0:
                k_sh, v_sh = shared_kv(h, kv_norm, w_kv)
            h = h + swa_sink_attention(rms_norm(h, attn_norm[bi]), k_sh, v_sh,
                                       attn_w_q[bi], attn_sinks[bi], attn_w_o[bi])
        h = h + conv_ffn(rms_norm(h, ffn_norm[layer]), ffn_w_up[layer], ffn_conv_w[layer],
                         ffn_conv_b[layer], ffn_w_down[layer])
    return rms_norm(h, final_norm)


def setup_inputs(seed=0):
    out = dict(first_inputs(seed))
    for name, value in second_inputs(seed + 1).items():
        if name != "x":
            out[name + "_2"] = value
    return out


def reference(
    x, meta_tokens, g_mix, w_in, conv_ssd_w, conv_ssd_b, dt_bias, a_log, d_skip, ssd_norm_w,
    conv_sc_w, w_out, g_ffn, w_q, sub_keys, expert_u, expert_v, g_final, hg_norm_2, hg_w_in_2,
    hg_lb_logits_2, hg_out_norm_2, hg_w_out_2, kv_norm_2, w_kv_2, attn_norm_2, attn_w_q_2,
    attn_sinks_2, attn_w_o_2, ffn_norm_2, ffn_w_up_2, ffn_conv_w_2, ffn_conv_b_2, ffn_w_down_2,
    final_norm_2,
):
    x = first_block(
        x, meta_tokens, g_mix, w_in, conv_ssd_w, conv_ssd_b, dt_bias, a_log, d_skip, ssd_norm_w,
        conv_sc_w, w_out, g_ffn, w_q, sub_keys, expert_u, expert_v, g_final,
    )
    return second_block(
        x, hg_norm_2, hg_w_in_2, hg_lb_logits_2, hg_out_norm_2, hg_w_out_2, kv_norm_2, w_kv_2,
        attn_norm_2, attn_w_q_2, attn_sinks_2, attn_w_o_2, ffn_norm_2, ffn_w_up_2, ffn_conv_w_2,
        ffn_conv_b_2, ffn_w_down_2, final_norm_2,
    )


_drawn_inputs = setup_inputs


def setup_inputs(seed=0):
    import zlib

    import numpy as np

    out = dict(_drawn_inputs(seed))
    spreads = {}
    factors = {'hg_norm_2': 3.036,
     'hg_lb_logits_2': 7.027,
     'hg_out_norm_2': 5.064,
     'kv_norm_2': 8.0,
     'attn_norm_2': 8.0,
     'attn_sinks_2': 83.793,
     'ffn_norm_2': 2.838,
     'ffn_conv_b_2': 4.368,
     'final_norm_2': 22.842}
    for name, (base, spread) in spreads.items():
        noise = np.random.default_rng([zlib.crc32(name.encode()), seed]).standard_normal(out[name].shape)
        drawn = base * np.exp(spread * noise) if base else spread * noise
        out[name] = __import__('jax').numpy.asarray(drawn.astype(out[name].dtype))
    for name, factor in factors.items():
        out[name] = (out[name] * factor).astype(out[name].dtype)
    return out
```

```python
from contextlib import ExitStack

import numpy as np

import concourse.bass as bass
from concourse import mybir

F32 = mybir.dt.float32
F32R = mybir.dt.float32r
U32 = mybir.dt.uint32
ACT = mybir.ActivationFunctionType
ALU = mybir.AluOpType
AX = mybir.AxisListType

P = 128
D = 1024
KT = D // P
SEQ = 256
TT = SEQ // P
META = 16
TM = META + SEQ
EPS = 1e-6
HEADS, HP, GROUPS, NST = 24, 64, 4, 128
DSSD = HEADS * HP
XS_T = DSSD // P
XBC_T = XS_T + 2 * GROUPS
SC_T = 4
GH = HEADS // GROUPS
GT = DSSD // GROUPS // P
PH, TOPK = 8, 16
KEYS = 128
HG_H = 8
FF_T = 22
ATT_H, ATT_D = 16, 64
NEG = -3.0e38

N_IN = 0
IN_SLABS = 1 + XBC_T + 3 * SC_T + XS_T
N_WOUT = N_IN + IN_SLABS
N_WQ = N_WOUT + 16
N_U = N_WQ + 16
N_V = N_U + KEYS
N_HG = N_V + KEYS
N_HGO = N_HG + 32
N_FF0 = N_HGO + 8
N_ATT = N_FF0 + 3 * FF_T
N_WO = N_ATT + 11
N_FF1 = N_WO + 8
N_SLABS = N_FF1 + 3 * FF_T
RING = 4
AHEAD = 3

VEC = {}


def _vec(name, width):
    VEC[name] = (sum(w for _, w in VEC.values()), width)


for _name, _w in (("g_mix", 8), ("conv_w", 4 * XBC_T), ("conv_b", XBC_T), ("d_skip", XS_T),
                  ("ssd_norm", XS_T), ("sc_w", 3 * SC_T), ("dt_bias", 1), ("a_log", 1), ("g_ffn", 8),
                  ("hg_norm", 8), ("lb_logits", 16), ("ffn_norm0", 8), ("ffn_norm1", 8),
                  ("kv_norm", 8), ("attn_norm", 8), ("fconv_w0", 3 * FF_T), ("fconv_w1", 3 * FF_T),
                  ("fconv_b0", FF_T), ("fconv_b1", FF_T), ("sinks", ATT_H), ("eps", 1), ("one", 1)):
    _vec(_name, _w)
NVEC = sum(w for _, w in VEC.values())

LEVELS = (64, 32, 16, 8, 4, 2, 1, 0)
TAB_TRIU, TAB_DIST, TAB_LEVEL = 0, P, P + 3 * P
NTAB = TAB_LEVEL + len(LEVELS) * P


class Chain:

    def __init__(self, eng, sem):
        self.eng, self.sem, self.n, self.dyn = eng, sem, 0, 0

    def inc(self, ins):
        self.n += 1
        ins.then_inc(self.sem, 1)

    def wait(self):
        self.eng.wait_ge(self.sem, self.dyn + self.n)

    def link(self, ins):
        self.inc(ins)
        self.wait()


def steps(eng, count, unroll, body, chain=None, per=0):
    full = count // unroll
    if full >= 2:
        start = chain.n if chain else 0
        with eng.Fori(0, full) as i:
            for r in range(unroll):
                if chain:
                    chain.dyn = i * (per * unroll)
                    before = chain.n
                body(i, r)
                if chain:
                    assert chain.n - before == per, (chain.n - before, per)
        if chain:
            chain.dyn = 0
            chain.n = start + per * unroll * full
        done = full * unroll
    else:
        done = 0
    for k in range(done, count):
        body(k // unroll, k % unroll)


def build(nc, t):
    ctx = ExitStack()
    with ctx:
        def sb(name, width, dt=F32):
            return ctx.enter_context(nc.sbuf_tensor(name, [P, width], dt))

        def sem(name):
            return ctx.enter_context(nc.semaphore(name))

        raw = sb("raw", RING * 1024)
        whi = sb("whi", RING * 1024, F32R)
        wlo = sb("wlo", RING * 1024, F32R)
        xhi = sb("xhi", KT * TM, F32R)
        xlo = sb("xlo", KT * TM, F32R)
        yhi = sb("yhi", 2 * SEQ, F32R)
        ylo = sb("ylo", 2 * SEQ, F32R)
        h = sb("h", TT * D)
        vec = sb("vec", NVEC)
        ident = sb("ident", P)
        iota = sb("iota", P)
        tiny = sb("tiny", 32)
        arena = sb("arena", 32768)
        bank = [ctx.enter_context(nc.psum_tensor(f"bank{i}", [P, 512], F32)) for i in range(8)]

        def V(name, i=0, n=1):
            o = VEC[name][0]
            if isinstance(i, int):
                return vec[:, o + i:o + i + n]
            return vec[:, bass.ds(i + o, n)]

        class Carve:
            def __init__(self, at=0):
                self.at = at

            def __call__(self, n):
                a = arena[:, self.at:self.at + n]
                self.at += n
                assert self.at <= 32768, self.at
                return a

        raw_ready = [sem(f"raw_ready{i}") for i in range(RING)]
        hi_ready = sem("hi_ready")
        lo_ready = sem("lo_ready")
        slabs_done = sem("slabs_done")
        up_evac = sem("up_evac")
        conv_begun = sem("conv_begun")
        silu_done = sem("silu_done")
        y_new = sem("y_new")
        y_hi = sem("y_hi")
        y_lo = sem("y_lo")
        zeroed = sem("zeroed")
        h_in = sem("h_in")
        vec_in = sem("vec_in")
        tab_in = sem("tab_in")
        act_self, dve_self, pool_self, pe_self = (sem(n) for n in
                                                  ("act_self", "dve_self", "pool_self", "pe_self"))
        ss_done, ms_done, rt_done, rs_done = (sem(n) for n in ("ss_done", "ms_done", "rt_done", "rs_done"))
        nt_done, tr_done, nhi_done, nlo_done = (sem(n) for n in ("nt_done", "tr_done", "nhi_done", "nlo_done"))
        h_done = sem("h_done")
        out_done = sem("out_done")
        S = {}

        def s(name):
            if name not in S:
                S[name] = sem(name)
            return S[name]

        block = ctx.enter_context(nc.Block())

        def slot(n0, r):
            return (n0 + r) % RING

        def at(n0, i, r, U):
            return n0 + r + i * U

        def rounds(n0, i, r, U):
            return (n0 + r) // RING + i * (U // RING)

        def load(sp, n0, i, r, U):
            if n0 + r >= RING:
                sp.wait_ge(lo_ready, at(n0, i, r, U) - RING + 1)
            q = slot(n0, r)
            n = at(n0, i, r, U)
            src = t["stream"][n] if isinstance(n, int) else \
                t["stream"][bass.ds(n, 1)].rearrange("a p c -> (a p) c")
            sp.dma_start(raw[:, q * 1024:(q + 1) * 1024], src).then_inc(raw_ready[q], 16)

        def split_hi(act, n0, i, r, U):
            if isinstance(i, int) and at(n0, i, r, U) >= N_SLABS:
                return
            q = slot(n0, r)
            act.wait_ge(raw_ready[q], (rounds(n0, i, r, U) + 1) * 16)
            act.wait_ge(slabs_done, at(n0, i, r, U) + 1)
            nc.scalar.activation(whi[:, q * 1024:(q + 1) * 1024], raw[:, q * 1024:(q + 1) * 1024],
                                 ACT.Copy).then_inc(hi_ready, 1)

        def split_lo(dve, n0, i, r, U):
            if isinstance(i, int) and at(n0, i, r, U) >= N_SLABS:
                return
            q = slot(n0, r)
            dve.wait_ge(hi_ready, at(n0, i, r, U) + 1)
            nc.vector.tensor_tensor(wlo[:, q * 1024:(q + 1) * 1024], raw[:, q * 1024:(q + 1) * 1024],
                                    whi[:, q * 1024:(q + 1) * 1024].bitcast(F32), ALU.subtract)\
                .then_inc(lo_ready, 1)

        def up(pe, n0, u0, i, r, U, T, t0=0, Tall=SEQ, uU=None, between=None):
            n, u = at(n0, i, r, U), at(u0, i, r, U if uU is None else uU)
            q, b = slot(n0, r), (u0 + r) % 2
            pe.wait_ge(lo_ready, n + 1)
            pe.wait_ge(up_evac, u + 1)
            for k in range(KT):
                w = slice(q * 1024 + k * P, q * 1024 + (k + 1) * P)
                x = slice(k * Tall + t0, k * Tall + t0 + T)
                nc.tensor.matmul(bank[b][:, 0:T], whi[:, w], xhi[:, x], start=k == 0, stop=False)
                nc.tensor.matmul(bank[b][:, 0:T], whi[:, w], xlo[:, x], start=False, stop=False)
                last = nc.tensor.matmul(bank[b][:, 0:T], wlo[:, w], xhi[:, x], start=False,
                                        stop=k == KT - 1)
                if between and k == KT // 2 - 1:
                    between()
            last.then_inc(slabs_done, 1)

        def up_tokens(pe, n0, u0, i, r, U):
            n, u = at(n0, i, r, U), at(u0, i, r, U)
            q, b = slot(n0, r), (u0 + r) % 2
            pe.wait_ge(lo_ready, n + 1)
            pe.wait_ge(up_evac, u + 1)
            for tt in range(TT):
                for k in range(KT):
                    w = slice(q * 1024 + k * P, q * 1024 + (k + 1) * P)
                    x = slice(k * SEQ + tt * P, k * SEQ + (tt + 1) * P)
                    o = bank[b][:, tt * P:(tt + 1) * P]
                    nc.tensor.matmul(o, xhi[:, x], whi[:, w], start=k == 0, stop=False)
                    nc.tensor.matmul(o, xlo[:, x], whi[:, w], start=False, stop=False)
                    last = nc.tensor.matmul(o, xhi[:, x], wlo[:, w], start=False, stop=k == KT - 1)
            last.then_inc(slabs_done, 1)

        def clear_accumulators(pe, d_stage):
            for b in range(4, 8):
                last = nc.tensor.matmul(bank[b][:, :], tiny[0:1, 31:32].to_broadcast([1, P]),
                                        tiny[0:1, 31:32].to_broadcast([1, 512]),
                                        start=True, stop=True)
            last.then_inc(zeroed, 1)
            pe.wait_ge(zeroed, d_stage + 1)

        def down(pe, n0, d0, i, r, U, dU=None, dr=None):
            dU, dr = (U if dU is None else dU), (r if dr is None else dr)
            n, d = at(n0, i, r, U), at(d0, i, dr, dU)
            q, yq = slot(n0, r), (d0 + dr) % 2
            pe.wait_ge(lo_ready, n + 1)
            pe.wait_ge(y_lo, d + 1)
            for tt in range(TT):
                y = slice(yq * SEQ + tt * P, yq * SEQ + (tt + 1) * P)
                for nh in range(2):
                    o = bank[4 + 2 * tt + nh][:, :]
                    w = slice(q * 1024 + nh * 512, q * 1024 + (nh + 1) * 512)
                    nc.tensor.matmul(o, yhi[:, y], whi[:, w], start=False, stop=False, skip_group_check=True)
                    nc.tensor.matmul(o, yhi[:, y], wlo[:, w], start=False, stop=False, skip_group_check=True)
                    last = nc.tensor.matmul(o, ylo[:, y], whi[:, w], start=False, stop=True,
                                            skip_group_check=True)
            last.then_inc(slabs_done, 1)

        U_IN, U_WQ = 0, IN_SLABS
        U_U = U_WQ + 16
        U_HG = U_U + KEYS
        U_FF0 = U_HG + 32
        U_ATT = U_FF0 + 2 * FF_T
        U_FF1 = U_ATT + 11
        D_WOUT = 0
        D_V = 16
        D_HGO = D_V + KEYS
        D_FF0 = D_HGO + 8
        D_WO = D_FF0 + FF_T
        D_FF1 = D_WO + 8
        ADDS = ("wout", "v", "hgo", "ff0", "wo", "ff1")

        def ss_count(r):
            return 0 if r == 0 else 3 + 2 * (r - 1)

        NQ = {0: 0, 1: 1, 3: 2, 4: 3, 5: 4, 6: 5}

        def nt_base(r):
            q = NQ[r]
            return 0 if q == 0 else 3 + 2 * (q - 1)

        def bank_base(r):
            q = NQ[r]
            return 0 if q == 0 else 8 + 4 * (q - 1) + (4 if q > 4 else 0)

        meta_x = arena[:, 0:D]
        nt = arena[:, D:4 * D]
        junk = arena[:, 4 * D:7 * D]
        SS, MS, RT, RS = (tiny[:, 3 * i:3 * i + 3] for i in range(4))

        def tiles_of(r):
            return [(0, P), (1, P)] + ([(2, META)] if r == 0 else [])

        def norm_act_sums(act, r):
            for tt, n in tiles_of(r):
                src = h[0:n, tt * D:(tt + 1) * D] if tt < 2 else meta_x[0:n, :]
                nc.scalar.activation(junk[0:n, tt * D:(tt + 1) * D], src, ACT.Square,
                                     accum_out=SS[0:n, tt:tt + 1]).then_inc(ss_done, 1)
            w = len(tiles_of(r))
            act.wait_ge(ms_done, r + 1)
            nc.scalar.activation(RT[:, 0:w], MS[:, 0:w], ACT.Sqrt).then_inc(rt_done, 1)

        def norm_dve_scale(dve, r):
            w = len(tiles_of(r))
            dve.wait_ge(ss_done, ss_count(r + 1))
            nc.vector.tensor_scalar(MS[:, 0:w], SS[:, 0:w], 1.0 / D, EPS, ALU.mult, ALU.add)\
                .then_inc(ms_done, 1)
            dve.wait_ge(rt_done, r + 1)
            nc.vector.reciprocal(RS[:, 0:w], RT[:, 0:w]).then_inc(rs_done, 1)

        def norm_dve_tokens(dve, r):
            dve.wait_ge(rs_done, r + 1)
            for tt, n in tiles_of(r):
                if tt != 1:
                    src = h[0:n, 0:D] if tt < 2 else meta_x[0:n, :]
                    nc.vector.tensor_scalar(nt[0:n, tt * D:(tt + 1) * D], src, RS[0:n, tt:tt + 1], None,
                                            ALU.mult).then_inc(nt_done, 1)

        def norm_act_tokens(act, r):
            act.wait_ge(rs_done, r + 1)
            nc.scalar.activation(nt[:, D:2 * D], h[:, D:2 * D], ACT.Copy, scale=RS[:, 1:2])\
                .then_inc(nt_done, 1)

        def norm_pe(pe, r):
            pe.wait_ge(nt_done, nt_base(r) + len(tiles_of(r)))
            for j in range(KT):
                if r == 0:
                    o, m = bank[j], META
                    nc.tensor.transpose(o[:, 0:META], nt[0:META, 2 * D + j * P:2 * D + (j + 1) * P],
                                        ident[0:META, 0:META])
                    base = META
                else:
                    o, base = bank[4 + j // 2], (j % 2) * SEQ
                for tt in range(TT):
                    last = nc.tensor.transpose(o[:, base + tt * P:base + (tt + 1) * P],
                                               nt[:, tt * D + j * P:tt * D + (j + 1) * P], ident[:, :])
                if r == 0 or j % 2:
                    last.then_inc(tr_done, 1)

        def tr_base(r):
            q = NQ[r]
            return 0 if q == 0 else 8 + 4 * (q - 1)

        def norm_tiles(r):
            T = TM if r == 0 else SEQ
            for j in range(KT):
                src = bank[j][:, 0:TM] if r == 0 else bank[4 + j // 2][:, (j % 2) * SEQ:(j % 2 + 1) * SEQ]
                yield j, src, slice(j * T, (j + 1) * T), (j if r == 0 else j // 2), (r == 0 or j % 2 == 1)

        def norm_act_hi(act, r, gain, again=0):
            for j, src, x, b, ends in norm_tiles(r):
                act.wait_ge(tr_done, tr_base(r) + b + 1)
                ins = nc.scalar.activation(xhi[:, x], src, ACT.Copy, scale=V(gain, j))
                if ends:
                    ins.then_inc(nhi_done, 1)

        def norm_dve_lo(dve, r, gain, again=0):
            for j, src, x, b, ends in norm_tiles(r):
                dve.wait_ge(nhi_done, bank_base(r) + 4 * again + b + 1)
                nc.vector.scalar_tensor_tensor(out=xlo[:, x], in0=src, scalar=V(gain, j),
                                               in1=xhi[:, x].bitcast(F32), op0=ALU.mult,
                                               op1=ALU.subtract).then_inc(nlo_done, 1)

        def nlo_total(r, again=0):
            q = NQ[r]
            return 8 * (q + 1) + (8 if q > 4 else 0) + 8 * again

        def add_dve(dve, name, n_last):
            dve.wait_ge(slabs_done, n_last + 1 + RING)
            for b in range(4):
                nc.vector.tensor_tensor(h[:, b * 512:(b + 1) * 512], h[:, b * 512:(b + 1) * 512],
                                        bank[4 + b][:, :], ALU.add).then_inc(h_done, 1)

        def h_count(name):
            return 4 * (ADDS.index(name) + 1)

        def y_act(act, n0, d0, i, r, U, src, prev):
            d = at(d0, i, r, U)
            yq = (d0 + r) % 2
            act.wait_ge(slabs_done, at(n0, i, r, U) - prev + 1 + RING)
            nc.scalar.activation(yhi[:, yq * SEQ:(yq + 1) * SEQ], src, ACT.Copy).then_inc(y_hi, 1)

        def y_dve(dve, d0, i, r, U, src):
            yq = (d0 + r) % 2
            dve.wait_ge(y_hi, at(d0, i, r, U) + 1)
            nc.vector.tensor_tensor(ylo[:, yq * SEQ:(yq + 1) * SEQ], src,
                                    yhi[:, yq * SEQ:(yq + 1) * SEQ].bitcast(F32), ALU.subtract)\
                .then_inc(y_lo, 1)

        def col(ap, i, r, U, width=SEQ):
            k = i * U + r
            return ap[:, k * width:(k + 1) * width] if isinstance(k, int) else ap[:, bass.ds(k * width, width)]

        c = Carve(0)
        XBC = c(XBC_T * TM)
        ZS = c(XS_T * SEQ)
        Y = c(16 * SEQ)
        CV = c(2 * TM)
        SCC = c(TM)
        PR = c(TM)
        DTR, DTA, DTE, DTT, AT, ACS, DST = (c(TM) for _ in range(7))
        XDT = c(3 * DSSD)
        XDD = c(2 * DSSD)
        BTOK = c(2 * GROUPS * NST)
        S0 = c(DSSD)
        S1 = c(DSSD)
        DD = c(2 * 384)
        EE = c(2 * 384)
        LL = c(2 * 384)
        MM = c(2 * 384)
        CE = c(2 * 384)
        CBM = c(2 * P)
        TOK = c(7 * HEADS)
        ELB = c(HEADS)
        LDG = c(HEADS)
        TRI = c(P)
        EA = c(1)
        assert c.at <= 32768
        CHUNK = (slice(0, META), slice(META, META + P), slice(META + P, TM))
        CW = (META, P, P)

        def xbc(k):
            return XBC[:, k * TM:(k + 1) * TM]

        def dve_setup(dve, chain):
            nc.vector.memset(tiny[:, :], 0.0).then_inc(s("setup"), 1)
            dve.wait_ge(s("setup"), 1)

        def pe_in_proj(pe):
            norm_pe(pe, 0)
            pe.wait_ge(nlo_done, nlo_total(0))
            steps(pe, 1 + XBC_T + 3, 4, lambda i, r: up(pe, 0, 0, i, r, 4, TM, 0, TM))
            for n in range(1 + XBC_T + 3, 1 + XBC_T + 3 * SC_T):
                up(pe, n, n, 0, 0, 4, TM, 0, TM)
            n0 = 1 + XBC_T + 3 * SC_T
            steps(pe, XS_T, 4, lambda i, r: up(pe, n0, n0, i, r, 4, SEQ, META, TM))

        def act_in_proj(act, chain):
            act.wait_ge(h_in, 32)
            act.wait_ge(vec_in, 48)
            act.wait_ge(s("setup"), 1)
            norm_act_sums(act, 0)
            norm_act_tokens(act, 0)
            norm_act_hi(act, 0, "g_mix")
            split_hi(act, AHEAD, 0, 0, 4)

            def first(n0, i, r):
                n = at(n0, i, r, 4)
                act.wait_ge(slabs_done, n + 1 + RING)
                act.wait_ge(silu_done, n)
                b = (n0 + r) % 2
                nc.scalar.activation(CV[:, b * TM:(b + 1) * TM], bank[b][:, 0:TM], ACT.Identity,
                                     scale=V("conv_w", (n - 1) * 4 + 3), bias=V("conv_b", n - 1))\
                    .then_inc(conv_begun, 1)

            def silu(n0, i, r):
                n = at(n0, i, r, 4)
                act.wait_ge(up_evac, n + 1 + 2)
                b = (n0 + r) % 2
                dst = xbc(n - 1) if isinstance(n, int) else XBC[:, bass.ds((n - 1) * TM, TM)]
                nc.scalar.activation(dst, CV[:, b * TM:(b + 1) * TM], ACT.Silu).then_inc(silu_done, 1)

            split_hi(act, 1 + AHEAD, 0, 0, 4)
            first(1, 0, 0)

            def step(i, r):
                split_hi(act, 2 + AHEAD, i, r, 4)
                first(2, i, r)
                silu(1, i, r)

            steps(act, XBC_T - 1, 4, step)
            silu(XBC_T, 0, 0)
            for j in range(SC_T):
                n = 1 + XBC_T + 3 * j
                split_hi(act, n + AHEAD, 0, 0, 4)
                act.wait_ge(slabs_done, n + 1 + RING)
                act.wait_ge(up_evac, n + 2)
                if j:
                    act.wait_ge(s("sc_prod"), j)
                nc.scalar.activation(SCC, bank[n % 2][:, 0:TM], ACT.Copy).then_inc(up_evac, 1)
                split_hi(act, n + 1 + AHEAD, 0, 0, 4)
                split_hi(act, n + 2 + AHEAD, 0, 0, 4)
            n0 = 1 + XBC_T + 3 * SC_T

            def z_step(i, r):
                split_hi(act, n0 + AHEAD, i, r, 4)
                act.wait_ge(slabs_done, at(n0, i, r, 4) + 1 + RING)
                nc.scalar.activation(col(ZS, i, r, 4), bank[(n0 + r) % 2][:, 0:SEQ], ACT.Silu)\
                    .then_inc(up_evac, 1)

            act.wait_ge(up_evac, n0 + 2)
            steps(act, XS_T, 4, z_step)

        def dve_in_proj(dve, chain):
            dve.wait_ge(vec_in, 48)
            norm_dve_scale(dve, 0)
            norm_dve_tokens(dve, 0)
            norm_dve_lo(dve, 0, "g_mix")
            split_lo(dve, AHEAD, 0, 0, 4)
            dve.wait_ge(slabs_done, 1 + RING)
            nc.vector.tensor_scalar(DTR[0:HEADS, :], bank[0][0:HEADS, 0:TM], V("dt_bias")[0:HEADS, :], None,
                                    ALU.add).then_inc(up_evac, 1)

            def conv(i, r):
                n = at(1, i, r, 4)
                b = (1 + r) % 2
                split_lo(dve, 1 + AHEAD, i, r, 4)
                dve.wait_ge(conv_begun, n)
                for sh in (1, 2, 3):
                    ins = nc.vector.scalar_tensor_tensor(
                        out=CV[:, b * TM + sh:(b + 1) * TM], in0=bank[b][:, 0:TM - sh],
                        scalar=V("conv_w", (n - 1) * 4 + 3 - sh), in1=CV[:, b * TM + sh:(b + 1) * TM],
                        op0=ALU.mult, op1=ALU.add)
                    if sh < 3:
                        chain.link(ins)
                ins.then_inc(up_evac, 1)

            steps(dve, XBC_T, 4, conv, chain, 2)
            for j in range(SC_T):
                n = 1 + XBC_T + 3 * j
                split_lo(dve, n + AHEAD, 0, 0, 4)
                split_lo(dve, n + 1 + AHEAD, 0, 0, 4)
                dve.wait_ge(slabs_done, n + 2 + RING)
                dve.wait_ge(up_evac, n + 1 + 2)
                chain.inc(nc.vector.tensor_tensor(PR, bank[(n + 1) % 2][:, 0:TM], SCC, ALU.mult))
                chain.wait()
                nc.vector.tensor_scalar(CV[:, 0:SEQ], PR[:, META:TM], V("sc_w", 3 * j + 2), None, ALU.mult)\
                    .then_inc(up_evac, 1)
                dve.wait_ge(up_evac, n + 2 + 2)
                chain.link(nc.vector.scalar_tensor_tensor(
                    out=CV[:, 0:SEQ], in0=PR[:, META - 1:TM - 1], scalar=V("sc_w", 3 * j + 1),
                    in1=CV[:, 0:SEQ], op0=ALU.mult, op1=ALU.add))
                nc.vector.scalar_tensor_tensor(
                    out=CV[:, 0:SEQ], in0=PR[:, META - 2:TM - 2], scalar=V("sc_w", 3 * j),
                    in1=CV[:, 0:SEQ], op0=ALU.mult, op1=ALU.add).then_inc(s("sc_prod"), 1)
                dve.wait_ge(s("sc_prod"), j + 1)
                split_lo(dve, n + 2 + AHEAD, 0, 0, 4)
                dve.wait_ge(slabs_done, n + 3 + RING)
                nc.vector.tensor_tensor(Y[:, (XS_T + j) * SEQ:(XS_T + j + 1) * SEQ], CV[:, 0:SEQ],
                                        bank[(n + 2) % 2][:, META:TM], ALU.mult).then_inc(up_evac, 1)
            n0 = 1 + XBC_T + 3 * SC_T
            steps(dve, XS_T, 4, lambda i, r: split_lo(dve, n0 + AHEAD, i, r, 4))

        DT_TOK, DS_TOK, AC_TOK = (0, 1, 2), (3, 4), (None, 5, 6)

        def tok(i, c):
            return TOK[0:CW[c], i * HEADS:(i + 1) * HEADS]

        def dve_ssd(dve, chain):
            a = slice(0, HEADS)
            chain.link(nc.vector.scalar_tensor_tensor(out=DTA[a, :], in0=DTR[a, :], scalar=-1.0,
                                                      in1=DTR[a, :], op0=ALU.mult, op1=ALU.min))
            nc.vector.memset(EA[:, :], 1.0).then_inc(s("dt_abs"), 1)
            dve.wait_ge(s("dt_ln"), 2)
            chain.link(nc.vector.scalar_tensor_tensor(out=DTT[a, :], in0=DTR[a, :], scalar=0.0,
                                                      in1=DTE[a, :], op0=ALU.max, op1=ALU.add))
            chain.link(nc.vector.tensor_scalar(AT[a, :], DTT[a, :], DTA[a, 0:1], -1.0, ALU.mult, ALU.mult))
            for c in range(3):
                ins = nc.vector.tensor_tensor_scan(ACS[a, CHUNK[c]], V("one")[a, :].to_broadcast([HEADS, CW[c]]),
                                                   AT[a, CHUNK[c]], 0.0, ALU.mult, ALU.add)
                chain.inc(ins)
            chain.wait()
            nc.vector.tensor_scalar(LDG[a, :], ident[a, 0:HEADS], ACS[a, META + P - 1:META + P], None,
                                    ALU.mult).then_inc(s("acs"), 1)
            dve.wait_ge(s("tok_tr"), 1)
            nc.vector.tensor_copy(TOK[0:META, 0:HEADS], bank[2][0:META, 0:HEADS]).then_inc(s("tok"), 1)
            nc.vector.tensor_copy(TOK[0:META, 3 * HEADS:4 * HEADS], bank[2][0:META, 3 * HEADS:4 * HEADS])\
                .then_inc(s("tok"), 1)
            for i in (1, 2, 4, 5, 6):
                nc.vector.tensor_copy(TOK[:, i * HEADS:(i + 1) * HEADS], bank[2][:, i * HEADS:(i + 1) * HEADS])\
                    .then_inc(s("tok"), 1)
            dve.wait_ge(s("tok"), 7)
            for j in range(9):
                c, b = j // 3, j % 3
                n = CW[c]
                dve.wait_ge(s("x_tr"), j + 1)
                nc.vector.tensor_tensor(
                    XDT[0:n, c * DSSD + b * 512:c * DSSD + (b + 1) * 512].rearrange("p (h d) -> p h d", d=HP),
                    bank[3 + j % 3][0:n, :].rearrange("p (h d) -> p h d", d=HP),
                    tok(DT_TOK[c], c)[:, b * 8:(b + 1) * 8].unsqueeze(2).to_broadcast([n, 8, HP]),
                    ALU.mult).then_inc(s("xdt"), 1)
            for g in range(GROUPS):
                gs = slice(g * 384, (g + 1) * 384)
                dve.wait_ge(s("s0e"), 1)
                dve.wait_ge(s("st_mm"), GROUPS + g + 1)
                nc.vector.tensor_tensor(S1[:, gs], S1[:, gs], bank[2 + g][:, 0:384], ALU.add)\
                    .then_inc(s("s1"), 1)
            for c in (1, 2):
                for g in range(GROUPS):
                    m = (c - 1) * GROUPS + g
                    dve.wait_ge(s("cb"), m + 1)
                    if m >= 2:
                        dve.wait_ge(s("y_mm"), m - 1)
                    nc.vector.tensor_tensor(CBM[:, (m % 2) * P:(m % 2 + 1) * P], bank[4][:, 0:P], TRI, ALU.mult)\
                        .then_inc(s("cbm"), 1)
                    for hh in range(2):
                        k = 2 * m + hh
                        q = slice((k % 2) * 384, (k % 2 + 1) * 384)
                        dve.wait_ge(s("ee"), k + 1)
                        for x in range(3):
                            hd = g * GH + hh * 3 + x
                            ins = nc.vector.tensor_scalar(
                                DD[:, q][:, x * P:(x + 1) * P], bank[2 + k % 2][:, x * P:(x + 1) * P],
                                tok(AC_TOK[c], c)[:, hd:hd + 1], 0.0, ALU.subtract, ALU.min)
                            ins.then_inc(s("dd"), 1)
                        dve.wait_ge(s("ll"), k + 1)
                        if hh == 0:
                            dve.wait_ge(s("cbm"), m + 1)
                        if k >= 2:
                            dve.wait_ge(s("y_half"), k - 1)
                        nc.vector.tensor_tensor(
                            MM[:, q].rearrange("p (x l) -> p x l", l=P), LL[:, q].rearrange("p (x l) -> p x l", l=P),
                            CBM[:, (m % 2) * P:(m % 2 + 1) * P].unsqueeze(1).to_broadcast([P, 3, P]), ALU.mult)\
                            .then_inc(s("mm"), 1)
                    dve.wait_ge(s("y_mm"), m + 1)
                    for x in range(GT):
                        k = g * GT + x
                        nc.vector.scalar_tensor_tensor(
                            out=Y[:, k * SEQ + (c - 1) * P:k * SEQ + c * P],
                            in0=xbc(k)[:, CHUNK[c]], scalar=V("d_skip", k),
                            in1=bank[5 + m % 2][:, x * P:(x + 1) * P],
                            op0=ALU.mult, op1=ALU.add).then_inc(s("y_out"), 1)
            for g in range(GROUPS):
                dve.wait_ge(s("g_rt"), g + 1)
                R = EE[:, (g % 2) * 256:(g % 2 + 1) * 256]
                chain.link(nc.vector.reciprocal(MM[:, (g % 2) * 256:(g % 2 + 1) * 256], R))
                for x in range(GT):
                    k = g * GT + x
                    y = Y[:, k * SEQ:(k + 1) * SEQ]
                    nc.vector.scalar_tensor_tensor(out=y, in0=y, scalar=V("ssd_norm", k),
                                                   in1=MM[:, (g % 2) * 256:(g % 2 + 1) * 256],
                                                   op0=ALU.mult, op1=ALU.mult).then_inc(s("y_normed"), 1)

        def act_ssd(act, chain):
            a = slice(0, HEADS)
            act.wait_ge(s("dt_abs"), 1)
            chain.link(nc.scalar.activation(DTE[a, :], DTA[a, :], ACT.Exp))
            nc.scalar.activation(DTE[a, :], DTE[a, :], ACT.Ln, bias=V("one")[a, :]).then_inc(s("dt_ln"), 1)
            act.wait_ge(s("dt_ln"), 1)
            nc.scalar.activation(DTA[a, 0:1], V("a_log")[a, :], ACT.Exp).then_inc(s("dt_ln"), 1)
            act.wait_ge(s("acs"), 1)
            for c in (0, 1):
                last = ACS[a, CHUNK[c].stop - 1:CHUNK[c].stop]
                nc.scalar.activation(DST[a, CHUNK[c]], ACS[a, CHUNK[c]], ACT.Exp, scale=-1.0, bias=last)\
                    .then_inc(s("dst"), 1)
            act.wait_ge(s("elb_mm"), 1)
            nc.scalar.activation(ELB, bank[7][:, 0:HEADS], ACT.Exp).then_inc(s("elb"), 1)
            for c in (0, 1):
                act.wait_ge(s("b_tr"), c + 1)
                nc.scalar.activation(BTOK[0:CW[c], c * 512:(c + 1) * 512], bank[6 + c][0:CW[c], :], ACT.Copy)\
                    .then_inc(s("btok"), 1)
            for g in range(GROUPS):
                act.wait_ge(s("st_mm"), g + 1)
                nc.scalar.activation(S0[:, g * 384:(g + 1) * 384], bank[2 + g][:, 0:384], ACT.Copy)\
                    .then_inc(s("s0"), 1)
            for k in range(4 * GROUPS):
                q = slice((k % 2) * 384, (k % 2 + 1) * 384)
                act.wait_ge(s("rr"), k + 1)
                if k >= 2:
                    act.wait_ge(s("ce"), k - 1)
                nc.scalar.activation(EE[:, q], bank[2 + k % 2][:, 0:384], ACT.Exp).then_inc(s("ee"), 1)
                act.wait_ge(s("dd"), 3 * (k + 1))
                if k >= 2:
                    act.wait_ge(s("mm"), k - 1)
                nc.scalar.activation(LL[:, q], DD[:, q], ACT.Exp).then_inc(s("ll"), 1)
            for g in range(GROUPS):
                act.wait_ge(s("y_gated"), 6 * GROUPS)
                nc.scalar.activation(XDT[:, g * 768:(g + 1) * 768], Y[:, g * 768:(g + 1) * 768], ACT.Square)\
                    .then_inc(s("y_sq"), 1)
            for g in range(GROUPS):
                act.wait_ge(s("g_mm"), g + 1)
                if g >= 2:
                    act.wait_ge(s("y_normed"), 3 * (g - 1))
                nc.scalar.activation(EE[:, (g % 2) * 256:(g % 2 + 1) * 256], bank[2 + g][:, 0:SEQ], ACT.Sqrt,
                                     scale=1.0 / (GT * P), bias=V("eps")).then_inc(s("g_rt"), 1)

        def pe_ssd(pe):
            a = slice(0, HEADS)
            i24 = ident[a, 0:HEADS]
            pe.wait_ge(s("dst"), 2)
            pe.wait_ge(up_evac, IN_SLABS + 2)
            for i, (src, c) in enumerate(((DTT, 0), (DTT, 1), (DTT, 2), (DST, 0), (DST, 1), (ACS, 1), (ACS, 2))):
                last = nc.tensor.transpose(bank[2][0:CW[c], i * HEADS:(i + 1) * HEADS], src[a, CHUNK[c]], i24)
            last.then_inc(s("tok_tr"), 1)
            nc.tensor.matmul(bank[7][:, 0:HEADS], V("one")[a, :].to_broadcast([HEADS, P]), LDG[a, :],
                             start=True, stop=True).then_inc(s("elb_mm"), 1)
            pe.wait_ge(s("elb"), 1)
            for c in (0, 1):
                for g in range(GROUPS):
                    last = nc.tensor.transpose(bank[6 + c][0:CW[c], g * P:(g + 1) * P],
                                               xbc(XS_T + g)[:, CHUNK[c]], ident[:, :])
                last.then_inc(s("b_tr"), 1)
            for j in range(9):
                c, b = j // 3, j % 3
                if j >= 3:
                    pe.wait_ge(s("xdt"), j - 2)
                for x in range(4):
                    last = nc.tensor.transpose(bank[3 + j % 3][0:CW[c], x * P:(x + 1) * P],
                                               xbc(4 * b + x)[:, CHUNK[c]], ident[:, :])
                last.then_inc(s("x_tr"), 1)
            pe.wait_ge(s("btok"), 2)
            pe.wait_ge(s("xdt"), 9)
            pe.wait_ge(s("xdd"), 6)
            for c in (0, 1):
                n = CW[c]
                for g in range(GROUPS):
                    if c:
                        pe.wait_ge(s("s0"), g + 1)
                    nc.tensor.matmul(bank[2 + g][:, 0:384], BTOK[0:n, c * 512 + g * P:c * 512 + (g + 1) * P],
                                     XDD[0:n, c * DSSD + g * 384:c * DSSD + (g + 1) * 384],
                                     start=True, stop=True).then_inc(s("st_mm"), 1)

            def half_r(k):
                c, g, hh = 1 + k // 8, (k // 2) % 4, k % 2
                if k >= 2:
                    pe.wait_ge(s("dd"), 3 * (k - 1))
                else:
                    pe.wait_ge(s("s1"), GROUPS)
                for x in range(3):
                    hd = g * GH + hh * 3 + x
                    last = nc.tensor.matmul(bank[2 + k % 2][:, x * P:(x + 1) * P],
                                            ident[a, hd:hd + 1].to_broadcast([HEADS, P]), ACS[a, CHUNK[c]],
                                            start=True, stop=True)
                last.then_inc(s("rr"), 1)

            def cb(m):
                c, g = 1 + m // 4, m % 4
                if m:
                    pe.wait_ge(s("cbm"), m)
                nc.tensor.matmul(bank[4][:, 0:P], xbc(XS_T + g)[:, CHUNK[c]], xbc(XS_T + GROUPS + g)[:, CHUNK[c]],
                                 start=True, stop=True).then_inc(s("cb"), 1)

            half_r(0)
            cb(0)
            for k in range(4 * GROUPS):
                m, hh = k // 2, k % 2
                c, g = 1 + m // 4, m % 4
                if k + 1 < 4 * GROUPS:
                    half_r(k + 1)
                if hh and m + 1 < 2 * GROUPS:
                    cb(m + 1)
                pe.wait_ge(s("mm"), k + 1)
                pe.wait_ge(s("ce"), k + 1)
                if hh == 0 and m >= 2:
                    pe.wait_ge(s("y_out"), 3 * (m - 1))
                for x in range(3):
                    hd = g * GH + hh * 3 + x
                    po = (hd % 2) * HP
                    tile = (hd - g * GH) // 2
                    o = bank[5 + m % 2][po:po + HP, tile * P:(tile + 1) * P]
                    q = slice((k % 2) * 384 + x * P, (k % 2) * 384 + (x + 1) * P)
                    state = S0 if c == 1 else S1
                    nc.tensor.matmul(o, XDT[:, c * DSSD + hd * HP:c * DSSD + (hd + 1) * HP], MM[:, q],
                                     start=True, stop=False)
                    last = nc.tensor.matmul(o, state[:, hd * HP:(hd + 1) * HP], CE[:, q],
                                            start=False, stop=True)
                last.then_inc(s("y_half"), 1)
                if hh:
                    pe.wait_ge(s("y_half"), k + 1)
                    pe.sem_inc(s("y_mm"), 1)
            for g in range(GROUPS):
                pe.wait_ge(s("y_sq"), g + 1)
                for x in range(GT):
                    last = nc.tensor.matmul(bank[2 + g][:, 0:SEQ], V("one").to_broadcast([P, P]),
                                            XDT[:, (g * GT + x) * SEQ:(g * GT + x + 1) * SEQ],
                                            start=x == 0, stop=x == GT - 1)
                last.then_inc(s("g_mm"), 1)

        def pool_ssd(pool, chain):
            pool.dma_start(TRI, t["tables"][:, TAB_TRIU:TAB_TRIU + P]).then_inc(s("tri"), 16)
            pool.wait_ge(s("tri"), 16)
            for j in range(6):
                c, b = j // 3, j % 3
                n = CW[c]
                pool.wait_ge(s("xdt"), j + 1)
                q = slice(c * DSSD + b * 512, c * DSSD + (b + 1) * 512)
                nc.gpsimd.tensor_tensor(
                    XDD[0:n, q].rearrange("p (h d) -> p h d", d=HP), XDT[0:n, q].rearrange("p (h d) -> p h d", d=HP),
                    tok(DS_TOK[c], c)[:, b * 8:(b + 1) * 8].unsqueeze(2).to_broadcast([n, 8, HP]),
                    ALU.mult).then_inc(s("xdd"), 1)
            pool.wait_ge(s("s0"), GROUPS)
            pool.wait_ge(s("elb"), 1)
            nc.gpsimd.tensor_tensor(S1.rearrange("p (h d) -> p h d", d=HP), S0.rearrange("p (h d) -> p h d", d=HP),
                                    ELB.unsqueeze(2).to_broadcast([P, HEADS, HP]), ALU.mult)\
                .then_inc(s("s0e"), 1)
            for k in range(4 * GROUPS):
                c, g = 1 + k // 8, (k // 2) % 4
                q = slice((k % 2) * 384, (k % 2 + 1) * 384)
                pool.wait_ge(s("ee"), k + 1)
                if k >= 2:
                    pool.wait_ge(s("y_half"), k - 1)
                nc.gpsimd.tensor_tensor(
                    CE[:, q].rearrange("p (x l) -> p x l", l=P), EE[:, q].rearrange("p (x l) -> p x l", l=P),
                    xbc(XS_T + GROUPS + g)[:, CHUNK[c]].unsqueeze(1).to_broadcast([P, 3, P]), ALU.mult)\
                    .then_inc(s("ce"), 1)
                if k % 2 and k >= 3:
                    gate(pool, (k - 3) // 2)
            gate(pool, 2 * GROUPS - 1)

        def gate(pool, m):
            c, g = 1 + m // 4, m % 4
            for x in range(GT):
                k = g * GT + x
                pool.wait_ge(s("y_out"), 3 * m + x + 1)
                q = slice(k * SEQ + (c - 1) * P, k * SEQ + c * P)
                nc.gpsimd.tensor_tensor(Y[:, q], Y[:, q], ZS[:, q], ALU.mult).then_inc(s("y_gated"), 1)

        def pe_mixer(pe):
            pe_in_proj(pe)
            pe_ssd(pe)

        def act_mixer(act, chain):
            act_in_proj(act, chain)
            act_ssd(act, chain)

        def dve_mixer(dve, chain):
            dve_in_proj(dve, chain)
            dve_ssd(dve, chain)

        def pool_mixer(pool, chain):
            pool_ssd(pool, chain)

        def down_act(act, n0, d0, count, src):
            y_act(act, n0, d0, 0, 0, 4, col(src, 0, 0, 4), 2)

            def step(i, r):
                y_act(act, n0 + 1, d0 + 1, i, r, 4, col(src, i, r + 1, 4), 2)
                split_hi(act, n0 + AHEAD, i, r, 4)

            steps(act, count - 1, 4, step)
            split_hi(act, n0 + count - 1 + AHEAD, 0, 0, 4)

        def down_dve(dve, n0, d0, count, src):
            y_dve(dve, d0, 0, 0, 4, col(src, 0, 0, 4))

            def step(i, r):
                y_dve(dve, d0 + 1, i, r, 4, col(src, i, r + 1, 4))
                split_lo(dve, n0 + AHEAD, i, r, 4)

            steps(dve, count - 1, 4, step)
            split_lo(dve, n0 + count - 1 + AHEAD, 0, 0, 4)

        def down_pe(pe, stage, n0, d0, count):
            clear_accumulators(pe, stage)
            steps(pe, count, 4, lambda i, r: down(pe, n0, d0, i, r, 4))

        def pe_wout(pe):
            pe.wait_ge(s("g_rt"), GROUPS)
            down_pe(pe, 0, N_WOUT, D_WOUT, 16)

        def act_wout(act):
            act.wait_ge(s("y_normed"), XS_T)
            down_act(act, N_WOUT, D_WOUT, 16, Y)

        def dve_wout(dve):
            dve.wait_ge(s("y_normed"), XS_T)
            down_dve(dve, N_WOUT, D_WOUT, 16, Y)
            add_dve(dve, "wout", N_WOUT + 15)

        c = Carve(8192)
        QT = c(2 * PH * SEQ)
        KEY = c(2 * PH * KEYS)
        SC = c(TT * 2 * PH * KEYS)
        SC2 = c(KEYS)
        V16 = c(TT * 2 * PH * TOPK)
        I16 = c(TT * 2 * PH * TOPK)
        I16F = c(TT * 2 * PH * TOPK)
        CAND = c(TOPK * TOPK)
        CAND2 = c(TOPK * TOPK)
        BEST = c(TT * PH * TOPK)
        POS = c(TT * PH * TOPK)
        AB = c(TT * 2 * PH * TOPK)
        ABF = c(TT * 2 * PH * TOPK)
        EQ = c(TT * 2 * PH * TOPK * TOPK)
        II = c(TT * 2 * PH * TOPK)
        GATE = c(TT * PH * TOPK)
        GSUM = c(TT * PH)
        G = arena
        HR = h[:, 0:4 * SEQ]
        I1T, I2T = h[:, 4 * SEQ:5 * SEQ], h[:, 5 * SEQ:6 * SEQ]
        GTH, GTL = h[:, 6 * SEQ:7 * SEQ], h[:, 7 * SEQ:8 * SEQ]
        PRD = h[:, 4 * SEQ:6 * SEQ]
        E1 = 64
        TPS = SEQ // (KEYS - E1)
        PCOL = tiny[:, 12:12 + TPS]
        NHK = PH * TOPK

        def spill_sem(q):
            return s(f"act_moved{q}")

        def pe_peer(pe):
            norm_pe(pe, 1)
            pe.wait_ge(nlo_done, nlo_total(1))
            steps(pe, 16, 4, lambda i, r: up(pe, N_WQ, U_WQ, i, r, 4, SEQ))
            pe.wait_ge(s("keys_in"), 16)
            pe.wait_ge(up_evac, U_U + 2)
            for tt in range(TT):
                for hs in range(2 * PH):
                    last = nc.tensor.matmul(bank[4 * tt + hs // 4][:, (hs % 4) * P:(hs % 4 + 1) * P],
                                            QT[:, hs * SEQ + tt * P:hs * SEQ + (tt + 1) * P],
                                            KEY[:, hs * KEYS:(hs + 1) * KEYS], start=True, stop=True)
                    if hs % 4 == 3:
                        last.then_inc(s("scores"), 1)
            pe.wait_ge(s("scores_in"), 8)
            steps(pe, E1, 4, lambda i, r: up(pe, N_U, U_U, i, r, 4, SEQ))
            pe.wait_ge(s("gates"), 1)
            for tt in range(TT):
                for x, src in enumerate((II[:, (2 * tt) * NHK:(2 * tt + 1) * NHK],
                                         II[:, (2 * tt + 1) * NHK:(2 * tt + 2) * NHK],
                                         GATE[:, tt * NHK:(tt + 1) * NHK])):
                    last = nc.tensor.transpose(bank[4 + x // 2][:, (x % 2) * SEQ + tt * P:(x % 2) * SEQ + (tt + 1) * P],
                                               src, ident[:, :])
            last.then_inc(s("cols_tr"), 1)

            def pair(i, r, half):
                for x in range(TPS // 2):
                    y = half * (TPS // 2) + x
                    tokens = i * (4 * TPS) + r * TPS + y + 1
                    q = y % 2
                    pe.wait_ge(s("hot_a"), 2 * tokens)
                    pe.wait_ge(s("hot_b"), tokens + 1)
                    if y == 0:
                        pe.wait_ge(s("g_evac"), i * 4 + r + 1)
                    o = bank[2 + r % 2][:, y * P:(y + 1) * P]
                    nc.tensor.matmul(o, yhi[:, q * 256:q * 256 + P], ylo[:, q * 256:q * 256 + P],
                                     start=True, stop=False)
                    nc.tensor.matmul(o, yhi[:, q * 256 + P:q * 256 + 2 * P], ylo[:, q * 256:q * 256 + P],
                                     start=False, stop=True).then_inc(s("hot_free"), 1)

            def step(i, r):
                up(pe, N_U + E1, U_U + E1, i, r, 4, SEQ, between=lambda: pair(i, r, 0))
                pair(i, r, 1)

            pe.sem_inc(s("hot_free"), 2)
            steps(pe, KEYS - E1, 4, step)
            clear_accumulators(pe, 1)
            steps(pe, KEYS, 4, lambda i, r: down(pe, N_V, D_V, i, r, 4))

        def act_peer(act, chain):
            act.sem_inc(s("g_evac"), 2)
            act.wait_ge(h_done, h_count("wout"))
            norm_act_sums(act, 1)
            norm_act_tokens(act, 1)
            norm_act_hi(act, 1, "g_ffn")

            def q_step(i, r):
                split_hi(act, N_WQ + AHEAD, i, r, 4)
                act.wait_ge(slabs_done, at(N_WQ, i, r, 4) + 1 + RING)
                nc.scalar.activation(col(QT, i, r, 4), bank[(U_WQ + r) % 2][:, 0:SEQ], ACT.Copy)\
                    .then_inc(up_evac, 1)

            steps(act, 16, 4, q_step)
            for b in range(8):
                act.wait_ge(s("scores"), b + 1)
                nc.scalar.activation(SC[:, b * 512:(b + 1) * 512], bank[b][:, :], ACT.Copy)\
                    .then_inc(s("scores_in"), 1)
            act.wait_ge(s("h_spilled"), 16)

            def gelu(n0, u0, i, r):
                act.wait_ge(slabs_done, at(n0, i, r, 4) + 1 + RING)
                k = at(n0 - N_U, i, r, 4)
                q = (n0 - N_U + r) % 4
                act.wait_ge(spill_sem(q), rounds(n0 - N_U, i, r, 4) * 16 + 16)
                nc.scalar.activation(HR[:, q * SEQ:(q + 1) * SEQ], bank[(u0 + r) % 2][:, 0:SEQ], ACT.Gelu)\
                    .then_inc(up_evac, 1)

            def step1(i, r):
                split_hi(act, N_U + AHEAD, i, r, 4)
                gelu(N_U, U_U, i, r)

            steps(act, E1, 4, step1)
            act.wait_ge(s("gate_x"), 1)
            nc.scalar.activation(GATE, GATE, ACT.Exp).then_inc(s("gate_e"), 1)
            act.wait_ge(s("cols_tr"), 1)
            nc.scalar.activation(GTH.bitcast(F32R), bank[5][:, 0:SEQ], ACT.Copy).then_inc(s("gth"), 1)
            act.wait_ge(s("cols"), 1)

            def g_out(i, r):
                act.wait_ge(s("hot_free"), (i * 4 + r) * TPS + TPS + 2)
                w = TPS * KEYS
                k = i * 4 + r
                dst = G[:, k * w:(k + 1) * w] if isinstance(k, int) else G[:, bass.ds(k * w, w)]
                nc.scalar.activation(dst, bank[2 + r % 2][:, 0:w], ACT.Copy).then_inc(s("g_evac"), 1)

            split_hi(act, N_U + E1 + AHEAD, 0, 0, 4)
            gelu(N_U + E1, U_U + E1, 0, 0)

            def step2(i, r):
                split_hi(act, N_U + E1 + 1 + AHEAD, i, r, 4)
                g_out(i, r)
                gelu(N_U + E1 + 1, U_U + E1 + 1, i, r)

            steps(act, KEYS - E1 - 1, 4, step2)
            g_out(0, KEYS - E1 - 1)

            def y_step(n0, d0, i, r):
                d = at(d0, i, r, 4)
                yq = (d0 + r) % 2
                act.wait_ge(slabs_done, at(n0, i, r, 4) - 2 + 1 + RING)
                act.wait_ge(y_new, at(d0 - D_V, i, r, 4) + 1)
                nc.scalar.activation(yhi[:, yq * SEQ:(yq + 1) * SEQ], PRD[:, yq * SEQ:(yq + 1) * SEQ],
                                     ACT.Copy).then_inc(y_hi, 1)

            y_step(N_V, D_V, 0, 0)

            def step3(i, r):
                y_step(N_V + 1, D_V + 1, i, r)
                split_hi(act, N_V + AHEAD, i, r, 4)

            steps(act, KEYS - 1, 4, step3)
            split_hi(act, N_V + KEYS - 1 + AHEAD, 0, 0, 4)

        def dve_peer(dve, chain):
            norm_dve_scale(dve, 1)
            norm_dve_tokens(dve, 1)
            norm_dve_lo(dve, 1, "g_ffn")
            steps(dve, 16, 4, lambda i, r: split_lo(dve, N_WQ + AHEAD, i, r, 4))

            def half(tt, hs):
                k = tt * 2 * PH + hs
                dve.wait_ge(s("scores_in"), tt * 4 + hs // 4 + 1)
                src = SC[:, k * KEYS:(k + 1) * KEYS]
                lo, hi = slice(k * 16, k * 16 + 8), slice(k * 16 + 8, k * 16 + 16)
                best16(src, SC2, V16[:, lo], V16[:, hi], I16[:, lo], I16[:, hi])

            def best16(src, rest, v_lo, v_hi, i_lo, i_hi):
                chain.link(nc.vector.max(v_lo, src))
                chain.inc(nc.vector.match_replace(rest, v_lo, src, NEG))
                last = chain.n
                chain.inc(nc.vector.max_index(i_lo.bitcast(U32), v_lo, src))
                dve.wait_ge(dve_self, last)
                chain.link(nc.vector.max(v_hi, rest))
                chain.link(nc.vector.max_index(i_hi.bitcast(U32), v_hi, rest))

            def pairs(tt, hd):
                a = (tt * 2 * PH + 2 * hd) * TOPK
                grid = CAND.rearrange("p (a b) -> p a b", b=TOPK)
                chain.link(nc.vector.tensor_tensor(
                    grid, V16[:, a:a + TOPK].unsqueeze(2).to_broadcast([P, TOPK, TOPK]),
                    V16[:, a + TOPK:a + 2 * TOPK].unsqueeze(1).to_broadcast([P, TOPK, TOPK]), ALU.add))
                k = (tt * PH + hd) * TOPK
                best16(CAND, CAND2, BEST[:, k:k + 8], BEST[:, k + 8:k + 16], POS[:, k:k + 8], POS[:, k + 8:k + 16])

            def places(tt):
                pos = POS[:, tt * NHK:(tt + 1) * NHK].bitcast(U32)
                ab = AB[:, 2 * tt * NHK:(2 * tt + 2) * NHK].bitcast(U32)
                chain.inc(nc.vector.tensor_scalar(ab[:, 0:NHK], pos, 4, None, ALU.logical_shift_right))
                chain.link(nc.vector.tensor_scalar(ab[:, NHK:2 * NHK], pos, 15, None, ALU.bitwise_and))
                q = slice(2 * tt * NHK, (2 * tt + 2) * NHK)
                chain.inc(nc.vector.tensor_copy(ABF[:, q], ab))
                nc.vector.tensor_copy(I16F[:, q], I16[:, q].bitcast(U32)).then_inc(s("places"), 1)
                chain.wait()

            def one_hots(tt, side):
                k = 2 * tt + side
                nc.vector.tensor_tensor(
                    EQ[:, k * NHK * TOPK:(k + 1) * NHK * TOPK].rearrange("p (n a) -> p n a", a=TOPK),
                    iota[:, 0:TOPK].unsqueeze(1).to_broadcast([P, NHK, TOPK]),
                    ABF[:, k * NHK:(k + 1) * NHK].unsqueeze(2).to_broadcast([P, NHK, TOPK]), ALU.is_equal)\
                    .then_inc(s("places"), 1)

            def numbers(tt):
                for side in range(2):
                    k = 2 * tt + side
                    dve.wait_ge(s("picked"), k + 1)
                    chain.link(nc.vector.tensor_reduce(
                        II[:, k * NHK:(k + 1) * NHK],
                        EQ[:, k * NHK * TOPK:(k + 1) * NHK * TOPK].rearrange("p (n a) -> p n a", a=TOPK),
                        AX.X, ALU.add))

            def gate_x():
                b = BEST.rearrange("p (h k) -> p h k", k=TOPK)
                nc.vector.tensor_tensor(GATE.rearrange("p (h k) -> p h k", k=TOPK), b,
                                        b[:, :, 0:1].to_broadcast([P, TT * PH, TOPK]), ALU.subtract)\
                    .then_inc(s("gate_x"), 1)

            units = []
            for tt in range(TT):
                units += [lambda tt=tt, hs=hs: half(tt, hs) for hs in range(2 * PH)]
                units += [lambda tt=tt, hd=hd: pairs(tt, hd) for hd in range(PH)]
                units += [lambda tt=tt: places(tt), lambda tt=tt: one_hots(tt, 0), lambda tt=tt: one_hots(tt, 1)]
            units += [gate_x, lambda: numbers(0)]
            for k in range(E1):
                split_lo(dve, N_U + k + AHEAD, 0, 0, 4)
                if k < len(units):
                    units[k]()
            numbers(1)
            dve.wait_ge(s("gate_e"), 1)
            g3 = GATE.rearrange("p (h k) -> p h k", k=TOPK)
            chain.link(nc.vector.tensor_reduce(GSUM, g3, AX.X, ALU.add))
            chain.link(nc.vector.reciprocal(GSUM, GSUM))
            nc.vector.tensor_tensor(g3, g3, GSUM.unsqueeze(2).to_broadcast([P, TT * PH, TOPK]), ALU.mult)\
                .then_inc(s("gates"), 1)
            dve.wait_ge(s("cols_tr"), 1)
            dve.wait_ge(s("h_spilled"), 16)
            chain.inc(nc.vector.tensor_copy(h[:, 4 * SEQ:6 * SEQ], bank[4][:, :]))
            dve.wait_ge(s("gth"), 1)
            chain.link(nc.vector.tensor_tensor(GTL.bitcast(F32R), bank[5][:, 0:SEQ], GTH, ALU.subtract))
            chain.link(nc.vector.memset(SC2[:, 0:1], 0.0))
            nc.vector.memset(SC2[:, 0:1], 0.0).then_inc(s("cols"), 1)

            def one_token(i, r, y):
                n = i * (4 * TPS) + r * TPS + y
                q = y % 2
                dve.wait_ge(s("hot_free"), n + 1)
                c1 = lambda ap: ap[:, n:n + 1] if isinstance(n, int) else ap[:, bass.ds(n, 1)]
                nc.vector.tensor_scalar(yhi[:, q * 256:q * 256 + P], iota[:, :], c1(I1T), c1(GTH),
                                        ALU.is_equal, ALU.mult).then_inc(s("hot_a"), 1)
                nc.vector.tensor_scalar(yhi[:, q * 256 + P:q * 256 + 2 * P], iota[:, :], c1(I1T), c1(GTL),
                                        ALU.is_equal, ALU.mult).then_inc(s("hot_a"), 1)

            def step(i, r):
                one_token(i, r, 0)
                one_token(i, r, 1)
                split_lo(dve, N_U + E1 + AHEAD, i, r, 4)
                one_token(i, r, 2)
                one_token(i, r, 3)

            steps(dve, KEYS - E1, 4, step)

            def prod(k0, i, r):
                k = at(k0, i, r, 4)
                q, b = (k0 + r) % 4, (D_V + k0 + r) % 2
                dve.wait_ge(spill_sem(q), (rounds(k0, i, r, 4) + 1) * 16 + 16 + 16 * (KEYS // 4))
                dve.wait_ge(y_lo, at(D_V + k0, i, r, 4) - 1)
                gk = G[:, :].rearrange("p (t k) -> p t k", k=KEYS)
                gk = gk[:, :, k:k + 1] if isinstance(k, int) else gk[:, :, bass.ds(k, 1)]
                nc.vector.tensor_tensor(PRD[:, b * SEQ:(b + 1) * SEQ].unsqueeze(2),
                                        HR[:, q * SEQ:(q + 1) * SEQ].unsqueeze(2), gk, ALU.mult)\
                    .then_inc(y_new, 1)
                yq = (D_V + k0 + r) % 2
                dve.wait_ge(y_hi, at(D_V + k0, i, r, 4) + 1)
                nc.vector.tensor_tensor(ylo[:, yq * SEQ:(yq + 1) * SEQ], PRD[:, yq * SEQ:(yq + 1) * SEQ],
                                        yhi[:, yq * SEQ:(yq + 1) * SEQ].bitcast(F32), ALU.subtract)\
                    .then_inc(y_lo, 1)

            dve.wait_ge(s("g_evac"), KEYS - E1 + 2)
            prod(0, 0, 0)

            def step3(i, r):
                prod(1, i, r)
                split_lo(dve, N_V + AHEAD, i, r, 4)

            steps(dve, KEYS - 1, 4, step3)
            split_lo(dve, N_V + KEYS - 1 + AHEAD, 0, 0, 4)
            dve.wait_ge(s("h_back"), 16)
            add_dve(dve, "v", N_V + KEYS - 1)

        def pool_peer(pool, chain):
            pool.wait_ge(s("y_sq"), GROUPS)
            pool.wait_ge(y_lo, 16)
            pool.dma_start(KEY, t["keys"]).then_inc(s("keys_in"), 16)
            for tt in range(TT):
                pool.wait_ge(s("places"), 3 * (tt + 1))
                for side in range(2):
                    k = 2 * tt + side
                    eq = EQ[:, k * NHK * TOPK:(k + 1) * NHK * TOPK]
                    lists = I16F[:, 2 * tt * NHK:(2 * tt + 2) * NHK]\
                        .rearrange("p (h s a) -> p h s a", s=2, a=TOPK)[:, :, side, :]
                    e4 = eq.rearrange("p (h k a) -> p h k a", k=TOPK, a=TOPK)
                    nc.gpsimd.tensor_tensor(e4, e4, lists.unsqueeze(2).to_broadcast([P, PH, TOPK, TOPK]),
                                            ALU.mult).then_inc(s("picked"), 1)
            pool.wait_ge(s("cols"), 1)

            def step(i, r):
                n = (i * 4 + r) * TPS
                src = I2T[:, n:n + TPS] if isinstance(n, int) else I2T[:, bass.ds(n, TPS)]
                pool.wait_ge(s("hot_b"), n + 1)
                pool.sem_inc(s("pool_turn"), 1)
                nc.gpsimd.tensor_copy(PCOL, src).then_inc(s("pcol"), 1)
                pool.wait_ge(s("pcol"), i * 4 + r + 1)
                pool.sem_inc(s("pool_turn"), 1)
                for y in range(TPS):
                    q = y % 2
                    pool.wait_ge(s("hot_free"), n + y + 1)
                    pool.sem_inc(s("pool_turn"), 1)
                    nc.gpsimd.tensor_scalar(ylo[:, q * 256:q * 256 + P], iota[:, :], PCOL[:, y:y + 1], None,
                                            ALU.is_equal).then_inc(s("hot_b"), 1)

            pool.sem_inc(s("hot_b"), 1)
            steps(pool, KEYS - E1, 4, step)

        def sp_peer_loads(sp):
            spill_at = N_WQ + 8
            steps(sp, spill_at - RING, 4, lambda i, r: load(sp, RING, i, r, 4))
            sp.wait_ge(nt_done, nt_base(1) + 2)
            sp.dma_start(t["h_spill"], h[:, :]).then_inc(s("h_spilled"), 16)
            lead = RING + AHEAD
            steps(sp, N_U + lead - spill_at, 4, lambda i, r: load(sp, spill_at, i, r, 4))
            for q in range(4):
                sp.sem_inc(spill_sem(q), 16)

            def act_dram(i, r, k0=0):
                k = at(k0, i, r, 4)
                return t["act_spill"][k] if isinstance(k, int) else \
                    t["act_spill"][bass.ds(k, 1)].rearrange("a p c -> (a p) c")

            def store(i, r):
                load(sp, N_U + lead, i, r, 4)
                sp.wait_ge(up_evac, at(U_U, i, r, 4) + 1 + 2)
                sp.dma_start(act_dram(i, r), HR[:, r * SEQ:(r + 1) * SEQ]).then_inc(spill_sem(r), 16)

            steps(sp, KEYS, 4, store)
            for q in range(4):
                sp.wait_ge(spill_sem(q), 16 + 16 * (KEYS // 4))
            for k in range(3):
                sp.dma_start(HR[:, k * SEQ:(k + 1) * SEQ], act_dram(0, k)).then_inc(spill_sem(k), 16)

            def fetch(k0, i, r):
                q = (k0 + r + 3) % 4
                sp.wait_ge(y_new, at(k0, i, r, 4))
                sp.dma_start(HR[:, q * SEQ:(q + 1) * SEQ], act_dram(i, r, k0 + 3)).then_inc(spill_sem(q), 16)

            sp.dma_start(HR[:, 3 * SEQ:4 * SEQ], act_dram(0, 3)).then_inc(spill_sem(3), 16)
            load(sp, N_V + lead, 0, 0, 4)

            def fetch_and_load(i, r):
                fetch(1, i, r)
                load(sp, N_V + lead + 1, i, r, 4)

            steps(sp, KEYS - 4, 4, fetch_and_load)
            for n in range(N_V + lead + KEYS - 3, N_V + lead + KEYS):
                load(sp, n, 0, 0, 4)
            sp.wait_ge(y_lo, D_V + KEYS)
            sp.dma_start(h[:, :], t["h_spill"]).then_inc(s("h_back"), 16)

        def pe_rest(pe):
            pe_peer(pe)
            pe_block2(pe)

        def act_rest(act, chain):
            act_peer(act, chain)
            act_block2(act, chain)

        def dve_rest(dve, chain):
            dve_peer(dve, chain)
            dve_block2(dve, chain)

        def pool_rest(pool, chain):
            pool_peer(pool, chain)
            pool_block2(pool, chain)

        def rest_of_kernel_loads(sp):
            sp_peer_loads(sp)
            sp_block2(sp)

        GROW = arena[:, 0:D]
        B0 = 7 * D
        c = Carve(B0)
        FG, QQ, KK, CUM, VT, GS = (c(HG_H * SEQ) for _ in range(6))
        QK = [c(HG_H * SEQ), c(HG_H * SEQ)]
        PP = c(HG_H * SEQ)
        CR = c(HG_H * P)
        MASK = c(len(LEVELS) * P)
        ONR = c(P)
        LBE = c(16)
        LBM, LBS, LB, LB1 = (c(8) for _ in range(4))
        OSS, OMS, ORT, ORS = (c(16) for _ in range(4))
        OO, OSQ, OT = QK[0], QK[1], QQ

        def pe_hgrn(pe):
            norm_pe(pe, 3)
            pe.wait_ge(nlo_done, nlo_total(3))
            steps(pe, 16, 4, lambda i, r: up(pe, N_HG, U_HG, i, r, 4, SEQ))

            def level(x):
                if x < 8:
                    pe.wait_ge(s("qk_q"), x + 1)
                    pe.wait_ge(s("qk_k"), x + 1)
                if x:
                    pe.wait_ge(s("level_out"), 4 * x)
                qk = QK[x % 2]
                if x == 0:
                    for hd in range(HG_H):
                        nc.tensor.matmul(bank[4 + hd // 4][:, (hd % 4) * P:(hd % 4 + 1) * P],
                                         qk[:, hd * SEQ:hd * SEQ + P], qk[:, hd * SEQ + P:(hd + 1) * SEQ],
                                         start=True, stop=True).then_inc(s("level_mm"), 2)
                    return
                for hc in range(2 * HG_H):
                    q = slice(hc * P, (hc + 1) * P)
                    a, b = (KK[:, q], QQ[:, q]) if x == 8 else (qk[:, q], qk[:, q])
                    nc.tensor.matmul(bank[4 + hc // 4][:, (hc % 4) * P:(hc % 4 + 1) * P], a, b,
                                     start=True, stop=True).then_inc(s("level_mm"), 1)

            for k in range(16):
                up_tokens(pe, N_HG + 16 + k, U_HG + 16 + k, 0, 0, 4)
                if k % 2 and k >= 3:
                    level((k - 3) // 2)
            level(7)
            level(8)
            pe.wait_ge(s("level_out"), 4 * 9)
            pe.wait_ge(up_evac, U_HG + 32 + 2)
            for tt in range(TT):
                for hd in range(HG_H):
                    o = bank[4 + 2 * tt + hd // 4][:, (hd % 4) * P:(hd % 4 + 1) * P]
                    v = lambda half: VT[:, half * D + hd * P:half * D + (hd + 1) * P]
                    if tt == 0:
                        last = nc.tensor.matmul(o, PP[:, hd * SEQ:hd * SEQ + P], v(0), start=True, stop=True)
                    else:
                        nc.tensor.matmul(o, CR[:, hd * P:(hd + 1) * P], v(0), start=True, stop=False)
                        last = nc.tensor.matmul(o, PP[:, hd * SEQ + P:(hd + 1) * SEQ], v(1), start=False, stop=True)
                    if hd % 4 == 3:
                        last.then_inc(s("o_mm"), 1)
            pe.wait_ge(s("o_gated"), 4)
            for j in range(HG_H):
                for tt in range(TT):
                    last = nc.tensor.transpose(bank[j // 2][:, (j % 2) * SEQ + tt * P:(j % 2) * SEQ + (tt + 1) * P],
                                               OO[:, tt * D + j * P:tt * D + (j + 1) * P], ident[:, :])
                if j % 2:
                    last.then_inc(s("o_tr"), 1)
            pe.wait_ge(s("ot"), 4)
            down_pe(pe, 2, N_HGO, D_HGO, 8)

        def act_hgrn(act, chain):
            act.wait_ge(h_done, h_count("v"))
            norm_act_sums(act, 2)
            act.wait_ge(s("x2"), 2)
            norm_act_sums(act, 3)
            norm_act_tokens(act, 3)
            norm_act_hi(act, 3, "hg_norm")
            act.wait_ge(s("lb_x"), 2)
            nc.scalar.activation(LBE, LBE, ACT.Exp).then_inc(s("lb_e"), 1)
            for j in range(8):
                split_hi(act, N_HG + j + AHEAD, 0, 0, 4)
                act.wait_ge(slabs_done, N_HG + j + 1 + RING)
                nc.scalar.activation(FG[:, j * SEQ:(j + 1) * SEQ], bank[(U_HG + j) % 2][:, 0:SEQ], ACT.Sigmoid)\
                    .then_inc(up_evac, 1)
            for j in range(8):
                split_hi(act, N_HG + 8 + j + AHEAD, 0, 0, 4)
                act.wait_ge(slabs_done, N_HG + 8 + j + 1 + RING)
                nc.scalar.activation(QQ[:, j * SEQ:(j + 1) * SEQ], bank[(U_HG + j) % 2][:, 0:SEQ], ACT.Copy)\
                    .then_inc(up_evac, 1)
            act.wait_ge(s("keys"), 8)
            nc.scalar.activation(FG, FG, ACT.Ln).then_inc(s("logf"), 1)
            act.wait_ge(up_evac, U_HG + 16 + 2)
            nc.scalar.activation(QQ, QQ, ACT.Silu).then_inc(s("q_silu"), 1)

            def level_exp(x):
                m = (P,) + LEVELS[:-1]
                m = m[x]
                act.wait_ge(s("dcum"), x + 1)
                e = QK[x % 2].rearrange("p (b w) -> p b w", w=2 * m)
                nc.scalar.activation(e[:, :, m:2 * m], e[:, :, m:2 * m], ACT.Exp).then_inc(s("e_q"), 1)
                nc.scalar.activation(e[:, :, 0:m], e[:, :, 0:m], ACT.Exp, scale=-1.0).then_inc(s("e_k"), 1)

            for k in range(16):
                n = N_HG + 16 + k
                split_hi(act, n + AHEAD, 0, 0, 4)
                if k % 2 == 0:
                    level_exp(k // 2)
                act.wait_ge(slabs_done, n + 1 + RING)
                dst, j = (VT, k) if k < 8 else (GS, k - 8)
                nc.scalar.activation(dst.rearrange("p (t d) -> p t d", t=TT)[:, :, j * P:(j + 1) * P],
                                     bank[(U_HG + k) % 2][:, 0:SEQ].rearrange("p (t d) -> p t d", t=TT),
                                     ACT.Copy).then_inc(up_evac, 1)
            act.wait_ge(up_evac, U_HG + 32 + 2)
            nc.scalar.activation(GS, GS, ACT.Silu).then_inc(s("g_silu"), 1)
            for b in range(4):
                act.wait_ge(s("o_mm"), b + 1)
                nc.scalar.activation(OSQ[:, b * 512:(b + 1) * 512], bank[4 + b][:, :], ACT.Square)\
                    .then_inc(s("o_sq"), 1)
            act.wait_ge(s("o_ms"), 1)
            nc.scalar.activation(ORT, OMS, ACT.Sqrt).then_inc(s("o_rt"), 1)
            for b in range(4):
                act.wait_ge(s("o_tr"), b + 1)
                nc.scalar.activation(OT[:, b * 512:(b + 1) * 512], bank[b][:, :], ACT.Copy).then_inc(s("ot"), 1)
            act.wait_ge(s("ot"), 4)
            down_act(act, N_HGO, D_HGO, 8, OT)

        def dve_hgrn(dve, chain):
            norm_dve_scale(dve, 2)
            dve.wait_ge(s("row_in"), 16)
            dve.wait_ge(rs_done, 3)
            for tt in range(TT):
                q = slice(tt * D, (tt + 1) * D)
                nc.vector.scalar_tensor_tensor(out=h[:, q], in0=h[:, q], scalar=RS[:, tt:tt + 1], in1=GROW,
                                               op0=ALU.mult, op1=ALU.mult).then_inc(s("x2"), 1)
            dve.wait_ge(s("x2"), 2)
            norm_dve_scale(dve, 3)
            norm_dve_tokens(dve, 3)
            norm_dve_lo(dve, 3, "hg_norm")
            l0, l1 = V("lb_logits", 0, 8), V("lb_logits", 8, 8)
            chain.link(nc.vector.tensor_tensor(LBM, l0, l1, ALU.max))
            nc.vector.tensor_tensor(LBE[:, 0:8], l0, LBM, ALU.subtract).then_inc(s("lb_x"), 1)
            nc.vector.tensor_tensor(LBE[:, 8:16], l1, LBM, ALU.subtract).then_inc(s("lb_x"), 1)
            dve.wait_ge(s("lb_e"), 1)
            chain.link(nc.vector.tensor_tensor(LBS, LBE[:, 0:8], LBE[:, 8:16], ALU.add))
            chain.link(nc.vector.reciprocal(LBS, LBS))
            chain.link(nc.vector.tensor_tensor(LB, LBE[:, 0:8], LBS, ALU.mult))
            chain.link(nc.vector.tensor_scalar(LB1, LB, -1.0, 1.0, ALU.mult, ALU.add))
            for j in range(8):
                split_lo(dve, N_HG + j + AHEAD, 0, 0, 4)
            for j in range(8):
                split_lo(dve, N_HG + 8 + j + AHEAD, 0, 0, 4)
                dve.wait_ge(up_evac, U_HG + j + 1 + 2)
                f = FG[:, j * SEQ:(j + 1) * SEQ]
                nc.vector.tensor_scalar(f, f, LB1[:, j:j + 1], LB[:, j:j + 1], ALU.mult, ALU.add)\
                    .then_inc(s("forget"), 1)
                if j:
                    dve.wait_ge(s("forget"), j)
                    f = slice((j - 1) * SEQ, j * SEQ)
                    nc.vector.tensor_scalar(KK[:, f], FG[:, f], -1.0, 1.0, ALU.mult, ALU.add)\
                        .then_inc(s("keys"), 1)
            dve.wait_ge(s("forget"), 8)
            nc.vector.tensor_scalar(KK[:, 7 * SEQ:], FG[:, 7 * SEQ:], -1.0, 1.0, ALU.mult, ALU.add)\
                .then_inc(s("keys"), 1)
            nc.vector.memset(PP, 0.0).then_inc(s("keys"), 1)
            dve.wait_ge(s("logf"), 1)
            for j in range(8):
                q = slice(j * SEQ, (j + 1) * SEQ)
                nc.vector.tensor_tensor_scan(CUM[:, q], V("one").to_broadcast([P, SEQ]), FG[:, q], 0.0,
                                             ALU.mult, ALU.add).then_inc(s("cum"), 1)

            def q_side(x):
                m = ((P,) + LEVELS[:-1])[x]
                dve.wait_ge(s("e_q"), x + 1)
                e = QK[x % 2].rearrange("p (b w) -> p b w", w=2 * m)
                q3 = QQ.rearrange("p (b w) -> p b w", w=2 * m)
                nc.vector.tensor_tensor(e[:, :, m:2 * m], e[:, :, m:2 * m], q3[:, :, m:2 * m], ALU.mult)\
                    .then_inc(s("qk_q"), 1)

            def take(x):
                if x == 0:
                    for b in range(2):
                        dve.wait_ge(s("level_mm"), 8 * (b + 1))
                        nc.vector.tensor_copy(CR[:, b * 512:(b + 1) * 512], bank[4 + b][:, :])\
                            .then_inc(s("level_out"), 2)
                    return
                dve.wait_ge(s("masks"), 16)
                for b in range(4):
                    dve.wait_ge(s("level_mm"), 16 * x + 4 * (b + 1))
                    if x > 1:
                        dve.wait_ge(s("level_out"), 4 * (x - 1) + b + 1)
                    nc.vector.copy_predicated(
                        PP[:, b * 512:(b + 1) * 512].rearrange("p (c t) -> p c t", t=P),
                        MASK[:, (x - 1) * P:x * P].bitcast(U32).unsqueeze(1).to_broadcast([P, 4, P]),
                        bank[4 + b][:, :].rearrange("p (c t) -> p c t", t=P)).then_inc(s("level_out"), 1)

            dve.wait_ge(s("q_scaled"), 1)
            dve.wait_ge(s("keys"), 9)
            for k in range(16):
                split_lo(dve, N_HG + 16 + k + AHEAD, 0, 0, 4)
                if k % 2 == 0:
                    q_side(k // 2)
                elif k >= 5:
                    take((k - 5) // 2)
            take(6)
            take(7)
            take(8)
            for b in range(4):
                dve.wait_ge(s("o_sq"), b + 1)
                nc.vector.tensor_reduce(OSS[:, 4 * b:4 * b + 4],
                                        OSQ[:, b * 512:(b + 1) * 512].rearrange("p (h d) -> p h d", d=P),
                                        AX.X, ALU.add).then_inc(s("o_ss"), 1)
            dve.wait_ge(s("o_ss"), 4)
            nc.vector.tensor_scalar(OMS, OSS, 1.0 / P, EPS, ALU.mult, ALU.add).then_inc(s("o_ms"), 1)
            dve.wait_ge(s("o_rt"), 1)
            chain.link(nc.vector.reciprocal(ORS, ORT))
            dve.wait_ge(s("gg"), 1)
            for b in range(4):
                q = slice(b * 512, (b + 1) * 512)
                chain.inc(nc.vector.tensor_tensor(
                    OO[:, q].rearrange("p (h d) -> p h d", d=P), bank[4 + b][:, :].rearrange("p (h d) -> p h d", d=P),
                    ORS[:, 4 * b:4 * b + 4].unsqueeze(2).to_broadcast([P, 4, P]), ALU.mult))
            chain.wait()
            for b in range(4):
                q = slice(b * 512, (b + 1) * 512)
                nc.vector.tensor_tensor(OO[:, q], OO[:, q], GS[:, q], ALU.mult).then_inc(s("o_gated"), 1)
            dve.wait_ge(s("ot"), 4)
            down_dve(dve, N_HGO, D_HGO, 8, OT)
            add_dve(dve, "hgo", N_HGO + 7)

        def pool_hgrn(pool, chain):
            pool.wait_ge(y_new, KEYS)
            pool.dma_start(GROW, t["g_final"]).then_inc(s("row_in"), 16)
            pool.dma_start(MASK, t["tables"][:, TAB_LEVEL:TAB_LEVEL + len(LEVELS) * P]).then_inc(s("masks"), 16)
            pool.dma_start(ONR, t["hg_out_norm"]).then_inc(s("onr_in"), 16)
            pool.wait_ge(s("q_silu"), 1)
            nc.gpsimd.tensor_scalar(QQ, QQ, float(P) ** -0.5, None, ALU.mult).then_inc(s("q_scaled"), 1)
            pool.wait_ge(s("q_scaled"), 1)
            pool.wait_ge(s("cum"), 8)
            pool.wait_ge(s("keys"), 9)

            def differences(x):
                m = ((P,) + LEVELS[:-1])[x]
                if x >= 2:
                    pool.wait_ge(s("level_mm"), 16 * (x - 1))
                c3 = CUM.rearrange("p (b w) -> p b w", w=2 * m)
                nc.gpsimd.tensor_tensor(QK[x % 2].rearrange("p (b w) -> p b w", w=2 * m), c3,
                                        c3[:, :, m - 1:m].to_broadcast([P, HG_H * SEQ // (2 * m), 2 * m]),
                                        ALU.subtract).then_inc(s("dcum"), 1)

            differences(0)
            for x in range(8):
                if x < 7:
                    differences(x + 1)
                m = ((P,) + LEVELS[:-1])[x]
                pool.wait_ge(s("e_k"), x + 1)
                e = QK[x % 2].rearrange("p (b w) -> p b w", w=2 * m)
                k3 = KK.rearrange("p (b w) -> p b w", w=2 * m)
                nc.gpsimd.tensor_tensor(e[:, :, 0:m], e[:, :, 0:m], k3[:, :, 0:m], ALU.mult)\
                    .then_inc(s("qk_k"), 1)
            pool.wait_ge(s("g_silu"), 1)
            pool.wait_ge(s("onr_in"), 16)
            g3 = GS.rearrange("p (h d) -> p h d", d=P)
            nc.gpsimd.tensor_tensor(g3, g3, ONR.unsqueeze(1).to_broadcast([P, 2 * HG_H, P]), ALU.mult)\
                .then_inc(s("gg"), 1)

        FFN = ((N_FF0, U_FF0, D_FF0, 4, 3, "ff0"), (N_FF1, U_FF1, D_FF1, 6, 5, "ff1"))
        c = Carve(B0)
        CVF = c(2 * SEQ)
        SG = c(2 * SEQ)
        YB = c(2 * SEQ)

        def ffn_steps(f, body):
            n0, u0, d0 = FFN[f][:3]

            def step(i, r):
                body(n0 + 2 + 3 * r, u0 + 2 + 2 * r, d0 + 1 + r, i, 1 + r)

            return step

        def pe_ffn(pe, f):
            n0, u0, d0, r0, st, _ = FFN[f]
            norm_pe(pe, r0)
            pe.wait_ge(nlo_done, nlo_total(r0))
            clear_accumulators(pe, st)
            up(pe, n0, u0, 0, 0, 12, SEQ)
            up(pe, n0 + 1, u0 + 1, 0, 0, 12, SEQ)

            def body(n, u, d, i, j):
                up(pe, n, u, i, 0, 12, SEQ, uU=8)
                up(pe, n + 1, u + 1, i, 0, 12, SEQ, uU=8)
                down(pe, n + 2, d - 1, i, 0, 12, dU=4)

            steps(pe, FF_T - 1, 4, ffn_steps(f, body))
            down(pe, n0 + 3 * FF_T - 1, d0 + FF_T - 1, 0, 0, 4)

        def act_ffn(act, f):
            n0, u0, d0, r0, _, before = FFN[f][:5] + ({0: "hgo", 1: "wo"}[f],)
            cb = XBC_T + FF_T * f
            act.wait_ge(h_done, h_count(before))
            norm_act_sums(act, r0)
            norm_act_tokens(act, r0)
            norm_act_hi(act, r0, f"ffn_norm{f}")

            def body(n, u, d, i, j, first=False):
                x = d - d0 + i * 4
                b = (d - d0) % 2
                split_hi(act, n + AHEAD, i, 0, 12)
                act.wait_ge(slabs_done, n + i * 12 + 1 + RING)
                act.wait_ge(silu_done, cb + x + 1)
                nc.scalar.activation(CVF[:, b * SEQ:(b + 1) * SEQ], bank[u % 2][:, 0:SEQ], ACT.Identity,
                                     scale=V(f"fconv_w{f}", x * 3 + 2), bias=V(f"fconv_b{f}", x))\
                    .then_inc(conv_begun, 1)
                split_hi(act, n + 1 + AHEAD, i, 0, 12)
                act.wait_ge(up_evac, u + i * 8 + 1 + 2)
                nc.scalar.activation(SG[:, b * SEQ:(b + 1) * SEQ], CVF[:, b * SEQ:(b + 1) * SEQ], ACT.Silu)\
                    .then_inc(silu_done, 1)
                if not first:
                    split_hi(act, n + 2 + AHEAD, i, 0, 12)
                act.wait_ge(up_evac, u + i * 8 + 2 + 2)
                if first:
                    act.wait_ge(slabs_done, n0)
                else:
                    act.wait_ge(slabs_done, n + i * 12 + RING)
                yq = d % 2
                nc.scalar.activation(yhi[:, yq * SEQ:(yq + 1) * SEQ], YB[:, b * SEQ:(b + 1) * SEQ], ACT.Copy)\
                    .then_inc(y_hi, 1)

            body(n0, u0, d0, 0, 0, True)
            steps(act, FF_T - 1, 4, ffn_steps(f, body))
            split_hi(act, n0 + 3 * FF_T - 1 + AHEAD, 0, 0, 4)

        def dve_ffn(dve, f, chain):
            n0, u0, d0, r0, _, name = FFN[f]
            cb = XBC_T + FF_T * f
            norm_dve_scale(dve, r0)
            norm_dve_tokens(dve, r0)
            norm_dve_lo(dve, r0, f"ffn_norm{f}")

            def body(n, u, d, i, j, first=False):
                x = d - d0 + i * 4
                b = (d - d0) % 2
                split_lo(dve, n + AHEAD, i, 0, 12)
                dve.wait_ge(conv_begun, cb + x + 1)
                for sh in (1, 2):
                    ins = nc.vector.scalar_tensor_tensor(
                        out=CVF[:, b * SEQ + sh:(b + 1) * SEQ], in0=bank[u % 2][:, 0:SEQ - sh],
                        scalar=V(f"fconv_w{f}", x * 3 + 2 - sh), in1=CVF[:, b * SEQ + sh:(b + 1) * SEQ],
                        op0=ALU.mult, op1=ALU.add)
                    if sh == 1:
                        chain.link(ins)
                ins.then_inc(up_evac, 1)
                split_lo(dve, n + 1 + AHEAD, i, 0, 12)
                dve.wait_ge(slabs_done, n + i * 12 + 2 + RING)
                dve.wait_ge(silu_done, cb + x + 1 + 2)
                y = YB[:, b * SEQ:(b + 1) * SEQ]
                nc.vector.tensor_tensor(y, SG[:, b * SEQ:(b + 1) * SEQ], bank[(u + 1) % 2][:, 0:SEQ],
                                        ALU.mult).then_inc(up_evac, 1)
                if not first:
                    split_lo(dve, n + 2 + AHEAD, i, 0, 12)
                yq = d % 2
                dve.wait_ge(y_hi, d + i * 4 + 1)
                nc.vector.tensor_tensor(ylo[:, yq * SEQ:(yq + 1) * SEQ], y,
                                        yhi[:, yq * SEQ:(yq + 1) * SEQ].bitcast(F32), ALU.subtract)\
                    .then_inc(y_lo, 1)

            body(n0, u0, d0, 0, 0, True)
            steps(dve, FF_T - 1, 4, ffn_steps(f, body), chain, 1)
            split_lo(dve, n0 + 3 * FF_T - 1 + AHEAD, 0, 0, 4)
            add_dve(dve, name, n0 + 3 * FF_T - 1)

        c = Carve(B0)
        KTA = c(2 * SEQ)
        VTA = c(TT * P)
        QA = c(8 * SEQ)
        DIST = c(3 * P)
        SCO = c(2 * 4 * 3 * P)
        PT = c(2 * 3 * P)
        ATT = c(8 * SEQ)
        SK8 = c(ATT_H)
        MX, NM, SM, SE, RD = (c(2 * 8) for _ in range(5))
        W3 = 3 * P
        SCALE = float(ATT_D) ** -0.5

        def pe_attn(pe):
            norm_pe(pe, 5)
            pe.wait_ge(nlo_done, nlo_total(5))
            for k in range(2):
                up(pe, N_ATT + k, U_ATT + k, 0, 0, 4, SEQ)
            up_tokens(pe, N_ATT + 2, U_ATT + 2, 0, 0, 4)
            pe.wait_ge(nlo_done, nlo_total(5, 1))
            steps(pe, 8, 4, lambda i, r: up(pe, N_ATT + 3, U_ATT + 3, i, r, 4, SEQ))
            pe.wait_ge(up_evac, U_ATT + 11 + 2)

            def scores(g):
                for x in range(4):
                    hd = 4 * g + x
                    if g:
                        pe.wait_ge(s("sco"), 4 * (g - 1) + x + 1)
                    p = slice((hd % 2) * 64, (hd % 2) * 64 + 64)
                    q = QA[p, (hd // 2) * SEQ:(hd // 2 + 1) * SEQ]
                    kk = KTA[p, (hd // 8) * SEQ:(hd // 8 + 1) * SEQ]
                    nc.tensor.matmul(bank[x][:, 0:P], q[:, 0:P], kk[:, 0:P], start=True, stop=True)
                    nc.tensor.matmul(bank[x][:, P:W3], q[:, P:SEQ], kk[:, :], start=True, stop=True)\
                        .then_inc(s("sc_mm"), 1)

            def transposes(hd):
                pe.wait_ge(s("probs"), 2 * (hd // 4) + 2)
                if hd >= 2:
                    pe.wait_ge(s("pt"), hd - 1)
                g, x = hd // 4, hd % 4
                src = SCO[:, ((g % 2) * 4 + x) * W3:((g % 2) * 4 + x + 1) * W3]
                for y in range(3):
                    last = nc.tensor.transpose(bank[4 + hd % 2][:, y * P:(y + 1) * P], src[:, y * P:(y + 1) * P],
                                               ident[:, :])
                last.then_inc(s("p_tr"), 1)

            def values(hd):
                pe.wait_ge(s("pt"), hd + 1)
                j = hd // 2
                if hd % 2 == 0 and j >= 2:
                    pe.wait_ge(s("att"), j - 1)
                p = PT[:, (hd % 2) * W3:(hd % 2 + 1) * W3]
                po = (hd % 2) * 64
                o = bank[6 + j % 2]
                v = lambda tt: VTA[:, tt * P + (hd // 8) * 64:tt * P + (hd // 8) * 64 + 64]
                nc.tensor.matmul(o[po:po + 64, 0:P], v(0), p[:, 0:P], start=True, stop=True)
                nc.tensor.matmul(o[po:po + 64, P:SEQ], v(0), p[:, P:2 * P], start=True, stop=False)
                nc.tensor.matmul(o[po:po + 64, P:SEQ], v(1), p[:, 2 * P:W3], start=False, stop=True)\
                    .then_inc(s("pv"), 1)

            scores(0)
            for g in range(4):
                if g < 3:
                    scores(g + 1)
                for x in range(4):
                    transposes(4 * g + x)
                    if 4 * g + x:
                        values(4 * g + x - 1)
            values(ATT_H - 1)
            pe.wait_ge(s("att"), 8)
            down_pe(pe, 4, N_WO, D_WO, 8)

        def act_attn(act, chain):
            act.wait_ge(h_done, h_count("ff0"))
            norm_act_sums(act, 5)
            norm_act_tokens(act, 5)
            norm_act_hi(act, 5, "kv_norm")
            for k in range(2):
                split_hi(act, N_ATT + k + AHEAD, 0, 0, 4)
                act.wait_ge(slabs_done, N_ATT + k + 1 + RING)
                nc.scalar.activation(KTA[:, k * SEQ:(k + 1) * SEQ], bank[(U_ATT + k) % 2][:, 0:SEQ], ACT.Copy)\
                    .then_inc(up_evac, 1)
            split_hi(act, N_ATT + 2 + AHEAD, 0, 0, 4)
            act.wait_ge(slabs_done, N_ATT + 3 + RING)
            nc.scalar.activation(VTA, bank[(U_ATT + 2) % 2][:, 0:SEQ], ACT.Copy).then_inc(up_evac, 1)
            norm_act_hi(act, 5, "attn_norm", 1)
            for k in range(8):
                n = N_ATT + 3 + k
                split_hi(act, n + AHEAD, 0, 0, 4)
                act.wait_ge(slabs_done, n + 1 + RING)
                nc.scalar.activation(QA[:, k * SEQ:(k + 1) * SEQ], bank[(U_ATT + 3 + k) % 2][:, 0:SEQ], ACT.Copy)\
                    .then_inc(up_evac, 1)

            def softmax(g):
                act.wait_ge(s("negmax"), 2 * g + 2)
                b8 = slice((g % 2) * 8, (g % 2) * 8 + 8)
                nc.scalar.activation(SE[:, b8], SE[:, b8], ACT.Exp, scale=SCALE).then_inc(s("sink_e"), 1)
                for x in range(4):
                    sc = SCO[:, ((g % 2) * 4 + x) * W3:((g % 2) * 4 + x + 1) * W3]
                    for b, q in ((0, slice(0, P)), (1, slice(P, W3))):
                        col1 = (g % 2) * 8 + 2 * x + b
                        nc.scalar.activation(sc[:, q], sc[:, q], ACT.Exp, scale=SCALE, bias=NM[:, col1:col1 + 1],
                                             accum_out=SM[:, col1:col1 + 1]).then_inc(s("exps"), 1)

            def copies(g):
                for x in range(4):
                    hd = 4 * g + x
                    act.wait_ge(s("p_tr"), hd + 1)
                    if hd >= 2:
                        act.wait_ge(s("pv"), hd - 1)
                    nc.scalar.activation(PT[:, (hd % 2) * W3:(hd % 2 + 1) * W3], bank[4 + hd % 2][:, 0:W3], ACT.Copy)\
                        .then_inc(s("pt"), 1)

            softmax(0)
            for g in range(4):
                if g < 3:
                    softmax(g + 1)
                copies(g)
            act.wait_ge(s("att"), 8)
            down_act(act, N_WO, D_WO, 8, ATT)

        def dve_attn(dve, chain):
            norm_dve_scale(dve, 5)
            norm_dve_tokens(dve, 5)
            norm_dve_lo(dve, 5, "kv_norm")
            for k in range(3):
                split_lo(dve, N_ATT + k + AHEAD, 0, 0, 4)
            norm_dve_lo(dve, 5, "attn_norm", 1)
            for k in range(8):
                split_lo(dve, N_ATT + 3 + k + AHEAD, 0, 0, 4)
            chain.link(nc.vector.tensor_scalar(SK8, V("sinks", 0, ATT_H), 1.0 / SCALE, None, ALU.mult))
            dve.wait_ge(s("dist_in"), 16)

            def stats(g):
                base = (g % 2) * 4 * W3
                for x in range(4):
                    hd = 4 * g + x
                    dve.wait_ge(s("sc_mm"), hd + 1)
                    if g >= 2:
                        dve.wait_ge(s("p_tr"), 4 * (g - 1))
                    slope = 2.0 ** (-8.0 * (hd + 1) / ATT_H)
                    nc.vector.scalar_tensor_tensor(out=SCO[:, base + x * W3:base + (x + 1) * W3], in0=DIST,
                                                   scalar=-slope / SCALE, in1=bank[x][:, 0:W3],
                                                   op0=ALU.mult, op1=ALU.add).then_inc(s("sco"), 1)
                dve.wait_ge(s("sco"), 4 * g + 4)
                b8 = slice((g % 2) * 8, (g % 2) * 8 + 8)
                s3 = SCO[:, base:base + 4 * W3].rearrange("p (h w) -> p h w", w=W3)
                m3 = MX[:, b8].rearrange("p (h b) -> p h b", b=2)
                chain.inc(nc.vector.tensor_reduce(m3[:, :, 0:1], s3[:, :, 0:P], AX.X, ALU.max))
                chain.link(nc.vector.tensor_reduce(m3[:, :, 1:2], s3[:, :, P:W3], AX.X, ALU.max))
                sk = SK8[:, 4 * g:4 * g + 4].unsqueeze(2).to_broadcast([P, 4, 2])
                chain.link(nc.vector.tensor_tensor(m3, m3, sk, ALU.max))
                nc.vector.tensor_tensor(SE[:, b8].rearrange("p (h b) -> p h b", b=2), sk, m3, ALU.subtract)\
                    .then_inc(s("negmax"), 1)
                nc.vector.tensor_scalar(NM[:, b8], MX[:, b8], -SCALE, None, ALU.mult).then_inc(s("negmax"), 1)

            def divide(g):
                b8 = slice((g % 2) * 8, (g % 2) * 8 + 8)
                base = (g % 2) * 4 * W3
                dve.wait_ge(s("sink_e"), g + 1)
                dve.wait_ge(s("exps"), 8 * (g + 1))
                chain.link(nc.vector.tensor_tensor(RD[:, b8], SM[:, b8], SE[:, b8], ALU.add))
                chain.link(nc.vector.reciprocal(RD[:, b8], RD[:, b8]))
                s3 = SCO[:, base:base + 4 * W3].rearrange("p (h w) -> p h w", w=W3)
                r3 = RD[:, b8].rearrange("p (h b) -> p h b", b=2)
                nc.vector.tensor_tensor(s3[:, :, 0:P], s3[:, :, 0:P], r3[:, :, 0:1].to_broadcast([P, 4, P]),
                                        ALU.mult).then_inc(s("probs"), 1)
                nc.vector.tensor_tensor(s3[:, :, P:W3], s3[:, :, P:W3], r3[:, :, 1:2].to_broadcast([P, 4, 2 * P]),
                                        ALU.mult).then_inc(s("probs"), 1)

            def outputs(g):
                for j in (2 * g, 2 * g + 1):
                    dve.wait_ge(s("pv"), 2 * j + 2)
                    nc.vector.tensor_copy(ATT[:, j * SEQ:(j + 1) * SEQ], bank[6 + j % 2][:, 0:SEQ])\
                        .then_inc(s("att"), 1)

            stats(0)
            for g in range(4):
                if g < 3:
                    stats(g + 1)
                divide(g)
                if g:
                    outputs(g - 1)
            outputs(3)
            dve.wait_ge(s("att"), 8)
            down_dve(dve, N_WO, D_WO, 8, ATT)
            add_dve(dve, "wo", N_WO + 7)

        def dve_output(dve):
            norm_dve_scale(dve, 7)
            dve.wait_ge(rs_done, 8)
            dve.wait_ge(s("row_in"), 32)
            for tt in range(TT):
                q = slice(tt * D, (tt + 1) * D)
                nc.vector.scalar_tensor_tensor(out=nt[:, q], in0=h[:, q], scalar=RS[:, tt:tt + 1], in1=GROW,
                                               op0=ALU.mult, op1=ALU.mult).then_inc(s("out_ready"), 1)

        def pe_block2(pe):
            pe_hgrn(pe)
            pe_ffn(pe, 0)
            pe_attn(pe)
            pe_ffn(pe, 1)

        def act_block2(act, chain):
            act_hgrn(act, chain)
            act_ffn(act, 0)
            act_attn(act, chain)
            act_ffn(act, 1)
            act.wait_ge(h_done, h_count("ff1"))
            norm_act_sums(act, 7)

        def dve_block2(dve, chain):
            dve_hgrn(dve, chain)
            dve_ffn(dve, 0, chain)
            dve_attn(dve, chain)
            dve_ffn(dve, 1, chain)
            dve_output(dve)

        def pool_block2(pool, chain):
            pool_hgrn(pool, chain)
            pool.wait_ge(s("gg"), 1)
            pool.wait_ge(h_done, h_count("hgo"))
            pool.dma_start(GROW, t["final_norm"]).then_inc(s("row_in"), 16)
            pool.wait_ge(h_done, h_count("ff0"))
            pool.dma_start(DIST, t["tables"][:, TAB_DIST:TAB_DIST + W3]).then_inc(s("dist_in"), 16)

        def sp_block2(sp):
            done = N_V + KEYS + RING + AHEAD
            steps(sp, N_SLABS - done, 4, lambda i, r: load(sp, done, i, r, 4))

        @block.sync
        def _(sp):
            sp.dma_start(h[:, :], t["x"]).then_inc(h_in, 16)
            sp.dma_start(meta_x[0:META, :], t["meta"]).then_inc(h_in, 16)
            sp.dma_start(vec[:, :], t["vec"]).then_inc(vec_in, 16)
            sp.dma_start(ident[:, :], t["ident"]).then_inc(vec_in, 16)
            sp.dma_start(iota[:, :], t["iota"]).then_inc(vec_in, 16)
            for n in range(RING):
                load(sp, n, 0, 0, 4)
            rest_of_kernel_loads(sp)
            for tt in range(TT):
                q = slice(tt * D, (tt + 1) * D)
                sp.wait_ge(s("out_ready"), tt + 1)
                sp.dma_start(t["out"][:, q], nt[:, q]).then_inc(out_done, 16)
            sp.wait_ge(out_done, 32)

        @block.tensor
        def _(pe):
            pe.sem_inc(slabs_done, RING)
            pe.sem_inc(up_evac, 2)
            pe.wait_ge(vec_in, 48)
            pe_mixer(pe)
            pe_wout(pe)
            pe_rest(pe)

        @block.scalar
        def _(act):
            act.sem_inc(silu_done, 2)
            chain = Chain(act, act_self)
            for n in range(AHEAD):
                split_hi(act, n, 0, 0, 4)
            act_mixer(act, chain)
            act_wout(act)
            act_rest(act, chain)

        @block.vector
        def _(dve):
            chain = Chain(dve, dve_self)
            dve_setup(dve, chain)
            for n in range(AHEAD):
                split_lo(dve, n, 0, 0, 4)
            dve_mixer(dve, chain)
            dve_wout(dve)
            dve_rest(dve, chain)
        @block.gpsimd
        def _(pool):
            chain = Chain(pool, pool_self)
            pool_mixer(pool, chain)
            pool_rest(pool, chain)
def _features(v):
    return v.reshape(-1, P).T


def _up_slabs(w):
    n = w.shape[1] // P
    return w.reshape(KT, P, n, P).transpose(2, 1, 0, 3).reshape(n, P, KT * P)


def _down_slabs(w):
    return w.reshape(-1, P, D)


def _interleave(*parts):
    return np.stack(parts, 1).reshape(-1, P, D)


def _stream(a):
    w_in = a["w_in"][0]
    o = np.cumsum([0, DSSD, DSSD + 2 * GROUPS * NST, HEADS, 512, 512, 512])
    z, xbc, dt, sc_b, sc_c, sc_x = (w_in[:, o[i]:o[i + 1]] for i in range(6))
    dt = np.concatenate([dt, np.zeros((D, P - HEADS), dt.dtype)], 1)
    u = a["expert_u"][0].reshape(KEYS, KEYS, KT, P)
    v = a["expert_v"][0].reshape(KEYS, KEYS, D)
    w_kv = a["w_kv_2"]
    k0, k1, vv = w_kv[:, 0:64], w_kv[:, 64:128], w_kv[:, 128:256]
    hq, hf, hi, hg = (a["hg_w_in_2"][0][:, i * D:(i + 1) * D] for i in range(4))

    def ffn(n):
        w = a["ffn_w_up_2"][n]
        g, x = _up_slabs(w[:, :FF_T * P]), _up_slabs(w[:, FF_T * P:])
        d = _down_slabs(a["ffn_w_down_2"][n])
        mid = _interleave(g[1:], x[1:], d[:-1])
        return [g[:1], x[:1], mid, d[-1:]]

    parts = [_up_slabs(dt), _up_slabs(xbc), _interleave(_up_slabs(sc_c), _up_slabs(sc_x), _up_slabs(sc_b)),
             _up_slabs(z), _down_slabs(a["w_out"][0]), _up_slabs(a["w_q"][0]),
             u.transpose(1, 3, 2, 0).reshape(KEYS, P, KT * P), v.transpose(1, 0, 2),
             _up_slabs(hf), _up_slabs(hq), _up_slabs(hi), _up_slabs(hg), _down_slabs(a["hg_w_out_2"][0]),
             *ffn(0), _up_slabs(np.concatenate([k0, k0, k1, k1, vv], 1)), _up_slabs(a["attn_w_q_2"][0]),
             _down_slabs(a["attn_w_o_2"][0]), *ffn(1)]
    out = np.concatenate(parts, 0)
    assert out.shape[0] == N_SLABS, out.shape
    return out


def _vectors(a):
    def heads(v):
        out = np.zeros((P, 1), v.dtype)
        out[:HEADS, 0] = v
        return out

    def taps(w):
        return w.reshape(w.shape[0], -1, P).transpose(2, 1, 0).reshape(P, -1)

    got = {"g_mix": _features(a["g_mix"][0]), "conv_w": taps(a["conv_ssd_w"][0]),
           "conv_b": _features(a["conv_ssd_b"][0]), "d_skip": _features(np.repeat(a["d_skip"][0], HP)),
           "ssd_norm": _features(a["ssd_norm_w"][0]), "sc_w": taps(a["conv_sc_w"][0]),
           "dt_bias": heads(a["dt_bias"][0]), "a_log": heads(a["a_log"][0]),
           "g_ffn": _features(a["g_ffn"][0]), "hg_norm": _features(a["hg_norm_2"][0]),
           "lb_logits": _features(a["hg_lb_logits_2"].reshape(-1)),
           "ffn_norm0": _features(a["ffn_norm_2"][0]), "ffn_norm1": _features(a["ffn_norm_2"][1]),
           "kv_norm": _features(a["kv_norm_2"]), "attn_norm": _features(a["attn_norm_2"][0]),
           "fconv_w0": taps(a["ffn_conv_w_2"][0]), "fconv_w1": taps(a["ffn_conv_w_2"][1]),
           "fconv_b0": _features(a["ffn_conv_b_2"][0]), "fconv_b1": _features(a["ffn_conv_b_2"][1]),
           "sinks": np.broadcast_to(a["attn_sinks_2"][0][None], (P, ATT_H)),
           "eps": np.full((P, 1), EPS, np.float32), "one": np.ones((P, 1), np.float32)}
    out = np.concatenate([got[n] for n in VEC], 1)
    assert out.shape == (P, NVEC), out.shape
    return out


def _tables():
    p = np.arange(P)[:, None]
    f = np.arange(P)[None, :]
    dist = np.arange(P)[:, None] + P - np.arange(2 * P)[None, :]
    dist = np.where((dist >= 0) & (dist < P), dist, 1e30).astype(np.float32)
    levels = []
    for m in LEVELS:
        if m:
            ok = (p // (2 * m) == f // (2 * m)) & (p // m % 2 == 0) & (f // m % 2 == 1)
        else:
            ok = p == f
        levels.append(ok.astype(np.float32))
    return np.concatenate([(p <= f).astype(np.float32), dist[:, P:], dist, *levels], 1)


def kernel(**inputs):
    import concourse.bacc as bacc
    from concourse.bass_utils import run_bass_kernel_spmd

    a = {k: np.asarray(v) for k, v in inputs.items()}
    tokens = lambda x: x.reshape(-1, P, D).transpose(1, 0, 2).reshape(P, -1)
    rows = lambda v: np.broadcast_to(v[None], (P, v.size))
    arrays = {
        "x": tokens(a["x"][0]), "meta": a["meta_tokens"], "vec": _vectors(a), "tables": _tables(),
        "ident": np.eye(P, dtype=np.float32), "iota": rows(np.arange(P, dtype=np.float32)),
        "stream": _stream(a),
        "keys": a["sub_keys"][0].reshape(2 * PH, KEYS, P).transpose(2, 0, 1).reshape(P, -1),
        "g_final": rows(a["g_final"]), "final_norm": rows(a["final_norm_2"]),
        "hg_out_norm": rows(a["hg_out_norm_2"][0]),
    }
    arrays = {k: np.ascontiguousarray(v) for k, v in arrays.items()}
    nc = bacc.Bacc("TRN2", target_bir_lowering=False, num_devices=1)
    t = {k: nc.dram_tensor(f"in_{k}", v.shape, F32, kind="ExternalInput").ap() for k, v in arrays.items()}
    t["out"] = nc.dram_tensor("out", (P, TT * D), F32, kind="ExternalOutput").ap()
    for name, shape in (("h_spill", (P, TT * D)), ("act_spill", (KEYS, P, SEQ))):
        t[name] = nc.dram_tensor(name, shape, F32, kind="Internal").ap()
    build(nc, t)
    r = run_bass_kernel_spmd(nc, [{f"in_{k}": v for k, v in arrays.items()}], core_ids=[0])
    got = r.results[0]["out"]
    return got.reshape(P, TT, D).transpose(1, 0, 2).reshape(1, SEQ, D)
```

```python
from contextlib import ExitStack

import numpy as np

import concourse.bass as bass
from concourse import mybir

F32 = mybir.dt.float32
F32R = mybir.dt.float32r
U32 = mybir.dt.uint32
BF16 = mybir.dt.bfloat16
ACT = mybir.ActivationFunctionType
ALU = mybir.AluOpType
AX = mybir.AxisListType

P = 128
D = 1024
KT = D // P
SEQ = 256
TT = SEQ // P
META = 16
TM = META + SEQ
EPS = 1e-6
HEADS, HP, GROUPS, NST = 24, 64, 4, 128
DSSD = HEADS * HP
XS_T = DSSD // P
XBC_T = XS_T + 2 * GROUPS
SC_T = 4
GH = HEADS // GROUPS
GT = DSSD // GROUPS // P
PH, TOPK = 8, 16
KEYS = 128
HG_H = 8
FF_T = 22
ATT_H, ATT_D = 16, 64
NEG = -3.0e38

N_IN = 0
IN_SLABS = 1 + XBC_T + 3 * SC_T + XS_T
N_Z = N_IN + 1 + XBC_T
N_SC = N_Z + XS_T
N_WOUT = N_IN + IN_SLABS
N_WQ = N_WOUT + 16
N_U = N_WQ + 16
N_V = N_U + KEYS
N_HG = N_V + KEYS
N_HGO = N_HG + 32
N_FF0 = N_HGO + 8
N_ATT = N_FF0 + 3 * FF_T
N_WO = N_ATT + 11
N_FF1 = N_WO + 8
N_SLABS = N_FF1 + 3 * FF_T
RING = 4
AHEAD = 3

VEC = {}


def _vec(name, width):
    VEC[name] = (sum(w for _, w in VEC.values()), width)


for _name, _w in (("g_mix", 8), ("conv_w", 4 * XBC_T), ("conv_b", XBC_T), ("d_skip", XS_T),
                  ("ssd_norm", XS_T), ("sc_w", 3 * SC_T), ("dt_bias", 1), ("a_log", 1), ("g_ffn", 8),
                  ("hg_norm", 8), ("lb_logits", 16), ("ffn_norm0", 8), ("ffn_norm1", 8),
                  ("kv_norm", 8), ("attn_norm", 8), ("fconv_w0", 3 * FF_T), ("fconv_w1", 3 * FF_T),
                  ("fconv_b0", FF_T), ("fconv_b1", FF_T), ("sinks", ATT_H), ("eps", 1), ("one", 1)):
    _vec(_name, _w)
NVEC = sum(w for _, w in VEC.values())

LEVELS = (64, 32, 16, 8, 4, 2, 1, 0)
TAB_TRIU, TAB_DIST, TAB_LEVEL = 0, P, P + 3 * P
NTAB = TAB_LEVEL + len(LEVELS) * P


class Chain:

    def __init__(self, eng, sem):
        self.eng, self.sem, self.n, self.dyn = eng, sem, 0, 0

    def inc(self, ins):
        self.n += 1
        ins.then_inc(self.sem, 1)

    def wait(self):
        self.eng.wait_ge(self.sem, self.dyn + self.n)

    def link(self, ins):
        self.inc(ins)
        self.wait()


def steps(eng, count, unroll, body, chain=None, per=0):
    full = count // unroll
    if full >= 2:
        start = chain.n if chain else 0
        with eng.Fori(0, full) as i:
            for r in range(unroll):
                if chain:
                    chain.dyn = i * (per * unroll)
                    before = chain.n
                body(i, r)
                if chain:
                    assert chain.n - before == per, (chain.n - before, per)
        if chain:
            chain.dyn = 0
            chain.n = start + per * unroll * full
        done = full * unroll
    else:
        done = 0
    for k in range(done, count):
        body(k // unroll, k % unroll)


def build(nc, t):
    ctx = ExitStack()
    with ctx:
        def sb(name, width, dt=F32):
            return ctx.enter_context(nc.sbuf_tensor(name, [P, width], dt))

        def sem(name):
            return ctx.enter_context(nc.semaphore(name))

        raw = sb("raw", RING * 1024)
        whi = sb("whi", RING * 1024, F32R)
        wlo = sb("wlo", RING * 1024, F32R)
        xhi = sb("xhi", KT * TM, F32R)
        xlo = sb("xlo", KT * TM, F32R)
        yhi = sb("yhi", 2 * SEQ, F32R)
        ylo = sb("ylo", 2 * SEQ, F32R)
        h = sb("h", TT * D)
        vec = sb("vec", NVEC)
        ident = sb("ident", P)
        iota = sb("iota", P)
        tiny = sb("tiny", 32)
        arena = sb("arena", 32768)
        bank = [ctx.enter_context(nc.psum_tensor(f"bank{i}", [P, 512], F32)) for i in range(8)]

        def V(name, i=0, n=1):
            o = VEC[name][0]
            if isinstance(i, int):
                return vec[:, o + i:o + i + n]
            return vec[:, bass.ds(i + o, n)]

        class Carve:
            def __init__(self, at=0):
                self.at = at

            def __call__(self, n):
                a = arena[:, self.at:self.at + n]
                self.at += n
                assert self.at <= 32768, self.at
                return a

        raw_ready = [sem(f"raw_ready{i}") for i in range(RING)]
        hi_ready = sem("hi_ready")
        lo_ready = sem("lo_ready")
        slabs_done = sem("slabs_done")
        halves_done = sem("halves_done")
        up_evac = sem("up_evac")
        conv_begun = sem("conv_begun")
        silu_done = sem("silu_done")
        y_new = sem("y_new")
        y_hi = sem("y_hi")
        y_lo = sem("y_lo")
        zeroed = sem("zeroed")
        h_in = sem("h_in")
        vec_in = sem("vec_in")
        tab_in = sem("tab_in")
        act_self, dve_self, pool_self, pe_self = (sem(n) for n in
                                                  ("act_self", "dve_self", "pool_self", "pe_self"))
        ss_done, ms_done, rt_done, rs_done = (sem(n) for n in ("ss_done", "ms_done", "rt_done", "rs_done"))
        nt_done, tr_done, nhi_done, nlo_done = (sem(n) for n in ("nt_done", "tr_done", "nhi_done", "nlo_done"))
        h_done = sem("h_done")
        out_done = sem("out_done")
        S = {}

        def s(name):
            if name not in S:
                S[name] = sem(name)
            return S[name]

        block = ctx.enter_context(nc.Block())

        def slot(n0, r):
            return (n0 + r) % RING

        def at(n0, i, r, U):
            return n0 + r + i * U

        def rounds(n0, i, r, U):
            return (n0 + r) // RING + i * (U // RING)

        def load(sp, n0, i, r, U):
            if n0 + r >= RING:
                sp.wait_ge(lo_ready, at(n0, i, r, U) - RING + 1)
            q = slot(n0, r)
            n = at(n0, i, r, U)
            src = t["stream"][n] if isinstance(n, int) else \
                t["stream"][bass.ds(n, 1)].rearrange("a p c -> (a p) c")
            sp.dma_start(raw[:, q * 1024:(q + 1) * 1024], src).then_inc(raw_ready[q], 16)

        def split_hi(act, n0, i, r, U):
            if isinstance(i, int) and at(n0, i, r, U) >= N_SLABS:
                return
            q = slot(n0, r)
            act.wait_ge(raw_ready[q], (rounds(n0, i, r, U) + 1) * 16)
            act.wait_ge(slabs_done, at(n0, i, r, U) + 1)
            nc.scalar.activation(whi[:, q * 1024:(q + 1) * 1024], raw[:, q * 1024:(q + 1) * 1024],
                                 ACT.Copy).then_inc(hi_ready, 1)

        def split_lo(dve, n0, i, r, U):
            if isinstance(i, int) and at(n0, i, r, U) >= N_SLABS:
                return
            q = slot(n0, r)
            dve.wait_ge(hi_ready, at(n0, i, r, U) + 1)
            nc.vector.tensor_tensor(wlo[:, q * 1024:(q + 1) * 1024], raw[:, q * 1024:(q + 1) * 1024],
                                    whi[:, q * 1024:(q + 1) * 1024].bitcast(F32), ALU.subtract)\
                .then_inc(lo_ready, 1)

        def up(pe, n0, u0, i, r, U, T, t0=0, Tall=SEQ, uU=None, between=None, x_ready=None):
            n, u = at(n0, i, r, U), at(u0, i, r, U if uU is None else uU)
            q, b = slot(n0, r), (u0 + r) % 2
            pe.wait_ge(lo_ready, n + 1)
            pe.wait_ge(up_evac, u + 1)
            for k in range(KT):
                w = slice(q * 1024 + k * P, q * 1024 + (k + 1) * P)
                x = slice(k * Tall + t0, k * Tall + t0 + T)
                if x_ready is not None:
                    pe.wait_ge(nlo_done, x_ready + k + 1)
                nc.tensor.matmul(bank[b][:, 0:T], whi[:, w], xhi[:, x], start=k == 0, stop=False)
                nc.tensor.matmul(bank[b][:, 0:T], whi[:, w], xlo[:, x], start=False, stop=False)
                last = nc.tensor.matmul(bank[b][:, 0:T], wlo[:, w], xhi[:, x], start=False,
                                        stop=k == KT - 1)
                if between and k == KT // 2 - 1:
                    between()
            last.then_inc(slabs_done, 1)

        def up_tokens(pe, n0, u0, i, r, U):
            n, u = at(n0, i, r, U), at(u0, i, r, U)
            q, b = slot(n0, r), (u0 + r) % 2
            pe.wait_ge(lo_ready, n + 1)
            pe.wait_ge(up_evac, u + 1)
            for tt in range(TT):
                for k in range(KT):
                    w = slice(q * 1024 + k * P, q * 1024 + (k + 1) * P)
                    x = slice(k * SEQ + tt * P, k * SEQ + (tt + 1) * P)
                    o = bank[b][:, tt * P:(tt + 1) * P]
                    nc.tensor.matmul(o, xhi[:, x], whi[:, w], start=k == 0, stop=False)
                    nc.tensor.matmul(o, xlo[:, x], whi[:, w], start=False, stop=False)
                    last = nc.tensor.matmul(o, xhi[:, x], wlo[:, w], start=False, stop=k == KT - 1)
            last.then_inc(slabs_done, 1)

        def up_wide(pe, n0, k):
            q = slot(n0 + k, 0)
            pe.wait_ge(lo_ready, n0 + k + 1)
            for tt in range(TT):
                x = slice(k * SEQ + tt * P, k * SEQ + (tt + 1) * P)
                for nh in range(2):
                    o = bank[2 * tt + nh][:, :]
                    w = slice(q * 1024 + nh * 512, q * 1024 + (nh + 1) * 512)
                    nc.tensor.matmul(o, xhi[:, x], whi[:, w], start=k == 0, stop=False)
                    nc.tensor.matmul(o, xhi[:, x], wlo[:, w], start=False, stop=False)
                    last = nc.tensor.matmul(o, xlo[:, x], whi[:, w], start=False, stop=k == KT - 1)
            last.then_inc(slabs_done, 1)

        def clear_accumulators(pe, d_stage):
            zero = tiny[0:1, 31:32].bitcast(BF16)[:, 0:1]
            for b in range(4, 8):
                last = nc.tensor.matmul(bank[b][:, :], zero.to_broadcast([1, P]), zero.to_broadcast([1, 512]),
                                        start=True, stop=True)
            last.then_inc(zeroed, 1)
            pe.wait_ge(zeroed, d_stage + 1)

        def down(pe, n0, d0, i, r, U, dU=None, dr=None):
            dU, dr = (U if dU is None else dU), (r if dr is None else dr)
            n, d = at(n0, i, r, U), at(d0, i, dr, dU)
            q, yq = slot(n0, r), (d0 + dr) % 2
            pe.wait_ge(lo_ready, n + 1)
            pe.wait_ge(y_lo, d + 1)
            for tt in range(TT):
                y = slice(yq * SEQ + tt * P, yq * SEQ + (tt + 1) * P)
                for nh in range(2):
                    o = bank[4 + 2 * tt + nh][:, :]
                    w = slice(q * 1024 + nh * 512, q * 1024 + (nh + 1) * 512)
                    nc.tensor.matmul(o, yhi[:, y], whi[:, w], start=False, stop=False, skip_group_check=True)
                    nc.tensor.matmul(o, yhi[:, y], wlo[:, w], start=False, stop=False, skip_group_check=True)
                    last = nc.tensor.matmul(o, ylo[:, y], whi[:, w], start=False, stop=True,
                                            skip_group_check=True)
                last.then_inc(slabs_done if tt else halves_done, 1)

        U_IN, U_WQ = 0, IN_SLABS
        U_U = U_WQ + 16
        U_HG = U_U + KEYS
        U_FF0 = U_HG + 16
        U_ATT = U_FF0 + 2 * FF_T
        U_FF1 = U_ATT + 11
        D_WOUT = 0
        D_V = 16
        D_HGO = D_V + KEYS
        D_FF0 = D_HGO + 8
        D_WO = D_FF0 + FF_T
        D_FF1 = D_WO + 8
        ADDS = ("wout", "v", "hgo", "ff0", "wo", "ff1")

        def ss_count(r):
            return 0 if r == 0 else 3 + 2 * (r - 1)

        NQ = {0: 0, 1: 1, 3: 2, 4: 3, 5: 4, 6: 5}

        def nt_base(r):
            q = NQ[r]
            return 0 if q == 0 else 3 + 2 * (q - 1)

        def bank_base(r):
            q = NQ[r]
            return 0 if q == 0 else 8 + 4 * (q - 1) + (4 if q > 4 else 0)

        meta_x = arena[:, 0:D]
        nt = arena[:, D:4 * D]
        junk = arena[:, 4 * D:7 * D]
        SS, MS, RT, RS = (tiny[:, 3 * i:3 * i + 3] for i in range(4))

        def tiles_of(r):
            return [(0, P), (1, P)] + ([(2, META)] if r == 0 else [])

        def norm_act_sums(act, r, ready=None):
            nc.scalar.activation(tiny[:, 20 + r:21 + r], tiny[:, 31:32], ACT.Sqrt)
            for tt, n in tiles_of(r):
                if ready:
                    ready(tt)
                src = h[0:n, tt * D:(tt + 1) * D] if tt < 2 else meta_x[0:n, :]
                nc.scalar.activation(junk[0:n, tt * D:(tt + 1) * D], src, ACT.Square,
                                     accum_out=SS[0:n, tt:tt + 1]).then_inc(ss_done, 1)
            w = len(tiles_of(r))
            act.wait_ge(ms_done, r + 1)
            nc.scalar.activation(RT[:, 0:w], MS[:, 0:w], ACT.Sqrt).then_inc(rt_done, 1)

        def norm_dve_scale(dve, r):
            w = len(tiles_of(r))
            dve.wait_ge(ss_done, ss_count(r + 1))
            nc.vector.tensor_scalar(MS[:, 0:w], SS[:, 0:w], 1.0 / D, EPS, ALU.mult, ALU.add)\
                .then_inc(ms_done, 1)
            dve.wait_ge(rt_done, r + 1)
            nc.vector.reciprocal(RS[:, 0:w], RT[:, 0:w]).then_inc(rs_done, 1)

        def norm_dve_tokens(dve, r):
            dve.wait_ge(rs_done, r + 1)
            for tt, n in tiles_of(r):
                if tt != 1:
                    src = h[0:n, 0:D] if tt < 2 else meta_x[0:n, :]
                    nc.vector.tensor_scalar(nt[0:n, tt * D:(tt + 1) * D], src, RS[0:n, tt:tt + 1], None,
                                            ALU.mult).then_inc(nt_done, 1)

        def norm_act_tokens(act, r):
            act.wait_ge(rs_done, r + 1)
            nc.scalar.activation(nt[:, D:2 * D], h[:, D:2 * D], ACT.Copy, scale=RS[:, 1:2])\
                .then_inc(nt_done, 1)

        def norm_pe(pe, r):
            pe.wait_ge(nt_done, nt_base(r) + len(tiles_of(r)))
            for j in range(KT):
                if r == 0:
                    o, m = bank[j], META
                    nc.tensor.transpose(o[:, 0:META], nt[0:META, 2 * D + j * P:2 * D + (j + 1) * P],
                                        ident[0:META, 0:META])
                    base = META
                else:
                    o, base = bank[4 + j // 2], (j % 2) * SEQ
                for tt in range(TT):
                    last = nc.tensor.transpose(o[:, base + tt * P:base + (tt + 1) * P],
                                               nt[:, tt * D + j * P:tt * D + (j + 1) * P], ident[:, :])
                if r == 0 or j % 2:
                    last.then_inc(tr_done, 1)

        def tr_base(r):
            q = NQ[r]
            return 0 if q == 0 else 8 + 4 * (q - 1)

        def norm_tiles(r):
            T = TM if r == 0 else SEQ
            for j in range(KT):
                src = bank[j][:, 0:TM] if r == 0 else bank[4 + j // 2][:, (j % 2) * SEQ:(j % 2 + 1) * SEQ]
                yield j, src, slice(j * T, (j + 1) * T), (j if r == 0 else j // 2), (r == 0 or j % 2 == 1)

        def norm_act_hi(act, r, gain, again=0):
            for j, src, x, b, ends in norm_tiles(r):
                act.wait_ge(tr_done, tr_base(r) + b + 1)
                ins = nc.scalar.activation(xhi[:, x], src, ACT.Copy, scale=V(gain, j))
                if ends:
                    ins.then_inc(nhi_done, 1)

        def norm_dve_lo(dve, r, gain, again=0):
            for j, src, x, b, ends in norm_tiles(r):
                dve.wait_ge(nhi_done, bank_base(r) + 4 * again + b + 1)
                nc.vector.scalar_tensor_tensor(out=xlo[:, x], in0=src, scalar=V(gain, j),
                                               in1=xhi[:, x].bitcast(F32), op0=ALU.mult,
                                               op1=ALU.subtract).then_inc(nlo_done, 1)

        def nlo_total(r, again=0):
            q = NQ[r]
            return 8 * (q + 1) + (8 if q > 4 else 0) + 8 * again

        def add_dve(dve, name, n_last, d_last):
            dve.wait_ge(halves_done, d_last + 1)
            for b in range(4):
                if b == 2:
                    dve.wait_ge(slabs_done, n_last + 1 + RING)
                nc.vector.tensor_tensor(h[:, b * 512:(b + 1) * 512], h[:, b * 512:(b + 1) * 512],
                                        bank[4 + b][:, :], ALU.add).then_inc(h_done, 1)
            split_lo(dve, n_last + AHEAD, 0, 0, 4)

        def h_count(name, tt=1):
            return 4 * ADDS.index(name) + 2 * (tt + 1)

        def nlo_before(r):
            return nlo_total(r) - KT

        def y_act(act, n0, d0, i, r, U, src, prev):
            d = at(d0, i, r, U)
            yq = (d0 + r) % 2
            act.wait_ge(slabs_done, at(n0, i, r, U) - prev + 1 + RING)
            nc.scalar.activation(yhi[:, yq * SEQ:(yq + 1) * SEQ], src, ACT.Copy).then_inc(y_hi, 1)

        def y_dve(dve, d0, i, r, U, src):
            yq = (d0 + r) % 2
            dve.wait_ge(y_hi, at(d0, i, r, U) + 1)
            nc.vector.tensor_tensor(ylo[:, yq * SEQ:(yq + 1) * SEQ], src,
                                    yhi[:, yq * SEQ:(yq + 1) * SEQ].bitcast(F32), ALU.subtract)\
                .then_inc(y_lo, 1)

        def col(ap, i, r, U, width=SEQ):
            k = i * U + r
            return ap[:, k * width:(k + 1) * width] if isinstance(k, int) else ap[:, bass.ds(k * width, width)]

        c = Carve(0)
        XBC = c(XBC_T * TM)
        ZS = c(XS_T * SEQ)
        Y = c(16 * SEQ)
        YS = Y[:, SC_T * SEQ:]
        CV = c(2 * TM)
        SCC = c(TM)
        PR = c(TM)
        DTR, DTA, DTE, DTT, AT, ACS, DST = (c(TM) for _ in range(7))
        XDT = c(3 * DSSD)
        XDD = c(2 * DSSD)
        BTOK = c(2 * GROUPS * NST)
        S0 = c(DSSD)
        S1 = c(DSSD)
        DD = c(2 * 384)
        EE = c(2 * 384)
        LL = c(2 * 384)
        MM = c(2 * 384)
        CE = c(2 * 384)
        CBM = c(2 * P)
        TOK = c(7 * HEADS)
        GRT, GRS = c(2 * GROUPS), c(2 * GROUPS)
        ELB = c(HEADS)
        LDG = c(HEADS)
        TRI = c(P)
        EA = c(1)
        assert c.at <= 32768
        CHUNK = (slice(0, META), slice(META, META + P), slice(META + P, TM))
        CW = (META, P, P)

        def xbc(k):
            return XBC[:, k * TM:(k + 1) * TM]

        def dve_setup(dve, chain):
            nc.vector.memset(tiny[:, :], 0.0).then_inc(s("setup"), 1)
            dve.wait_ge(s("setup"), 1)

        def pe_in_proj(pe):
            norm_pe(pe, 0)
            pe.wait_ge(nlo_done, 2)
            up(pe, 0, 0, 0, 0, 4, TM, 0, TM, x_ready=0)
            steps(pe, XBC_T, 4, lambda i, r: up(pe, 1, 1, i, r, 4, TM, 0, TM))
            steps(pe, XS_T, 4, lambda i, r: up(pe, N_Z, N_Z, i, r, 4, SEQ, META, TM))

        def sc_pe(pe, m):
            up(pe, N_SC + m, N_SC + m, 0, 0, 4, TM, 0, TM)

        def sc_act(act, m):
            n, j = N_SC + m, m // 3
            split_hi(act, n + AHEAD, 0, 0, 4)
            if m % 3 == 0:
                act.wait_ge(slabs_done, n + 1 + RING)
                act.wait_ge(up_evac, n + 2)
                if j:
                    act.wait_ge(s("sc_prod"), j)
                nc.scalar.activation(SCC, bank[n % 2][:, 0:TM], ACT.Copy).then_inc(up_evac, 1)

        def sc_dve(dve, chain, m):
            n, j = N_SC + m, m // 3
            split_lo(dve, n + AHEAD, 0, 0, 4)
            if m % 3 == 1:
                dve.wait_ge(slabs_done, n + 1 + RING)
                dve.wait_ge(up_evac, n + 2)
                chain.link(nc.vector.tensor_tensor(PR, bank[n % 2][:, 0:TM], SCC, ALU.mult))
                nc.vector.tensor_scalar(CV[:, 0:SEQ], PR[:, META:TM], V("sc_w", 3 * j + 2), None, ALU.mult)\
                    .then_inc(up_evac, 1)
                dve.wait_ge(up_evac, n + 1 + 2)
                chain.link(nc.vector.scalar_tensor_tensor(
                    out=CV[:, 0:SEQ], in0=PR[:, META - 1:TM - 1], scalar=V("sc_w", 3 * j + 1),
                    in1=CV[:, 0:SEQ], op0=ALU.mult, op1=ALU.add))
                nc.vector.scalar_tensor_tensor(
                    out=CV[:, 0:SEQ], in0=PR[:, META - 2:TM - 2], scalar=V("sc_w", 3 * j),
                    in1=CV[:, 0:SEQ], op0=ALU.mult, op1=ALU.add).then_inc(s("sc_prod"), 1)
            if m % 3 == 2:
                dve.wait_ge(s("sc_prod"), j + 1)
                dve.wait_ge(slabs_done, n + 1 + RING)
                nc.vector.tensor_tensor(Y[:, j * SEQ:(j + 1) * SEQ], CV[:, 0:SEQ],
                                        bank[n % 2][:, META:TM], ALU.mult).then_inc(up_evac, 1)

        def act_in_proj(act, chain):
            act.wait_ge(s("setup"), 1)
            norm_act_sums(act, 0, lambda tt: act.wait_ge(h_in, 32))
            split_hi(act, 0, 0, 0, 4)
            norm_act_tokens(act, 0)
            split_hi(act, 1, 0, 0, 4)
            act.wait_ge(vec_in, 48)
            norm_act_hi(act, 0, "g_mix")
            split_hi(act, 2, 0, 0, 4)
            split_hi(act, AHEAD, 0, 0, 4)

            def first(n0, i, r):
                n = at(n0, i, r, 4)
                act.wait_ge(slabs_done, n + 1 + RING)
                act.wait_ge(silu_done, n)
                b = (n0 + r) % 2
                nc.scalar.activation(CV[:, b * TM:(b + 1) * TM], bank[b][:, 0:TM], ACT.Identity,
                                     scale=V("conv_w", (n - 1) * 4 + 3), bias=V("conv_b", n - 1))\
                    .then_inc(conv_begun, 1)

            def silu(n0, i, r):
                n = at(n0, i, r, 4)
                act.wait_ge(up_evac, n + 1 + 2)
                b = (n0 + r) % 2
                dst = xbc(n - 1) if isinstance(n, int) else XBC[:, bass.ds((n - 1) * TM, TM)]
                nc.scalar.activation(dst, CV[:, b * TM:(b + 1) * TM], ACT.Silu).then_inc(silu_done, 1)

            split_hi(act, 1 + AHEAD, 0, 0, 4)
            first(1, 0, 0)

            def step(i, r):
                split_hi(act, 2 + AHEAD, i, r, 4)
                first(2, i, r)
                silu(1, i, r)

            steps(act, XBC_T - 1, 4, step)
            silu(XBC_T, 0, 0)
            def z_step(i, r):
                split_hi(act, N_Z + AHEAD, i, r, 4)
                act.wait_ge(slabs_done, at(N_Z, i, r, 4) + 1 + RING)
                nc.scalar.activation(col(ZS, i, r, 4), bank[(N_Z + r) % 2][:, 0:SEQ], ACT.Silu)\
                    .then_inc(up_evac, 1)

            act.wait_ge(up_evac, N_Z + 2)
            steps(act, XS_T, 4, z_step)

        def dve_in_proj(dve, chain):
            dve.wait_ge(vec_in, 48)
            norm_dve_scale(dve, 0)
            norm_dve_tokens(dve, 0)
            split_lo(dve, 0, 0, 0, 4)
            split_lo(dve, 1, 0, 0, 4)
            norm_dve_lo(dve, 0, "g_mix")
            split_lo(dve, 2, 0, 0, 4)
            split_lo(dve, AHEAD, 0, 0, 4)
            dve.wait_ge(slabs_done, 1 + RING)
            nc.vector.tensor_scalar(DTR[0:HEADS, :], bank[0][0:HEADS, 0:TM], V("dt_bias")[0:HEADS, :], None,
                                    ALU.add).then_inc(up_evac, 1)

            def conv(i, r):
                n = at(1, i, r, 4)
                b = (1 + r) % 2
                split_lo(dve, 1 + AHEAD, i, r, 4)
                dve.wait_ge(conv_begun, n)
                for sh in (1, 2, 3):
                    ins = nc.vector.scalar_tensor_tensor(
                        out=CV[:, b * TM + sh:(b + 1) * TM], in0=bank[b][:, 0:TM - sh],
                        scalar=V("conv_w", (n - 1) * 4 + 3 - sh), in1=CV[:, b * TM + sh:(b + 1) * TM],
                        op0=ALU.mult, op1=ALU.add)
                    if sh < 3:
                        chain.link(ins)
                ins.then_inc(up_evac, 1)

            steps(dve, XBC_T, 4, conv, chain, 2)
            steps(dve, XS_T, 4, lambda i, r: split_lo(dve, N_Z + AHEAD, i, r, 4))

        DT_TOK, DS_TOK, AC_TOK = (0, 1, 2), (3, 4), (None, 5, 6)

        def tok(i, c):
            return TOK[0:CW[c], i * HEADS:(i + 1) * HEADS]

        def dve_ssd(dve, chain):
            a = slice(0, HEADS)
            chain.link(nc.vector.scalar_tensor_tensor(out=DTA[a, :], in0=DTR[a, :], scalar=-1.0,
                                                      in1=DTR[a, :], op0=ALU.mult, op1=ALU.min))
            nc.vector.memset(EA[:, :], 1.0).then_inc(s("dt_abs"), 1)
            sc_dve(dve, chain, 0)
            sc_dve(dve, chain, 1)
            dve.wait_ge(s("dt_ln"), 2)
            chain.link(nc.vector.scalar_tensor_tensor(out=DTT[a, :], in0=DTR[a, :], scalar=0.0,
                                                      in1=DTE[a, :], op0=ALU.max, op1=ALU.add))
            chain.link(nc.vector.tensor_scalar(AT[a, :], DTT[a, :], DTA[a, 0:1], -1.0, ALU.mult, ALU.mult))
            for c in range(3):
                ins = nc.vector.tensor_tensor_scan(ACS[a, CHUNK[c]], V("one")[a, :].to_broadcast([HEADS, CW[c]]),
                                                   AT[a, CHUNK[c]], 0.0, ALU.mult, ALU.add)
                chain.inc(ins)
            chain.wait()
            nc.vector.tensor_scalar(LDG[a, :], ident[a, 0:HEADS], ACS[a, META + P - 1:META + P], None,
                                    ALU.mult).then_inc(s("acs"), 1)
            sc_dve(dve, chain, 2)
            dve.wait_ge(s("tok_tr"), 1)
            nc.vector.tensor_copy(TOK[0:META, 0:HEADS], bank[2][0:META, 0:HEADS]).then_inc(s("tok"), 1)
            nc.vector.tensor_copy(TOK[0:META, 3 * HEADS:4 * HEADS], bank[2][0:META, 3 * HEADS:4 * HEADS])\
                .then_inc(s("tok"), 1)
            for i in (1, 2, 4, 5, 6):
                nc.vector.tensor_copy(TOK[:, i * HEADS:(i + 1) * HEADS], bank[2][:, i * HEADS:(i + 1) * HEADS])\
                    .then_inc(s("tok"), 1)
            dve.wait_ge(s("tok"), 7)
            sc_dve(dve, chain, 3)
            for j in range(9):
                c, b = j // 3, j % 3
                n = CW[c]
                dve.wait_ge(s("x_tr"), j + 1)
                nc.vector.tensor_tensor(
                    XDT[0:n, c * DSSD + b * 512:c * DSSD + (b + 1) * 512].rearrange("p (h d) -> p h d", d=HP),
                    bank[3 + j % 3][0:n, :].rearrange("p (h d) -> p h d", d=HP),
                    tok(DT_TOK[c], c)[:, b * 8:(b + 1) * 8].unsqueeze(2).to_broadcast([n, 8, HP]),
                    ALU.mult).then_inc(s("xdt"), 1)
                if j in (1, 5, 8):
                    sc_dve(dve, chain, {1: 4, 5: 5, 8: 6}[j])
            for g in range(GROUPS):
                gs = slice(g * 384, (g + 1) * 384)
                dve.wait_ge(s("s0e"), 1)
                dve.wait_ge(s("st_mm"), GROUPS + g + 1)
                nc.vector.tensor_tensor(S1[:, gs], S1[:, gs], bank[2 + g][:, 0:384], ALU.add)\
                    .then_inc(s("s1"), 1)
            sc_dve(dve, chain, 7)
            def decay_differences(k):
                c, g, hh = 1 + k // 8, (k // 2) % 4, k % 2
                dve.wait_ge(s("ee"), k + 1)
                for x in range(3):
                    hd = g * GH + hh * 3 + x
                    nc.vector.tensor_scalar(
                        DD[:, (k % 2) * 384 + x * P:(k % 2) * 384 + (x + 1) * P],
                        bank[2 + k % 2][:, x * P:(x + 1) * P],
                        tok(AC_TOK[c], c)[:, hd:hd + 1], 0.0, ALU.subtract, ALU.min).then_inc(s("dd"), 1)

            def group_out(m):
                c, g = 1 + m // 4, m % 4
                dve.wait_ge(s("y_mm"), m + 1)
                for x in range(GT):
                    k = g * GT + x
                    nc.vector.scalar_tensor_tensor(
                        out=YS[:, k * SEQ + (c - 1) * P:k * SEQ + c * P],
                        in0=xbc(k)[:, CHUNK[c]], scalar=V("d_skip", k),
                        in1=bank[5 + m % 2][:, x * P:(x + 1) * P],
                        op0=ALU.mult, op1=ALU.add).then_inc(s("y_out"), 1)

            decay_differences(0)
            for k in range(4 * GROUPS):
                m, hh = k // 2, k % 2
                if k + 1 < 4 * GROUPS:
                    decay_differences(k + 1)
                if hh == 0:
                    dve.wait_ge(s("cb"), m + 1)
                    if m >= 2:
                        dve.wait_ge(s("y_mm"), m - 1)
                    nc.vector.tensor_tensor(CBM[:, (m % 2) * P:(m % 2 + 1) * P], bank[4][:, 0:P], TRI, ALU.mult)\
                        .then_inc(s("cbm"), 1)
                    dve.wait_ge(s("cbm"), m + 1)
                q = slice((k % 2) * 384, (k % 2 + 1) * 384)
                dve.wait_ge(s("ll"), k + 1)
                if k >= 2:
                    dve.wait_ge(s("y_half"), k - 1)
                nc.vector.tensor_tensor(
                    MM[:, q].rearrange("p (x l) -> p x l", l=P), LL[:, q].rearrange("p (x l) -> p x l", l=P),
                    CBM[:, (m % 2) * P:(m % 2 + 1) * P].unsqueeze(1).to_broadcast([P, 3, P]), ALU.mult)\
                    .then_inc(s("mm"), 1)
                if k in (3, 9):
                    sc_dve(dve, chain, {3: 8, 9: 9}[k])
                if hh and m:
                    group_out(m - 1)
            group_out(2 * GROUPS - 1)
            sc_dve(dve, chain, 10)
            sc_dve(dve, chain, 11)
            dve.wait_ge(s("g_rt"), 1)
            nc.vector.reciprocal(GRS, GRT).then_inc(s("g_rs"), 1)

        def act_ssd(act, chain):
            a = slice(0, HEADS)
            act.wait_ge(s("dt_abs"), 1)
            chain.link(nc.scalar.activation(DTE[a, :], DTA[a, :], ACT.Exp))
            sc_act(act, 0)
            sc_act(act, 1)
            nc.scalar.activation(DTE[a, :], DTE[a, :], ACT.Ln, bias=V("one")[a, :]).then_inc(s("dt_ln"), 1)
            act.wait_ge(s("dt_ln"), 1)
            nc.scalar.activation(DTA[a, 0:1], V("a_log")[a, :], ACT.Exp).then_inc(s("dt_ln"), 1)
            sc_act(act, 2)
            act.wait_ge(s("acs"), 1)
            for c in (0, 1):
                last = ACS[a, CHUNK[c].stop - 1:CHUNK[c].stop]
                nc.scalar.activation(DST[a, CHUNK[c]], ACS[a, CHUNK[c]], ACT.Exp, scale=-1.0, bias=last)\
                    .then_inc(s("dst"), 1)
            sc_act(act, 3)
            act.wait_ge(s("elb_mm"), 1)
            nc.scalar.activation(ELB, bank[7][:, 0:HEADS], ACT.Exp).then_inc(s("elb"), 1)
            sc_act(act, 4)
            for c in (0, 1):
                act.wait_ge(s("b_tr"), c + 1)
                nc.scalar.activation(BTOK[0:CW[c], c * 512:(c + 1) * 512], bank[6 + c][0:CW[c], :], ACT.Copy)\
                    .then_inc(s("btok"), 1)
            sc_act(act, 5)
            sc_act(act, 6)
            for g in range(GROUPS):
                act.wait_ge(s("st_mm"), g + 1)
                nc.scalar.activation(S0[:, g * 384:(g + 1) * 384], bank[2 + g][:, 0:384], ACT.Copy)\
                    .then_inc(s("s0"), 1)
            sc_act(act, 7)

            def decays(k):
                act.wait_ge(s("rr"), k + 1)
                if k >= 2:
                    act.wait_ge(s("ce"), k - 1)
                nc.scalar.activation(EE[:, (k % 2) * 384:(k % 2 + 1) * 384], bank[2 + k % 2][:, 0:384], ACT.Exp)\
                    .then_inc(s("ee"), 1)

            decays(0)
            for k in range(4 * GROUPS):
                q = slice((k % 2) * 384, (k % 2 + 1) * 384)
                if k + 1 < 4 * GROUPS:
                    decays(k + 1)
                act.wait_ge(s("dd"), 3 * (k + 1))
                if k >= 2:
                    act.wait_ge(s("mm"), k - 1)
                nc.scalar.activation(LL[:, q], DD[:, q], ACT.Exp).then_inc(s("ll"), 1)
                if k in (3, 9):
                    sc_act(act, {3: 8, 9: 9}[k])
            sc_act(act, 10)
            for g in range(GROUPS):
                act.wait_ge(s("y_gated"), 6 * GROUPS)
                nc.scalar.activation(XDT[:, g * 768:(g + 1) * 768], YS[:, g * 768:(g + 1) * 768], ACT.Square)\
                    .then_inc(s("y_sq"), 1)
            sc_act(act, 11)
            act.wait_ge(s("g_mm"), 1)
            nc.scalar.activation(GRT, bank[2][:, 0:2 * GROUPS], ACT.Sqrt, scale=1.0 / (GT * P), bias=V("eps"))\
                .then_inc(s("g_rt"), 1)

        def pe_ssd(pe):
            a = slice(0, HEADS)
            i24 = ident[a, 0:HEADS]
            for m in range(4):
                sc_pe(pe, m)
            pe.wait_ge(s("dst"), 2)
            for i, (src, c) in enumerate(((DTT, 0), (DTT, 1), (DTT, 2), (DST, 0), (DST, 1), (ACS, 1), (ACS, 2))):
                last = nc.tensor.transpose(bank[2][0:CW[c], i * HEADS:(i + 1) * HEADS], src[a, CHUNK[c]], i24)
            last.then_inc(s("tok_tr"), 1)
            nc.tensor.matmul(bank[7][:, 0:HEADS], V("one")[a, :].to_broadcast([HEADS, P]), LDG[a, :],
                             start=True, stop=True).then_inc(s("elb_mm"), 1)
            pe.wait_ge(s("elb"), 1)
            for c in (0, 1):
                for g in range(GROUPS):
                    last = nc.tensor.transpose(bank[6 + c][0:CW[c], g * P:(g + 1) * P],
                                               xbc(XS_T + g)[:, CHUNK[c]], ident[:, :])
                last.then_inc(s("b_tr"), 1)
            sc_pe(pe, 4)
            for j in range(9):
                c, b = j // 3, j % 3
                if j >= 3:
                    pe.wait_ge(s("xdt"), j - 2)
                for x in range(4):
                    last = nc.tensor.transpose(bank[3 + j % 3][0:CW[c], x * P:(x + 1) * P],
                                               xbc(4 * b + x)[:, CHUNK[c]], ident[:, :])
                last.then_inc(s("x_tr"), 1)
                if j == 3:
                    sc_pe(pe, 5)
            sc_pe(pe, 6)
            pe.wait_ge(s("btok"), 2)
            pe.wait_ge(s("xdt"), 9)
            pe.wait_ge(s("xdd"), 6)
            for c in (0, 1):
                n = CW[c]
                for g in range(GROUPS):
                    if c:
                        pe.wait_ge(s("s0"), g + 1)
                    nc.tensor.matmul(bank[2 + g][:, 0:384], BTOK[0:n, c * 512 + g * P:c * 512 + (g + 1) * P],
                                     XDD[0:n, c * DSSD + g * 384:c * DSSD + (g + 1) * 384],
                                     start=True, stop=True).then_inc(s("st_mm"), 1)

            def half_r(k):
                c, g, hh = 1 + k // 8, (k // 2) % 4, k % 2
                if k >= 2:
                    pe.wait_ge(s("dd"), 3 * (k - 1))
                else:
                    pe.wait_ge(s("s1"), GROUPS)
                for x in range(3):
                    hd = g * GH + hh * 3 + x
                    last = nc.tensor.matmul(bank[2 + k % 2][:, x * P:(x + 1) * P],
                                            ident[a, hd:hd + 1].to_broadcast([HEADS, P]), ACS[a, CHUNK[c]],
                                            start=True, stop=True)
                last.then_inc(s("rr"), 1)

            def cb(m):
                c, g = 1 + m // 4, m % 4
                if m:
                    pe.wait_ge(s("cbm"), m)
                nc.tensor.matmul(bank[4][:, 0:P], xbc(XS_T + g)[:, CHUNK[c]], xbc(XS_T + GROUPS + g)[:, CHUNK[c]],
                                 start=True, stop=True).then_inc(s("cb"), 1)

            sc_pe(pe, 7)
            half_r(0)
            half_r(1)
            cb(0)
            for k in range(4 * GROUPS):
                m, hh = k // 2, k % 2
                c, g = 1 + m // 4, m % 4
                if k + 2 < 4 * GROUPS:
                    half_r(k + 2)
                if hh and m + 1 < 2 * GROUPS:
                    cb(m + 1)
                if k in (3, 9):
                    sc_pe(pe, {3: 8, 9: 9}[k])
                pe.wait_ge(s("mm"), k + 1)
                pe.wait_ge(s("ce"), k + 1)
                if hh == 0 and m >= 2:
                    pe.wait_ge(s("y_out"), 3 * (m - 1))
                for x in range(3):
                    hd = g * GH + hh * 3 + x
                    po = (hd % 2) * HP
                    tile = (hd - g * GH) // 2
                    o = bank[5 + m % 2][po:po + HP, tile * P:(tile + 1) * P]
                    q = slice((k % 2) * 384 + x * P, (k % 2) * 384 + (x + 1) * P)
                    state = S0 if c == 1 else S1
                    nc.tensor.matmul(o, XDT[:, c * DSSD + hd * HP:c * DSSD + (hd + 1) * HP], MM[:, q],
                                     start=True, stop=False)
                    last = nc.tensor.matmul(o, state[:, hd * HP:(hd + 1) * HP], CE[:, q],
                                            start=False, stop=True)
                last.then_inc(s("y_half"), 1)
                if hh:
                    pe.wait_ge(s("y_half"), k + 1)
                    pe.sem_inc(s("y_mm"), 1)
            sc_pe(pe, 10)
            sc_pe(pe, 11)
            for g in range(GROUPS):
                pe.wait_ge(s("y_sq"), g + 1)
                for tt in range(TT):
                    for x in range(GT):
                        k = g * GT + x
                        last = nc.tensor.matmul(bank[2][:, 2 * g + tt:2 * g + tt + 1],
                                                XDT[:, k * SEQ + tt * P:k * SEQ + (tt + 1) * P], V("one"),
                                                start=x == 0, stop=x == GT - 1)
            last.then_inc(s("g_mm"), 1)
            clear_accumulators(pe, 0)
            pe.wait_ge(s("g_rs"), 1)
            for b in range(2 * GROUPS):
                last = nc.tensor.matmul(bank[2 + b // 4][:, (b % 4) * P:(b % 4 + 1) * P],
                                        GRS[:, b:b + 1].to_broadcast([P, P]), ident[:, :], start=True, stop=True)
            last.then_inc(s("g_bc"), 1)

        def pool_ssd(pool, chain):
            pool.dma_start(TRI, t["tables"][:, TAB_TRIU:TAB_TRIU + P]).then_inc(s("tri"), 16)
            pool.wait_ge(s("tri"), 16)
            for j in range(6):
                c, b = j // 3, j % 3
                n = CW[c]
                pool.wait_ge(s("xdt"), j + 1)
                q = slice(c * DSSD + b * 512, c * DSSD + (b + 1) * 512)
                nc.gpsimd.tensor_tensor(
                    XDD[0:n, q].rearrange("p (h d) -> p h d", d=HP), XDT[0:n, q].rearrange("p (h d) -> p h d", d=HP),
                    tok(DS_TOK[c], c)[:, b * 8:(b + 1) * 8].unsqueeze(2).to_broadcast([n, 8, HP]),
                    ALU.mult).then_inc(s("xdd"), 1)
            pool.wait_ge(s("s0"), GROUPS)
            pool.wait_ge(s("elb"), 1)
            nc.gpsimd.tensor_tensor(S1.rearrange("p (h d) -> p h d", d=HP), S0.rearrange("p (h d) -> p h d", d=HP),
                                    ELB.unsqueeze(2).to_broadcast([P, HEADS, HP]), ALU.mult)\
                .then_inc(s("s0e"), 1)
            for k in range(4 * GROUPS):
                c, g = 1 + k // 8, (k // 2) % 4
                q = slice((k % 2) * 384, (k % 2 + 1) * 384)
                pool.wait_ge(s("ee"), k + 1)
                if k >= 2:
                    pool.wait_ge(s("y_half"), k - 1)
                nc.gpsimd.tensor_tensor(
                    CE[:, q].rearrange("p (x l) -> p x l", l=P), EE[:, q].rearrange("p (x l) -> p x l", l=P),
                    xbc(XS_T + GROUPS + g)[:, CHUNK[c]].unsqueeze(1).to_broadcast([P, 3, P]), ALU.mult)\
                    .then_inc(s("ce"), 1)
                if k % 2 and k >= 5:
                    gate(pool, (k - 5) // 2)
            gate(pool, 2 * GROUPS - 2)
            gate(pool, 2 * GROUPS - 1)

        def gate(pool, m):
            c, g = 1 + m // 4, m % 4
            for x in range(GT):
                k = g * GT + x
                pool.wait_ge(s("y_out"), 3 * m + x + 1)
                q = slice(k * SEQ + (c - 1) * P, k * SEQ + c * P)
                nc.gpsimd.tensor_tensor(YS[:, q], YS[:, q], ZS[:, q], ALU.mult).then_inc(s("y_gated"), 1)

        def pe_mixer(pe):
            pe_in_proj(pe)
            pe_ssd(pe)

        def act_mixer(act, chain):
            act_in_proj(act, chain)
            act_ssd(act, chain)

        def dve_mixer(dve, chain):
            dve_in_proj(dve, chain)
            dve_ssd(dve, chain)

        def pool_mixer(pool, chain):
            pool_ssd(pool, chain)

        def down_act(act, n0, d0, count, src):
            y_act(act, n0, d0, 0, 0, 4, col(src, 0, 0, 4), 2)

            def step(i, r):
                y_act(act, n0 + 1, d0 + 1, i, r, 4, col(src, i, r + 1, 4), 2)
                split_hi(act, n0 + AHEAD, i, r, 4)

            steps(act, count - 1, 4, step)
            split_hi(act, n0 + count - 1 + AHEAD, 0, 0, 4)

        def down_dve(dve, n0, d0, count, src):
            y_dve(dve, d0, 0, 0, 4, col(src, 0, 0, 4))

            def step(i, r):
                y_dve(dve, d0 + 1, i, r, 4, col(src, i, r + 1, 4))
                split_lo(dve, n0 + AHEAD, i, r, 4)

            steps(dve, count - 1, 4, step)

        def down_pe(pe, stage, n0, d0, count):
            steps(pe, count, 4, lambda i, r: down(pe, n0, d0, i, r, 4))

        def pe_wout(pe):
            down_pe(pe, 0, N_WOUT, D_WOUT, 16)

        def act_wout(act):
            down_act(act, N_WOUT, D_WOUT, SC_T, Y)
            act.wait_ge(s("y_normed"), XS_T)
            down_act(act, N_WOUT + SC_T, D_WOUT + SC_T, XS_T, YS)

        def dve_wout(dve):
            y_dve(dve, D_WOUT, 0, 0, 4, col(Y, 0, 0, 4))
            for g in range(GROUPS):
                if g + 1 < SC_T:
                    y_dve(dve, D_WOUT + g + 1, 0, 0, 4, col(Y, 0, g + 1, 4))
                split_lo(dve, N_WOUT + g + AHEAD, 0, 0, 4)
                dve.wait_ge(s("g_bc"), 1)
                for x in range(GT):
                    k = g * GT + x
                    y = YS[:, k * SEQ:(k + 1) * SEQ]
                    nc.vector.scalar_tensor_tensor(out=y, in0=y, scalar=V("ssd_norm", k),
                                                   in1=bank[2 + g // 2][:, (g % 2) * SEQ:(g % 2 + 1) * SEQ],
                                                   op0=ALU.mult, op1=ALU.mult).then_inc(s("y_normed"), 1)
            dve.wait_ge(s("y_normed"), XS_T)
            down_dve(dve, N_WOUT + SC_T, D_WOUT + SC_T, XS_T, YS)
            add_dve(dve, "wout", N_WOUT + 15, D_WOUT + 15)

        c = Carve(8192)
        QT = c(2 * PH * SEQ)
        KEY = c(2 * PH * KEYS)
        SC = c(TT * 2 * PH * KEYS)
        SC2 = c(KEYS)
        V16 = c(TT * 2 * PH * TOPK)
        I16 = c(TT * 2 * PH * TOPK)
        I16F = c(TT * 2 * PH * TOPK)
        CAND = c(TOPK * TOPK)
        CAND2 = c(TOPK * TOPK)
        BEST = c(TT * PH * TOPK)
        POS = c(TT * PH * TOPK)
        AB = c(TT * 2 * PH * TOPK)
        ABF = c(TT * 2 * PH * TOPK)
        EQ = c(TT * 2 * PH * TOPK * TOPK)
        II = c(TT * 2 * PH * TOPK)
        GATE = c(TT * PH * TOPK)
        GSUM = c(TT * PH)
        G = arena
        HR = h[:, 0:4 * SEQ]
        I1T, I2T = h[:, 4 * SEQ:5 * SEQ], h[:, 5 * SEQ:6 * SEQ]
        GT_COLS = h[:, 6 * SEQ:7 * SEQ]
        PRD = h[:, 4 * SEQ:6 * SEQ]
        E1 = 64
        COLS_AT = E1 - 1
        TPS = SEQ // (KEYS - E1)
        PCOL = tiny[:, 12:12 + TPS]
        HOT1 = h[:, 7 * SEQ:8 * SEQ]
        HOT2 = ylo
        NHK = PH * TOPK

        def pool_splits(k):
            return k % 2 == 1 and (k < 24 or 30 <= k < 50)

        def spill_sem(q):
            return s(f"act_moved{q}")

        def pe_peer(pe):
            norm_pe(pe, 1)
            up(pe, N_WQ, U_WQ, 0, 0, 4, SEQ, x_ready=nlo_before(1))
            steps(pe, 15, 4, lambda i, r: up(pe, N_WQ + 1, U_WQ + 1, i, r, 4, SEQ))
            pe.wait_ge(s("keys_in"), 16)
            pe.wait_ge(up_evac, U_U + 2)
            for tt in range(TT):
                for hs in range(2 * PH):
                    last = nc.tensor.matmul(bank[4 * tt + hs // 4][:, (hs % 4) * P:(hs % 4 + 1) * P],
                                            QT[:, hs * SEQ + tt * P:hs * SEQ + (tt + 1) * P],
                                            KEY[:, hs * KEYS:(hs + 1) * KEYS], start=True, stop=True)
                    if hs % 4 == 3:
                        last.then_inc(s("scores"), 1)
            pe.wait_ge(s("scores_in"), 8)
            steps(pe, COLS_AT, 4, lambda i, r: up(pe, N_U, U_U, i, r, 4, SEQ))
            pe.wait_ge(s("gates"), 1)
            for tt in range(TT):
                for x, src in enumerate((II[:, (2 * tt) * NHK:(2 * tt + 1) * NHK],
                                         II[:, (2 * tt + 1) * NHK:(2 * tt + 2) * NHK],
                                         GATE[:, tt * NHK:(tt + 1) * NHK])):
                    last = nc.tensor.transpose(bank[4 + x // 2][:, (x % 2) * SEQ + tt * P:(x % 2) * SEQ + (tt + 1) * P],
                                               src, ident[:, :])
            last.then_inc(s("cols_tr"), 1)
            for k in range(COLS_AT, E1):
                up(pe, N_U + k, U_U + k, 0, 0, 4, SEQ)

            def pair(i, r, half):
                for x in range(TPS // 2):
                    y = half * (TPS // 2) + x
                    tokens = i * (4 * TPS) + r * TPS + y + 1
                    pe.wait_ge(s("hot_a"), tokens)
                    pe.wait_ge(s("hot_b"), tokens + 1)
                    if y == 0:
                        pe.wait_ge(s("g_evac"), i * 4 + r + 1)
                    o = bank[2 + r % 2][:, y * P:(y + 1) * P]
                    nc.tensor.matmul(o, HOT1[:, y % 2 * P:(y % 2 + 1) * P],
                                     HOT2[:, y * P:(y + 1) * P].bitcast(F32),
                                     start=True, stop=True).then_inc(s("hot_free"), 1)

            def step(i, r):
                up(pe, N_U + E1, U_U + E1, i, r, 4, SEQ, between=lambda: pair(i, r, 0))
                pair(i, r, 1)

            pe.sem_inc(s("hot_free"), TPS)
            steps(pe, KEYS - E1, 4, step)
            clear_accumulators(pe, 1)
            steps(pe, KEYS, 4, lambda i, r: down(pe, N_V, D_V, i, r, 4))

        def act_peer(act, chain):
            act.sem_inc(s("g_evac"), 2)
            norm_act_sums(act, 1, lambda tt: act.wait_ge(h_done, h_count("wout", tt)))
            norm_act_tokens(act, 1)
            norm_act_hi(act, 1, "g_ffn")

            def q_step(i, r):
                split_hi(act, N_WQ + AHEAD, i, r, 4)
                act.wait_ge(slabs_done, at(N_WQ, i, r, 4) + 1 + RING)
                nc.scalar.activation(col(QT, i, r, 4), bank[(U_WQ + r) % 2][:, 0:SEQ], ACT.Copy)\
                    .then_inc(up_evac, 1)

            steps(act, 16, 4, q_step)
            for b in range(8):
                act.wait_ge(s("scores"), b + 1)
                nc.scalar.activation(SC[:, b * 512:(b + 1) * 512], bank[b][:, :], ACT.Copy)\
                    .then_inc(s("scores_in"), 1)
            act.wait_ge(s("h_spilled"), 16)

            def gelu(n0, u0, i, r):
                act.wait_ge(slabs_done, at(n0, i, r, 4) + 1 + RING)
                k = at(n0 - N_U, i, r, 4)
                q = (n0 - N_U + r) % 4
                act.wait_ge(spill_sem(q), rounds(n0 - N_U, i, r, 4) * 16 + 16)
                nc.scalar.activation(HR[:, q * SEQ:(q + 1) * SEQ], bank[(u0 + r) % 2][:, 0:SEQ], ACT.Gelu)\
                    .then_inc(up_evac, 1)

            def step1(i, r):
                split_hi(act, N_U + AHEAD, i, r, 4)
                gelu(N_U, U_U, i, r)

            steps(act, E1 - 8, 4, step1)
            act.wait_ge(s("gate_x"), 1)
            nc.scalar.activation(GATE, GATE, ACT.Exp).then_inc(s("gate_e"), 1)
            for k in range(E1 - 8, COLS_AT):
                split_hi(act, N_U + k + AHEAD, 0, 0, 4)
                gelu(N_U + k, U_U + k, 0, 0)
            act.wait_ge(s("cols_tr"), 1)
            act.wait_ge(s("h_spilled"), 16)
            nc.scalar.activation(GT_COLS, bank[5][:, 0:SEQ], ACT.Copy).then_inc(s("gate_cols"), 1)
            for k in range(COLS_AT, E1):
                split_hi(act, N_U + k + AHEAD, 0, 0, 4)
                gelu(N_U + k, U_U + k, 0, 0)
            act.wait_ge(s("cols"), 1)

            def g_out(i, r):
                act.wait_ge(s("hot_free"), (i * 4 + r) * TPS + TPS + TPS)
                w = TPS * KEYS
                k = i * 4 + r
                dst = G[:, k * w:(k + 1) * w] if isinstance(k, int) else G[:, bass.ds(k * w, w)]
                nc.scalar.activation(dst, bank[2 + r % 2][:, 0:w], ACT.Copy).then_inc(s("g_evac"), 1)

            split_hi(act, N_U + E1 + AHEAD, 0, 0, 4)
            gelu(N_U + E1, U_U + E1, 0, 0)

            def step2(i, r):
                split_hi(act, N_U + E1 + 1 + AHEAD, i, r, 4)
                g_out(i, r)
                gelu(N_U + E1 + 1, U_U + E1 + 1, i, r)

            steps(act, KEYS - E1 - 1, 4, step2)
            g_out(0, KEYS - E1 - 1)

            def y_step(n0, d0, i, r):
                d = at(d0, i, r, 4)
                yq = (d0 + r) % 2
                act.wait_ge(slabs_done, at(n0, i, r, 4) - 2 + 1 + RING)
                act.wait_ge(y_new, at(d0 - D_V, i, r, 4) + 1)
                nc.scalar.activation(yhi[:, yq * SEQ:(yq + 1) * SEQ], PRD[:, yq * SEQ:(yq + 1) * SEQ],
                                     ACT.Copy).then_inc(y_hi, 1)

            y_step(N_V, D_V, 0, 0)

            def step3(i, r):
                y_step(N_V + 1, D_V + 1, i, r)
                split_hi(act, N_V + AHEAD, i, r, 4)

            steps(act, KEYS - 1, 4, step3)
            split_hi(act, N_V + KEYS - 1 + AHEAD, 0, 0, 4)

        def dve_peer(dve, chain):
            norm_dve_scale(dve, 1)
            norm_dve_tokens(dve, 1)
            norm_dve_lo(dve, 1, "g_ffn")
            steps(dve, 16, 4, lambda i, r: split_lo(dve, N_WQ + AHEAD, i, r, 4))

            def half(tt, hs):
                k = tt * 2 * PH + hs
                dve.wait_ge(s("scores_in"), tt * 4 + hs // 4 + 1)
                src = SC[:, k * KEYS:(k + 1) * KEYS]
                lo, hi = slice(k * 16, k * 16 + 8), slice(k * 16 + 8, k * 16 + 16)
                best16(src, SC2, V16[:, lo], V16[:, hi], I16[:, lo], I16[:, hi])

            def best16(src, rest, v_lo, v_hi, i_lo, i_hi):
                chain.link(nc.vector.max(v_lo, src))
                chain.inc(nc.vector.match_replace(rest, v_lo, src, NEG))
                last = chain.n
                chain.inc(nc.vector.max_index(i_lo.bitcast(U32), v_lo, src))
                dve.wait_ge(dve_self, last)
                chain.link(nc.vector.max(v_hi, rest))
                chain.link(nc.vector.max_index(i_hi.bitcast(U32), v_hi, rest))

            def pairs(tt, hd):
                a = (tt * 2 * PH + 2 * hd) * TOPK
                grid = CAND.rearrange("p (a b) -> p a b", b=TOPK)
                chain.link(nc.vector.tensor_tensor(
                    grid, V16[:, a:a + TOPK].unsqueeze(2).to_broadcast([P, TOPK, TOPK]),
                    V16[:, a + TOPK:a + 2 * TOPK].unsqueeze(1).to_broadcast([P, TOPK, TOPK]), ALU.add))
                k = (tt * PH + hd) * TOPK
                best16(CAND, CAND2, BEST[:, k:k + 8], BEST[:, k + 8:k + 16], POS[:, k:k + 8], POS[:, k + 8:k + 16])

            def places(tt):
                pos = POS[:, tt * NHK:(tt + 1) * NHK].bitcast(U32)
                ab = AB[:, 2 * tt * NHK:(2 * tt + 2) * NHK].bitcast(U32)
                chain.inc(nc.vector.tensor_scalar(ab[:, 0:NHK], pos, 4, None, ALU.logical_shift_right))
                chain.link(nc.vector.tensor_scalar(ab[:, NHK:2 * NHK], pos, 15, None, ALU.bitwise_and))
                q = slice(2 * tt * NHK, (2 * tt + 2) * NHK)
                chain.inc(nc.vector.tensor_copy(ABF[:, q], ab))
                nc.vector.tensor_copy(I16F[:, q], I16[:, q].bitcast(U32)).then_inc(s("places"), 1)
                chain.wait()

            def one_hots(tt, side):
                k = 2 * tt + side
                nc.vector.tensor_tensor(
                    EQ[:, k * NHK * TOPK:(k + 1) * NHK * TOPK].rearrange("p (n a) -> p n a", a=TOPK),
                    iota[:, 0:TOPK].unsqueeze(1).to_broadcast([P, NHK, TOPK]),
                    ABF[:, k * NHK:(k + 1) * NHK].unsqueeze(2).to_broadcast([P, NHK, TOPK]), ALU.is_equal)\
                    .then_inc(s("places"), 1)

            def numbers(tt, sides=(0, 1)):
                for side in sides:
                    k = 2 * tt + side
                    dve.wait_ge(s("picked"), k + 1)
                    chain.link(nc.vector.tensor_reduce(
                        II[:, k * NHK:(k + 1) * NHK],
                        EQ[:, k * NHK * TOPK:(k + 1) * NHK * TOPK].rearrange("p (n a) -> p n a", a=TOPK),
                        AX.X, ALU.add))

            def gate_x():
                b = BEST.rearrange("p (h k) -> p h k", k=TOPK)
                nc.vector.tensor_tensor(GATE.rearrange("p (h k) -> p h k", k=TOPK), b,
                                        b[:, :, 0:1].to_broadcast([P, TT * PH, TOPK]), ALU.subtract)\
                    .then_inc(s("gate_x"), 1)

            units = []
            for tt in range(TT):
                units += [lambda tt=tt, hs=hs: half(tt, hs) for hs in range(2 * PH)]
                units += [lambda tt=tt, hd=hd: pairs(tt, hd) for hd in range(PH)]
                units += [lambda tt=tt: places(tt), lambda tt=tt: one_hots(tt, 0), lambda tt=tt: one_hots(tt, 1)]

            def gates():
                dve.wait_ge(s("gate_e"), 1)
                g3 = GATE.rearrange("p (h k) -> p h k", k=TOPK)
                chain.link(nc.vector.tensor_reduce(GSUM, g3, AX.X, ALU.add))
                chain.link(nc.vector.reciprocal(GSUM, GSUM))
                nc.vector.tensor_tensor(g3, g3, GSUM.unsqueeze(2).to_broadcast([P, TT * PH, TOPK]), ALU.mult)\
                    .then_inc(s("gates"), 1)

            units.insert(len(units) - 2, gate_x)
            units.insert(len(units) - 1, lambda: numbers(0, (0,)))
            units.append(lambda: numbers(0, (1,)))
            units += [lambda: numbers(1, (0,)), lambda: numbers(1, (1,)), gates]
            for k in range(E1):
                if not pool_splits(k):
                    if k and pool_splits(k - 1):
                        dve.wait_ge(lo_ready, N_U + k + AHEAD)
                    split_lo(dve, N_U + k + AHEAD, 0, 0, 4)
                if k < len(units):
                    units[k]()
            dve.wait_ge(s("cols_tr"), 1)
            dve.wait_ge(s("h_spilled"), 16)
            chain.link(nc.vector.tensor_copy(h[:, 4 * SEQ:6 * SEQ], bank[4][:, :]))
            dve.wait_ge(s("gate_cols"), 1)
            chain.link(nc.vector.memset(SC2[:, 0:1], 0.0))
            nc.vector.memset(SC2[:, 0:1], 0.0).then_inc(s("cols"), 1)

            def one_token(i, r, y):
                n = i * (4 * TPS) + r * TPS + y
                dve.wait_ge(s("hot_free"), n - 2 + 1 + TPS)
                c1 = lambda ap: ap[:, n:n + 1] if isinstance(n, int) else ap[:, bass.ds(n, 1)]
                nc.vector.tensor_scalar(HOT1[:, y % 2 * P:(y % 2 + 1) * P], iota[:, :], c1(I1T), c1(GT_COLS),
                                        ALU.is_equal, ALU.mult).then_inc(s("hot_a"), 1)

            def step(i, r):
                one_token(i, r, 0)
                one_token(i, r, 1)
                split_lo(dve, N_U + E1 + AHEAD, i, r, 4)
                one_token(i, r, 2)
                one_token(i, r, 3)

            steps(dve, KEYS - E1, 4, step)

            def prod(k0, i, r):
                k = at(k0, i, r, 4)
                q, b = (k0 + r) % 4, (D_V + k0 + r) % 2
                dve.wait_ge(spill_sem(q), (rounds(k0, i, r, 4) + 1) * 16 + 16 + 16 * (KEYS // 4))
                dve.wait_ge(y_lo, at(D_V + k0, i, r, 4) - 1)
                gk = G[:, :].rearrange("p (t k) -> p t k", k=KEYS)
                gk = gk[:, :, k:k + 1] if isinstance(k, int) else gk[:, :, bass.ds(k, 1)]
                nc.vector.tensor_tensor(PRD[:, b * SEQ:(b + 1) * SEQ].unsqueeze(2),
                                        HR[:, q * SEQ:(q + 1) * SEQ].unsqueeze(2), gk, ALU.mult)\
                    .then_inc(y_new, 1)

            def prod_lo(k0, i, r):
                yq = (D_V + k0 + r) % 2
                dve.wait_ge(y_hi, at(D_V + k0, i, r, 4) + 1)
                nc.vector.tensor_tensor(ylo[:, yq * SEQ:(yq + 1) * SEQ], PRD[:, yq * SEQ:(yq + 1) * SEQ],
                                        yhi[:, yq * SEQ:(yq + 1) * SEQ].bitcast(F32), ALU.subtract)\
                    .then_inc(y_lo, 1)

            dve.wait_ge(s("g_evac"), KEYS - E1 + 2)
            prod(0, 0, 0)
            prod_lo(0, 0, 0)
            prod(1, 0, 0)

            def step3(i, r):
                prod_lo(1, i, r)
                prod(2, i, r)
                split_lo(dve, N_V + AHEAD, i, r, 4)

            steps(dve, KEYS - 2, 4, step3)
            prod_lo(KEYS - 1, 0, 0)
            split_lo(dve, N_V + KEYS - 2 + AHEAD, 0, 0, 4)
            dve.wait_ge(s("h_back"), 3 * 16)
            add_dve(dve, "v", N_V + KEYS - 1, D_V + KEYS - 1)

        def pool_peer(pool, chain):
            pool.wait_ge(s("y_sq"), GROUPS)
            pool.wait_ge(y_lo, 16)
            pool.dma_start(KEY, t["keys"]).then_inc(s("keys_in"), 16)
            for tt in range(TT):
                for k in ((range(24), range(24, 50))[tt]):
                    if pool_splits(k):
                        n = N_U + k + AHEAD
                        pool.wait_ge(lo_ready, n)
                        pool.wait_ge(hi_ready, n + 1)
                        q = slice(slot(n, 0) * 1024, (slot(n, 0) + 1) * 1024)
                        nc.gpsimd.tensor_tensor(wlo[:, q], raw[:, q], whi[:, q].bitcast(F32), ALU.subtract)\
                            .then_inc(lo_ready, 1)
                pool.wait_ge(s("places"), 3 * (tt + 1))
                for side in range(2):
                    k = 2 * tt + side
                    eq = EQ[:, k * NHK * TOPK:(k + 1) * NHK * TOPK]
                    lists = I16F[:, 2 * tt * NHK:(2 * tt + 2) * NHK]\
                        .rearrange("p (h s a) -> p h s a", s=2, a=TOPK)[:, :, side, :]
                    e4 = eq.rearrange("p (h k a) -> p h k a", k=TOPK, a=TOPK)
                    nc.gpsimd.tensor_tensor(e4, e4, lists.unsqueeze(2).to_broadcast([P, PH, TOPK, TOPK]),
                                            ALU.mult).then_inc(s("picked"), 1)
            pool.wait_ge(s("cols"), 1)

            def step(i, r):
                n = (i * 4 + r) * TPS
                src = I2T[:, n:n + TPS] if isinstance(n, int) else I2T[:, bass.ds(n, TPS)]
                pool.wait_ge(s("hot_b"), n + 1)
                pool.sem_inc(s("pool_turn"), 1)
                nc.gpsimd.tensor_copy(PCOL, src).then_inc(s("pcol"), 1)
                pool.wait_ge(s("pcol"), i * 4 + r + 1)
                pool.sem_inc(s("pool_turn"), 1)
                for y in range(TPS):
                    pool.wait_ge(s("hot_free"), n + y + 1)
                    pool.sem_inc(s("pool_turn"), 1)
                    nc.gpsimd.tensor_scalar(HOT2[:, y * P:(y + 1) * P], iota[:, :], PCOL[:, y:y + 1], None,
                                            ALU.is_equal).then_inc(s("hot_b"), 1)

            pool.sem_inc(s("hot_b"), 1)
            steps(pool, KEYS - E1, 4, step)
            for part, free, count in ((slice(6 * SEQ, 8 * SEQ), s("hot_free"), SEQ + TPS), (slice(0, 4 * SEQ), y_new, KEYS),
                                      (slice(4 * SEQ, 6 * SEQ), y_lo, D_V + KEYS)):
                pool.wait_ge(free, count)
                pool.dma_start(h[:, part], t["h_spill"][:, part]).then_inc(s("h_back"), 16)

        def sp_peer_loads(sp):
            spill_at = N_WQ + 8
            steps(sp, spill_at - RING, 4, lambda i, r: load(sp, RING, i, r, 4))
            sp.wait_ge(nt_done, nt_base(1) + 2)
            sp.dma_start(t["h_spill"], h[:, :]).then_inc(s("h_spilled"), 16)
            lead = RING + AHEAD
            steps(sp, N_U + lead - spill_at, 4, lambda i, r: load(sp, spill_at, i, r, 4))
            for q in range(4):
                sp.sem_inc(spill_sem(q), 16)

            def act_dram(i, r, k0=0):
                k = at(k0, i, r, 4)
                return t["act_spill"][k] if isinstance(k, int) else \
                    t["act_spill"][bass.ds(k, 1)].rearrange("a p c -> (a p) c")

            def store(i, r):
                load(sp, N_U + lead, i, r, 4)
                sp.wait_ge(up_evac, at(U_U, i, r, 4) + 1 + 2)
                sp.dma_start(act_dram(i, r), HR[:, r * SEQ:(r + 1) * SEQ]).then_inc(spill_sem(r), 16)

            steps(sp, KEYS - 4, 4, store)
            for k in range(KEYS - 4, KEYS - 1):
                store(k // 4, k % 4)
            for k in range(4):
                if k == 1:
                    store(KEYS // 4 - 1, 3)
                sp.wait_ge(spill_sem(k), 16 + 16 * (KEYS // 4))
                sp.dma_start(HR[:, k * SEQ:(k + 1) * SEQ], act_dram(0, k)).then_inc(spill_sem(k), 16)

            def fetch(k0, i, r):
                q = (k0 + r + 3) % 4
                sp.wait_ge(y_new, at(k0, i, r, 4))
                sp.dma_start(HR[:, q * SEQ:(q + 1) * SEQ], act_dram(i, r, k0 + 3)).then_inc(spill_sem(q), 16)

            load(sp, N_V + lead, 0, 0, 4)

            fetch(1, 0, 0)

            def fetch_and_load(i, r):
                fetch(2, i, r)
                load(sp, N_V + lead + 1, i, r, 4)

            steps(sp, KEYS - 5, 4, fetch_and_load)
            load(sp, N_V + lead + KEYS - 4, 0, 0, 4)
            for n in range(N_V + lead + KEYS - 3, N_V + lead + KEYS):
                load(sp, n, 0, 0, 4)

        def pe_rest(pe):
            pe_peer(pe)
            pe_block2(pe)

        def act_rest(act, chain):
            act_peer(act, chain)
            act_block2(act, chain)

        def dve_rest(dve, chain):
            dve_peer(dve, chain)
            dve_block2(dve, chain)

        def pool_rest(pool, chain):
            pool_peer(pool, chain)
            pool_block2(pool, chain)

        def rest_of_kernel_loads(sp):
            sp_peer_loads(sp)
            sp_block2(sp)

        GROW = arena[:, 0:D]
        B0 = 7 * D
        c = Carve(B0)
        FG, QQ, KK, CUM, VT, GS = (c(HG_H * SEQ) for _ in range(6))
        QK = [c(HG_H * SEQ), c(HG_H * SEQ)]
        PP = c(HG_H * SEQ)
        CR = c(HG_H * P)
        MASK = c(len(LEVELS) * P)
        ONR = c(P)
        LBE = c(16)
        LBM, LBS, LB, LB1 = (c(8) for _ in range(4))
        OSS, OMS, ORT, ORS = (c(16) for _ in range(4))
        OO, OSQ, OT = QK[0], QK[1], QQ

        O_ORDER = (0, 2, 1, 3)

        def pe_hgrn(pe):
            norm_pe(pe, 3)
            up(pe, N_HG, U_HG, 0, 0, 4, SEQ, x_ready=nlo_before(3))
            steps(pe, 15, 4, lambda i, r: up(pe, N_HG + 1, U_HG + 1, i, r, 4, SEQ))

            def level(x):
                if x < 8:
                    pe.wait_ge(s("qk_q"), x + 1)
                    pe.wait_ge(s("qk_k"), x + 1)
                if x:
                    pe.wait_ge(s("level_out"), 4 * x)
                qk = QK[x % 2]
                if x == 0:
                    for hd in range(HG_H):
                        nc.tensor.matmul(bank[4 + hd // 4][:, (hd % 4) * P:(hd % 4 + 1) * P],
                                         qk[:, hd * SEQ:hd * SEQ + P], qk[:, hd * SEQ + P:(hd + 1) * SEQ],
                                         start=True, stop=True).then_inc(s("level_mm"), 2)
                    return
                for hc in range(2 * HG_H):
                    q = slice(hc * P, (hc + 1) * P)
                    a, b = (KK[:, q], QQ[:, q]) if x == 8 else (qk[:, q], qk[:, q])
                    nc.tensor.matmul(bank[4 + hc // 4][:, (hc % 4) * P:(hc % 4 + 1) * P], a, b,
                                     start=True, stop=True).then_inc(s("level_mm"), 1)

            pe.wait_ge(up_evac, U_HG + 16 + 2)
            for k in range(16):
                if k == 8:
                    pe.wait_ge(s("v_out"), 4)
                up_wide(pe, N_HG + 16 + k // 8 * 8, k % 8)
                if k % 2:
                    level(k // 2)
            level(8)
            pe.wait_ge(s("level_out"), 4 * 9)
            for tt in range(TT):
                for hd in range(HG_H):
                    o = bank[4 + 2 * tt + hd // 4][:, (hd % 4) * P:(hd % 4 + 1) * P]
                    v = lambda half: VT[:, half * D + hd * P:half * D + (hd + 1) * P]
                    if tt == 0:
                        last = nc.tensor.matmul(o, PP[:, hd * SEQ:hd * SEQ + P], v(0), start=True, stop=True)
                    else:
                        nc.tensor.matmul(o, CR[:, hd * P:(hd + 1) * P], v(0), start=True, stop=False)
                        last = nc.tensor.matmul(o, PP[:, hd * SEQ + P:(hd + 1) * SEQ], v(1), start=False, stop=True)
                    if hd % 4 == 3:
                        last.then_inc(s("o_mm"), 1)
            pe.wait_ge(s("g_out"), 4)
            for x, b in enumerate(O_ORDER):
                pe.wait_ge(s("o_gated"), x + 1)
                tt, hh = b // 2, b % 2
                for j in range(4 * hh, 4 * hh + 4):
                    last = nc.tensor.transpose(bank[j // 2][:, (j % 2) * SEQ + tt * P:(j % 2) * SEQ + (tt + 1) * P],
                                               OO[:, tt * D + j * P:tt * D + (j + 1) * P], ident[:, :])
                    if tt and j % 2:
                        last.then_inc(s("o_tr"), 1)
            clear_accumulators(pe, 2)
            down_pe(pe, 2, N_HGO, D_HGO, 8)

        def act_hgrn(act, chain):
            norm_act_sums(act, 2, lambda tt: act.wait_ge(h_done, h_count("v", tt)))
            norm_act_sums(act, 3, lambda tt: act.wait_ge(s("x2"), tt + 1))
            norm_act_tokens(act, 3)
            norm_act_hi(act, 3, "hg_norm")
            act.wait_ge(s("lb_x"), 2)
            nc.scalar.activation(LBE, LBE, ACT.Exp).then_inc(s("lb_e"), 1)
            for j in range(8):
                split_hi(act, N_HG + j + AHEAD, 0, 0, 4)
                act.wait_ge(slabs_done, N_HG + j + 1 + RING)
                nc.scalar.activation(FG[:, j * SEQ:(j + 1) * SEQ], bank[(U_HG + j) % 2][:, 0:SEQ], ACT.Sigmoid)\
                    .then_inc(up_evac, 1)
            for j in range(8):
                split_hi(act, N_HG + 8 + j + AHEAD, 0, 0, 4)
                if j == 1:
                    act.wait_ge(s("keys"), 8)
                    nc.scalar.activation(FG, FG, ACT.Ln).then_inc(s("logf"), 1)
                if j == 4:
                    act.wait_ge(up_evac, U_HG + 12 + 2)
                if j >= 4:
                    act.wait_ge(slabs_done, N_HG + 8 + j + 1 + RING)
                    nc.scalar.activation(QQ[:, j * SEQ:(j + 1) * SEQ], bank[(U_HG + j) % 2][:, 0:SEQ], ACT.Silu)\
                        .then_inc(up_evac, 1)
                if j == 5:
                    nc.scalar.activation(QQ[:, 0:4 * SEQ], QQ[:, 0:4 * SEQ], ACT.Silu).then_inc(s("q_silu"), 1)

            def level_exp(x):
                m = (P,) + LEVELS[:-1]
                m = m[x]
                act.wait_ge(s("dcum"), x + 1)
                e = QK[x % 2].rearrange("p (b w) -> p b w", w=2 * m)
                nc.scalar.activation(e[:, :, m:2 * m], e[:, :, m:2 * m], ACT.Exp).then_inc(s("e_q"), 1)
                nc.scalar.activation(e[:, :, 0:m], e[:, :, 0:m], ACT.Exp, scale=-1.0).then_inc(s("e_k"), 1)

            for k in range(16):
                if k % 2 == 0:
                    level_exp(k // 2)
                split_hi(act, N_HG + 16 + k + AHEAD, 0, 0, 4)
                if k == 7:
                    act.wait_ge(slabs_done, N_HG + 16 + 8 + RING)
                    for b in range(4):
                        nc.scalar.activation(VT[:, b * 512:(b + 1) * 512], bank[b][:, :], ACT.Copy)\
                            .then_inc(s("v_out"), 1)
            act.wait_ge(slabs_done, N_HG + 32 + RING)
            for b in O_ORDER:
                nc.scalar.activation(GS[:, b * 512:(b + 1) * 512], bank[b][:, :], ACT.Silu).then_inc(s("g_out"), 1)
            nc.scalar.activation(tiny[:, 28:29], V("one"), ACT.Sqrt)
            for b in range(4):
                act.wait_ge(s("o_mm"), b + 1)
                nc.scalar.activation(OSQ[:, b * 512:(b + 1) * 512], bank[4 + b][:, :], ACT.Square)\
                    .then_inc(s("o_sq"), 1)
            act.wait_ge(s("o_ms"), 1)
            nc.scalar.activation(ORT, OMS, ACT.Sqrt).then_inc(s("o_rt"), 1)
            for b in range(4):
                act.wait_ge(s("o_tr"), b + 1)
                nc.scalar.activation(OT[:, b * 512:(b + 1) * 512], bank[b][:, :], ACT.Copy).then_inc(s("ot"), 1)
            act.wait_ge(s("ot"), 4)
            down_act(act, N_HGO, D_HGO, 8, OT)

        def k_side(ops, eng, x):
            m = ((P,) + LEVELS[:-1])[x]
            eng.wait_ge(s("e_k"), x + 1)
            e = QK[x % 2].rearrange("p (b w) -> p b w", w=2 * m)
            k3 = KK.rearrange("p (b w) -> p b w", w=2 * m)
            ops.tensor_tensor(e[:, :, 0:m], e[:, :, 0:m], k3[:, :, 0:m], ALU.mult).then_inc(s("qk_k"), 1)

        def dve_hgrn(dve, chain):
            norm_dve_scale(dve, 2)
            dve.wait_ge(s("row_in"), 16)
            dve.wait_ge(rs_done, 3)
            for tt in range(TT):
                q = slice(tt * D, (tt + 1) * D)
                nc.vector.scalar_tensor_tensor(out=h[:, q], in0=h[:, q], scalar=RS[:, tt:tt + 1], in1=GROW,
                                               op0=ALU.mult, op1=ALU.mult).then_inc(s("x2"), 1)
            dve.wait_ge(s("x2"), 2)
            norm_dve_scale(dve, 3)
            norm_dve_tokens(dve, 3)
            norm_dve_lo(dve, 3, "hg_norm")
            l0, l1 = V("lb_logits", 0, 8), V("lb_logits", 8, 8)
            chain.link(nc.vector.tensor_tensor(LBM, l0, l1, ALU.max))
            nc.vector.tensor_tensor(LBE[:, 0:8], l0, LBM, ALU.subtract).then_inc(s("lb_x"), 1)
            nc.vector.tensor_tensor(LBE[:, 8:16], l1, LBM, ALU.subtract).then_inc(s("lb_x"), 1)
            dve.wait_ge(s("lb_e"), 1)
            chain.link(nc.vector.tensor_tensor(LBS, LBE[:, 0:8], LBE[:, 8:16], ALU.add))
            chain.link(nc.vector.reciprocal(LBS, LBS))
            chain.link(nc.vector.tensor_tensor(LB, LBE[:, 0:8], LBS, ALU.mult))
            chain.link(nc.vector.tensor_scalar(LB1, LB, -1.0, 1.0, ALU.mult, ALU.add))

            def forget(j):
                dve.wait_ge(up_evac, U_HG + j + 1 + 2)
                f = slice(j * SEQ, (j + 1) * SEQ)
                nc.vector.tensor_scalar(FG[:, f], FG[:, f], LB1[:, j:j + 1], LB[:, j:j + 1], ALU.mult, ALU.add)\
                    .then_inc(s("forget"), 1)
                dve.wait_ge(s("forget"), j + 1)
                nc.vector.tensor_scalar(KK[:, f], FG[:, f], 1.0, -float(P) ** -0.5, ALU.subtract, ALU.mult)\
                    .then_inc(s("keys"), 1)

            for j in range(8):
                split_lo(dve, N_HG + j + AHEAD, 0, 0, 4)
                if j:
                    forget(j - 1)
            forget(7)
            for j in range(8):
                split_lo(dve, N_HG + 8 + j + AHEAD, 0, 0, 4)
                if j < 4:
                    if j == 0:
                        dve.wait_ge(up_evac, U_HG + 8 + 2)
                    dve.wait_ge(slabs_done, N_HG + 8 + j + 1 + RING)
                    nc.vector.tensor_copy(QQ[:, j * SEQ:(j + 1) * SEQ], bank[(U_HG + j) % 2][:, 0:SEQ])\
                        .then_inc(up_evac, 1)
                if j == 3:
                    dve.wait_ge(s("logf"), 1)
                    for hd in range(HG_H):
                        q = slice(hd * SEQ, (hd + 1) * SEQ)
                        nc.vector.tensor_tensor_scan(CUM[:, q], V("one").to_broadcast([P, SEQ]), FG[:, q], 0.0,
                                                     ALU.mult, ALU.add).then_inc(s("cum"), 1)

            def q_side(x):
                m = ((P,) + LEVELS[:-1])[x]
                dve.wait_ge(s("e_q"), x + 1)
                e = QK[x % 2].rearrange("p (b w) -> p b w", w=2 * m)
                q3 = QQ.rearrange("p (b w) -> p b w", w=2 * m)
                nc.vector.tensor_tensor(e[:, :, m:2 * m], e[:, :, m:2 * m], q3[:, :, m:2 * m], ALU.mult)\
                    .then_inc(s("qk_q"), 1)

            def take(x):
                if x == 0:
                    for b in range(2):
                        dve.wait_ge(s("level_mm"), 8 * (b + 1))
                        nc.vector.tensor_copy(CR[:, b * 512:(b + 1) * 512], bank[4 + b][:, :])\
                            .then_inc(s("level_out"), 2)
                    return
                dve.wait_ge(s("masks"), 16)
                for b in range(4):
                    dve.wait_ge(s("level_mm"), 16 * x + 4 * (b + 1))
                    if x > 1:
                        dve.wait_ge(s("level_out"), 4 * (x - 1) + b + 1)
                    nc.vector.copy_predicated(
                        PP[:, b * 512:(b + 1) * 512].rearrange("p (c t) -> p c t", t=P),
                        MASK[:, (x - 1) * P:x * P].bitcast(U32).unsqueeze(1).to_broadcast([P, 4, P]),
                        bank[4 + b][:, :].rearrange("p (c t) -> p c t", t=P)).then_inc(s("level_out"), 1)

            dve.wait_ge(up_evac, U_HG + 16 + 2)
            dve.wait_ge(s("q_silu"), 1)
            dve.wait_ge(s("scores_zero"), 1)
            for k in range(16):
                if k % 2 == 0:
                    if k:
                        take(k // 2 - 1)
                    q_side(k // 2)
                    if k == 0:
                        k_side(nc.vector, dve, 0)
                split_lo(dve, N_HG + 16 + k + AHEAD, 0, 0, 4)
            take(7)
            take(8)
            for b in range(4):
                dve.wait_ge(s("o_sq"), b + 1)
                nc.vector.tensor_reduce(OSS[:, 4 * b:4 * b + 4],
                                        OSQ[:, b * 512:(b + 1) * 512].rearrange("p (h d) -> p h d", d=P),
                                        AX.X, ALU.add).then_inc(s("o_ss"), 1)
            dve.wait_ge(s("o_ss"), 4)
            nc.vector.tensor_scalar(OMS, OSS, 1.0 / P, EPS, ALU.mult, ALU.add).then_inc(s("o_ms"), 1)
            dve.wait_ge(s("o_rt"), 1)
            chain.link(nc.vector.reciprocal(ORS, ORT))
            dve.wait_ge(s("gg"), 1)

            def normed(b):
                q = slice(b * 512, (b + 1) * 512)
                nc.vector.tensor_tensor(
                    OO[:, q].rearrange("p (h d) -> p h d", d=P), bank[4 + b][:, :].rearrange("p (h d) -> p h d", d=P),
                    ORS[:, 4 * b:4 * b + 4].unsqueeze(2).to_broadcast([P, 4, P]), ALU.mult).then_inc(s("o_norm"), 1)

            normed(O_ORDER[0])
            for x, b in enumerate(O_ORDER):
                if x < 3:
                    normed(O_ORDER[x + 1])
                q = slice(b * 512, (b + 1) * 512)
                dve.wait_ge(s("o_norm"), x + 1)
                nc.vector.tensor_tensor(OO[:, q], OO[:, q], GS[:, q], ALU.mult).then_inc(s("o_gated"), 1)
            dve.wait_ge(s("ot"), 4)
            down_dve(dve, N_HGO, D_HGO, 8, OT)
            add_dve(dve, "hgo", N_HGO + 7, D_HGO + 7)

        def pool_hgrn(pool, chain):
            pool.wait_ge(y_new, KEYS)
            pool.dma_start(GROW, t["g_final"]).then_inc(s("row_in"), 16)
            pool.dma_start(MASK, t["tables"][:, TAB_LEVEL:TAB_LEVEL + len(LEVELS) * P]).then_inc(s("masks"), 16)
            pool.dma_start(ONR, t["hg_out_norm"]).then_inc(s("onr_in"), 16)
            nc.gpsimd.memset(PP, 0.0).then_inc(s("scores_zero"), 1)
            pool.wait_ge(s("cum"), 8)
            pool.wait_ge(s("keys"), 8)

            def differences(x):
                m = ((P,) + LEVELS[:-1])[x]
                if x >= 2:
                    pool.wait_ge(s("level_mm"), 16 * (x - 1))
                c3 = CUM.rearrange("p (b w) -> p b w", w=2 * m)
                nc.gpsimd.tensor_tensor(QK[x % 2].rearrange("p (b w) -> p b w", w=2 * m), c3,
                                        c3[:, :, m - 1:m].to_broadcast([P, HG_H * SEQ // (2 * m), 2 * m]),
                                        ALU.subtract).then_inc(s("dcum"), 1)

            differences(0)
            for x in range(8):
                if x:
                    pool.wait_ge(s("qk_k"), x)
                    k_side(nc.gpsimd, pool, x)
                if x < 7:
                    differences(x + 1)
            pool.wait_ge(s("g_out"), 4)
            pool.wait_ge(s("onr_in"), 16)
            g3 = GS.rearrange("p (h d) -> p h d", d=P)
            nc.gpsimd.tensor_tensor(g3, g3, ONR.unsqueeze(1).to_broadcast([P, 2 * HG_H, P]), ALU.mult)\
                .then_inc(s("gg"), 1)

        FFN = ((N_FF0, U_FF0, D_FF0, 4, 3, "ff0"), (N_FF1, U_FF1, D_FF1, 6, 5, "ff1"))
        c = Carve(B0)
        CVF = c(2 * SEQ)
        SG = c(2 * SEQ)
        YB = c(2 * SEQ)

        def ffn_steps(f, body):
            n0, u0, d0 = FFN[f][:3]

            def step(i, r):
                body(n0 + 2 + 3 * r, u0 + 2 + 2 * r, d0 + 1 + r, i, 1 + r)

            return step

        def pe_ffn(pe, f):
            n0, u0, d0, r0, st, _ = FFN[f]
            norm_pe(pe, r0)
            up(pe, n0, u0, 0, 0, 12, SEQ, x_ready=nlo_before(r0))
            clear_accumulators(pe, st)
            up(pe, n0 + 1, u0 + 1, 0, 0, 12, SEQ)

            def body(n, u, d, i, j):
                up(pe, n, u, i, 0, 12, SEQ, uU=8)
                up(pe, n + 1, u + 1, i, 0, 12, SEQ, uU=8)
                down(pe, n + 2, d - 1, i, 0, 12, dU=4)

            steps(pe, FF_T - 1, 4, ffn_steps(f, body))
            down(pe, n0 + 3 * FF_T - 1, d0 + FF_T - 1, 0, 0, 4)

        def act_ffn(act, f):
            n0, u0, d0, r0, _, before = FFN[f][:5] + ({0: "hgo", 1: "wo"}[f],)
            cb = XBC_T + FF_T * f
            norm_act_sums(act, r0, lambda tt: act.wait_ge(h_done, h_count(before, tt)))
            norm_act_tokens(act, r0)
            norm_act_hi(act, r0, f"ffn_norm{f}")

            def body(n, u, d, i, j, first=False):
                x = d - d0 + i * 4
                b = (d - d0) % 2
                split_hi(act, n + AHEAD, i, 0, 12)
                act.wait_ge(slabs_done, n + i * 12 + 1 + RING)
                act.wait_ge(silu_done, cb + x + 1)
                nc.scalar.activation(CVF[:, b * SEQ:(b + 1) * SEQ], bank[u % 2][:, 0:SEQ], ACT.Identity,
                                     scale=V(f"fconv_w{f}", x * 3 + 2), bias=V(f"fconv_b{f}", x))\
                    .then_inc(conv_begun, 1)
                split_hi(act, n + 1 + AHEAD, i, 0, 12)
                act.wait_ge(up_evac, u + i * 8 + 1 + 2)
                nc.scalar.activation(SG[:, b * SEQ:(b + 1) * SEQ], CVF[:, b * SEQ:(b + 1) * SEQ], ACT.Silu)\
                    .then_inc(silu_done, 1)
                if not first:
                    split_hi(act, n + 2 + AHEAD, i, 0, 12)
                act.wait_ge(up_evac, u + i * 8 + 2 + 2)
                if first:
                    act.wait_ge(slabs_done, n0)
                else:
                    act.wait_ge(slabs_done, n + i * 12 + RING)
                yq = d % 2
                nc.scalar.activation(yhi[:, yq * SEQ:(yq + 1) * SEQ], YB[:, b * SEQ:(b + 1) * SEQ], ACT.Copy)\
                    .then_inc(y_hi, 1)

            body(n0, u0, d0, 0, 0, True)
            steps(act, FF_T - 1, 4, ffn_steps(f, body))
            split_hi(act, n0 + 3 * FF_T - 1 + AHEAD, 0, 0, 4)

        def dve_ffn(dve, f, chain):
            n0, u0, d0, r0, _, name = FFN[f]
            cb = XBC_T + FF_T * f
            norm_dve_scale(dve, r0)
            norm_dve_tokens(dve, r0)
            norm_dve_lo(dve, r0, f"ffn_norm{f}")

            def body(n, u, d, i, j, first=False):
                x = d - d0 + i * 4
                b = (d - d0) % 2
                split_lo(dve, n + AHEAD, i, 0, 12)
                dve.wait_ge(conv_begun, cb + x + 1)
                for sh in (1, 2):
                    ins = nc.vector.scalar_tensor_tensor(
                        out=CVF[:, b * SEQ + sh:(b + 1) * SEQ], in0=bank[u % 2][:, 0:SEQ - sh],
                        scalar=V(f"fconv_w{f}", x * 3 + 2 - sh), in1=CVF[:, b * SEQ + sh:(b + 1) * SEQ],
                        op0=ALU.mult, op1=ALU.add)
                    if sh == 1:
                        chain.link(ins)
                ins.then_inc(up_evac, 1)
                split_lo(dve, n + 1 + AHEAD, i, 0, 12)
                dve.wait_ge(slabs_done, n + i * 12 + 2 + RING)
                dve.wait_ge(silu_done, cb + x + 1 + 2)
                y = YB[:, b * SEQ:(b + 1) * SEQ]
                nc.vector.tensor_tensor(y, SG[:, b * SEQ:(b + 1) * SEQ], bank[(u + 1) % 2][:, 0:SEQ],
                                        ALU.mult).then_inc(up_evac, 1)
                if not first:
                    split_lo(dve, n + 2 + AHEAD, i, 0, 12)
                yq = d % 2
                dve.wait_ge(y_hi, d + i * 4 + 1)
                nc.vector.tensor_tensor(ylo[:, yq * SEQ:(yq + 1) * SEQ], y,
                                        yhi[:, yq * SEQ:(yq + 1) * SEQ].bitcast(F32), ALU.subtract)\
                    .then_inc(y_lo, 1)

            body(n0, u0, d0, 0, 0, True)
            steps(dve, FF_T - 1, 4, ffn_steps(f, body), chain, 1)
            add_dve(dve, name, n0 + 3 * FF_T - 1, d0 + FF_T - 1)

        c = Carve(B0)
        KTA = c(2 * SEQ)
        VTA = c(TT * P)
        QA = c(8 * SEQ)
        DIST = c(3 * P)
        SCO = c(ATT_H * 3 * P)
        PT = c(2 * 3 * P)
        ATT = c(8 * SEQ)
        SK8 = c(ATT_H)
        MX, NM, SM, SE, RD = (c(2 * ATT_H) for _ in range(5))
        W3 = 3 * P
        SCALE = float(ATT_D) ** -0.5

        def pe_attn(pe):
            norm_pe(pe, 5)
            up(pe, N_ATT, U_ATT, 0, 0, 4, SEQ, x_ready=nlo_before(5))
            up(pe, N_ATT + 1, U_ATT + 1, 0, 0, 4, SEQ)
            up_tokens(pe, N_ATT + 2, U_ATT + 2, 0, 0, 4)
            up(pe, N_ATT + 3, U_ATT + 3, 0, 0, 4, SEQ, x_ready=nlo_total(5, 1) - KT)
            steps(pe, 7, 4, lambda i, r: up(pe, N_ATT + 4, U_ATT + 4, i, r, 4, SEQ))
            pe.wait_ge(up_evac, U_ATT + 11 + 2)

            def scores(g):
                for x in range(4):
                    hd = 4 * g + x
                    if g:
                        pe.wait_ge(s("sco"), 4 * (g - 1) + x + 1)
                    p = slice((hd % 2) * 64, (hd % 2) * 64 + 64)
                    q = QA[p, (hd // 2) * SEQ:(hd // 2 + 1) * SEQ]
                    kk = KTA[p, (hd // 8) * SEQ:(hd // 8 + 1) * SEQ]
                    nc.tensor.matmul(bank[x][:, 0:P], q[:, 0:P], kk[:, 0:P], start=True, stop=True)
                    nc.tensor.matmul(bank[x][:, P:W3], q[:, P:SEQ], kk[:, :], start=True, stop=True)\
                        .then_inc(s("sc_mm"), 1)

            def transposes(hd):
                pe.wait_ge(s("probs"), 2 * (hd // 4) + 2)
                if hd >= 2:
                    pe.wait_ge(s("pt"), hd - 1)
                src = SCO[:, hd * W3:(hd + 1) * W3]
                for y in range(3):
                    last = nc.tensor.transpose(bank[4 + hd % 2][:, y * P:(y + 1) * P], src[:, y * P:(y + 1) * P],
                                               ident[:, :])
                last.then_inc(s("p_tr"), 1)

            def values(hd):
                pe.wait_ge(s("pt"), hd + 1)
                j = hd // 2
                if hd % 2 == 0 and j >= 2:
                    pe.wait_ge(s("att"), j - 1)
                p = PT[:, (hd % 2) * W3:(hd % 2 + 1) * W3]
                po = (hd % 2) * 64
                o = bank[6 + j % 2]
                v = lambda tt: VTA[:, tt * P + (hd // 8) * 64:tt * P + (hd // 8) * 64 + 64]
                nc.tensor.matmul(o[po:po + 64, 0:P], v(0), p[:, 0:P], start=True, stop=True)
                nc.tensor.matmul(o[po:po + 64, P:SEQ], v(0), p[:, P:2 * P], start=True, stop=False)
                nc.tensor.matmul(o[po:po + 64, P:SEQ], v(1), p[:, 2 * P:W3], start=False, stop=True)\
                    .then_inc(s("pv"), 1)

            scores(0)
            scores(1)
            for g in range(4):
                if g < 2:
                    scores(g + 2)
                for x in range(4):
                    transposes(4 * g + x)
                    if 4 * g + x:
                        values(4 * g + x - 1)
            values(ATT_H - 1)
            pe.wait_ge(s("att"), 8)
            clear_accumulators(pe, 4)
            down_pe(pe, 4, N_WO, D_WO, 8)

        def act_attn(act, chain):
            norm_act_sums(act, 5, lambda tt: act.wait_ge(h_done, h_count("ff0", tt)))
            norm_act_tokens(act, 5)
            norm_act_hi(act, 5, "kv_norm")
            for k in range(2):
                split_hi(act, N_ATT + k + AHEAD, 0, 0, 4)
                act.wait_ge(slabs_done, N_ATT + k + 1 + RING)
                nc.scalar.activation(KTA[:, k * SEQ:(k + 1) * SEQ], bank[(U_ATT + k) % 2][:, 0:SEQ], ACT.Copy)\
                    .then_inc(up_evac, 1)
            split_hi(act, N_ATT + 2 + AHEAD, 0, 0, 4)
            act.wait_ge(slabs_done, N_ATT + 3 + RING)
            nc.scalar.activation(VTA, bank[(U_ATT + 2) % 2][:, 0:SEQ], ACT.Copy).then_inc(up_evac, 1)
            norm_act_hi(act, 5, "attn_norm", 1)
            for k in range(8):
                n = N_ATT + 3 + k
                split_hi(act, n + AHEAD, 0, 0, 4)
                act.wait_ge(slabs_done, n + 1 + RING)
                nc.scalar.activation(QA[:, k * SEQ:(k + 1) * SEQ], bank[(U_ATT + 3 + k) % 2][:, 0:SEQ], ACT.Copy)\
                    .then_inc(up_evac, 1)

            def softmax(g):
                act.wait_ge(s("negmax"), 2 * g + 2)
                b8 = slice(g * 8, g * 8 + 8)
                nc.scalar.activation(SE[:, b8], SE[:, b8], ACT.Exp, scale=SCALE).then_inc(s("sink_e"), 1)
                for x in range(4):
                    sc = SCO[:, (4 * g + x) * W3:(4 * g + x + 1) * W3]
                    for b, q in ((0, slice(0, P)), (1, slice(P, W3))):
                        col1 = g * 8 + 2 * x + b
                        nc.scalar.activation(sc[:, q], sc[:, q], ACT.Exp, scale=SCALE, bias=NM[:, col1:col1 + 1],
                                             accum_out=SM[:, col1:col1 + 1]).then_inc(s("exps"), 1)

            def copies(g):
                for x in range(4):
                    hd = 4 * g + x
                    act.wait_ge(s("p_tr"), hd + 1)
                    if hd >= 2:
                        act.wait_ge(s("pv"), hd - 1)
                    nc.scalar.activation(PT[:, (hd % 2) * W3:(hd % 2 + 1) * W3], bank[4 + hd % 2][:, 0:W3], ACT.Copy)\
                        .then_inc(s("pt"), 1)

            softmax(0)
            for g in range(4):
                if g < 3:
                    softmax(g + 1)
                copies(g)
            act.wait_ge(s("att"), 8)
            down_act(act, N_WO, D_WO, 8, ATT)

        def normalise(ops, eng, g):
            eng.wait_ge(s("sum_inv"), g + 1)
            s3 = SCO[:, g * 4 * W3:(g + 1) * 4 * W3].rearrange("p (h w) -> p h w", w=W3)
            r3 = RD[:, g * 8:g * 8 + 8].rearrange("p (h b) -> p h b", b=2)
            for b, q in ((0, slice(0, P)), (1, slice(P, W3))):
                ops.tensor_tensor(s3[:, :, q], s3[:, :, q], r3[:, :, b:b + 1].to_broadcast([P, 4, q.stop - q.start]),
                                  ALU.mult).then_inc(s("probs"), 1)

        def dve_attn(dve, chain):
            norm_dve_scale(dve, 5)
            norm_dve_tokens(dve, 5)
            norm_dve_lo(dve, 5, "kv_norm")
            for k in range(3):
                split_lo(dve, N_ATT + k + AHEAD, 0, 0, 4)
            norm_dve_lo(dve, 5, "attn_norm", 1)
            for k in range(8):
                split_lo(dve, N_ATT + 3 + k + AHEAD, 0, 0, 4)
            chain.link(nc.vector.tensor_scalar(SK8, V("sinks", 0, ATT_H), 1.0 / SCALE, None, ALU.mult))
            dve.wait_ge(s("dist_in"), 16)

            def stats(g):
                base = g * 4 * W3
                for x in range(4):
                    hd = 4 * g + x
                    dve.wait_ge(s("sc_mm"), hd + 1)
                    slope = 2.0 ** (-8.0 * (hd + 1) / ATT_H)
                    nc.vector.scalar_tensor_tensor(out=SCO[:, base + x * W3:base + (x + 1) * W3], in0=DIST,
                                                   scalar=-slope / SCALE, in1=bank[x][:, 0:W3],
                                                   op0=ALU.mult, op1=ALU.add).then_inc(s("sco"), 1)
                dve.wait_ge(s("sco"), 4 * g + 4)
                b8 = slice(g * 8, g * 8 + 8)
                s3 = SCO[:, base:base + 4 * W3].rearrange("p (h w) -> p h w", w=W3)
                m3 = MX[:, b8].rearrange("p (h b) -> p h b", b=2)
                chain.inc(nc.vector.tensor_reduce(m3[:, :, 0:1], s3[:, :, 0:P], AX.X, ALU.max))
                chain.link(nc.vector.tensor_reduce(m3[:, :, 1:2], s3[:, :, P:W3], AX.X, ALU.max))
                sk = SK8[:, 4 * g:4 * g + 4].unsqueeze(2).to_broadcast([P, 4, 2])
                chain.link(nc.vector.tensor_tensor(m3, m3, sk, ALU.max))
                nc.vector.tensor_tensor(SE[:, b8].rearrange("p (h b) -> p h b", b=2), sk, m3, ALU.subtract)\
                    .then_inc(s("negmax"), 1)
                nc.vector.tensor_scalar(NM[:, b8], MX[:, b8], -SCALE, None, ALU.mult).then_inc(s("negmax"), 1)

            def divide(g):
                b8 = slice(g * 8, g * 8 + 8)
                dve.wait_ge(s("sink_e"), g + 1)
                dve.wait_ge(s("exps"), 8 * (g + 1))
                chain.link(nc.vector.tensor_tensor(RD[:, b8], SM[:, b8], SE[:, b8], ALU.add))
                nc.vector.reciprocal(RD[:, b8], RD[:, b8]).then_inc(s("sum_inv"), 1)
                if g == 3:
                    dve.wait_ge(s("probs"), 6)
                    normalise(nc.vector, dve, g)

            def outputs(g):
                for j in (2 * g, 2 * g + 1):
                    dve.wait_ge(s("pv"), 2 * j + 2)
                    nc.vector.tensor_copy(ATT[:, j * SEQ:(j + 1) * SEQ], bank[6 + j % 2][:, 0:SEQ])\
                        .then_inc(s("att"), 1)

            stats(0)
            stats(1)
            for g in range(4):
                divide(g)
                if g < 2:
                    stats(g + 2)
                if g:
                    outputs(g - 1)
            outputs(3)
            dve.wait_ge(s("att"), 8)
            down_dve(dve, N_WO, D_WO, 8, ATT)
            add_dve(dve, "wo", N_WO + 7, D_WO + 7)

        def dve_output(dve):
            norm_dve_scale(dve, 7)
            dve.wait_ge(rs_done, 8)
            dve.wait_ge(s("row_in"), 32)
            for tt in range(TT):
                q = slice(tt * D, (tt + 1) * D)
                nc.vector.scalar_tensor_tensor(out=nt[:, q], in0=h[:, q], scalar=RS[:, tt:tt + 1], in1=GROW,
                                               op0=ALU.mult, op1=ALU.mult).then_inc(s("out_ready"), 1)

        def pe_block2(pe):
            pe_hgrn(pe)
            pe_ffn(pe, 0)
            pe_attn(pe)
            pe_ffn(pe, 1)

        def act_block2(act, chain):
            act_hgrn(act, chain)
            act_ffn(act, 0)
            act_attn(act, chain)
            act_ffn(act, 1)
            norm_act_sums(act, 7, lambda tt: act.wait_ge(h_done, h_count("ff1", tt)))

        def dve_block2(dve, chain):
            dve_hgrn(dve, chain)
            dve_ffn(dve, 0, chain)
            dve_attn(dve, chain)
            dve_ffn(dve, 1, chain)
            dve_output(dve)

        def pool_block2(pool, chain):
            pool_hgrn(pool, chain)
            pool.wait_ge(s("gg"), 1)
            pool.wait_ge(h_done, h_count("hgo"))
            pool.dma_start(GROW, t["final_norm"]).then_inc(s("row_in"), 16)
            pool.wait_ge(h_done, h_count("ff0"))
            pool.dma_start(DIST, t["tables"][:, TAB_DIST:TAB_DIST + W3]).then_inc(s("dist_in"), 16)
            for g in range(3):
                normalise(nc.gpsimd, pool, g)

        def sp_block2(sp):
            done = N_V + KEYS + RING + AHEAD
            steps(sp, N_SLABS - done, 4, lambda i, r: load(sp, done, i, r, 4))

        @block.sync
        def _(sp):
            sp.dma_start(h[:, :], t["x"]).then_inc(h_in, 16)
            sp.dma_start(meta_x[0:META, :], t["meta"]).then_inc(h_in, 16)
            sp.dma_start(vec[:, :], t["vec"]).then_inc(vec_in, 16)
            sp.dma_start(ident[:, :], t["ident"]).then_inc(vec_in, 16)
            sp.dma_start(iota[:, :], t["iota"]).then_inc(vec_in, 16)
            for n in range(RING):
                load(sp, n, 0, 0, 4)
            rest_of_kernel_loads(sp)
            for tt in range(TT):
                q = slice(tt * D, (tt + 1) * D)
                sp.wait_ge(s("out_ready"), tt + 1)
                sp.dma_start(t["out"][:, q], nt[:, q]).then_inc(out_done, 16)
            sp.wait_ge(out_done, 32)

        @block.tensor
        def _(pe):
            pe.sem_inc(slabs_done, RING)
            pe.sem_inc(up_evac, 2)
            pe.wait_ge(vec_in, 48)
            pe_mixer(pe)
            pe_wout(pe)
            pe_rest(pe)

        @block.scalar
        def _(act):
            act.sem_inc(silu_done, 2)
            chain = Chain(act, act_self)
            act_mixer(act, chain)
            act_wout(act)
            act_rest(act, chain)

        @block.vector
        def _(dve):
            chain = Chain(dve, dve_self)
            dve_setup(dve, chain)
            dve_mixer(dve, chain)
            dve_wout(dve)
            dve_rest(dve, chain)
        @block.gpsimd
        def _(pool):
            chain = Chain(pool, pool_self)
            pool_mixer(pool, chain)
            pool_rest(pool, chain)
def _features(v):
    return v.reshape(-1, P).T


def _up_slabs(w):
    n = w.shape[1] // P
    return w.reshape(KT, P, n, P).transpose(2, 1, 0, 3).reshape(n, P, KT * P)


def _down_slabs(w):
    return w.reshape(-1, P, D)


def _interleave(*parts):
    return np.stack(parts, 1).reshape(-1, P, D)


def _stream(a):
    w_in = a["w_in"][0]
    o = np.cumsum([0, DSSD, DSSD + 2 * GROUPS * NST, HEADS, 512, 512, 512])
    z, xbc, dt, sc_b, sc_c, sc_x = (w_in[:, o[i]:o[i + 1]] for i in range(6))
    dt = np.concatenate([dt, np.zeros((D, P - HEADS), dt.dtype)], 1)
    u = a["expert_u"][0].reshape(KEYS, KEYS, KT, P)
    v = a["expert_v"][0].reshape(KEYS, KEYS, D)
    w_kv = a["w_kv_2"]
    k0, k1, vv = w_kv[:, 0:64], w_kv[:, 64:128], w_kv[:, 128:256]
    hq, hf, hi, hg = (a["hg_w_in_2"][0][:, i * D:(i + 1) * D] for i in range(4))

    def ffn(n):
        w = a["ffn_w_up_2"][n]
        g, x = _up_slabs(w[:, :FF_T * P]), _up_slabs(w[:, FF_T * P:])
        d = _down_slabs(a["ffn_w_down_2"][n])
        mid = _interleave(g[1:], x[1:], d[:-1])
        return [g[:1], x[:1], mid, d[-1:]]

    parts = [_up_slabs(dt), _up_slabs(xbc), _up_slabs(z),
             _interleave(_up_slabs(sc_c), _up_slabs(sc_x), _up_slabs(sc_b)),
             np.roll(_down_slabs(a["w_out"][0]), SC_T, 0), _up_slabs(a["w_q"][0]),
             u.transpose(1, 3, 2, 0).reshape(KEYS, P, KT * P), v.transpose(1, 0, 2),
             _up_slabs(hf), _up_slabs(hq), _down_slabs(hi), _down_slabs(hg), _down_slabs(a["hg_w_out_2"][0]),
             *ffn(0), _up_slabs(np.concatenate([k0, k0, k1, k1, vv], 1)), _up_slabs(a["attn_w_q_2"][0]),
             _down_slabs(a["attn_w_o_2"][0]), *ffn(1)]
    out = np.concatenate(parts, 0)
    assert out.shape[0] == N_SLABS, out.shape
    return out


def _vectors(a):
    def heads(v):
        out = np.zeros((P, 1), v.dtype)
        out[:HEADS, 0] = v
        return out

    def taps(w):
        return w.reshape(w.shape[0], -1, P).transpose(2, 1, 0).reshape(P, -1)

    got = {"g_mix": _features(a["g_mix"][0]), "conv_w": taps(a["conv_ssd_w"][0]),
           "conv_b": _features(a["conv_ssd_b"][0]), "d_skip": _features(np.repeat(a["d_skip"][0], HP)),
           "ssd_norm": _features(a["ssd_norm_w"][0]), "sc_w": taps(a["conv_sc_w"][0]),
           "dt_bias": heads(a["dt_bias"][0]), "a_log": heads(a["a_log"][0]),
           "g_ffn": _features(a["g_ffn"][0]), "hg_norm": _features(a["hg_norm_2"][0]),
           "lb_logits": _features(a["hg_lb_logits_2"].reshape(-1)),
           "ffn_norm0": _features(a["ffn_norm_2"][0]), "ffn_norm1": _features(a["ffn_norm_2"][1]),
           "kv_norm": _features(a["kv_norm_2"]), "attn_norm": _features(a["attn_norm_2"][0]),
           "fconv_w0": taps(a["ffn_conv_w_2"][0]), "fconv_w1": taps(a["ffn_conv_w_2"][1]),
           "fconv_b0": _features(a["ffn_conv_b_2"][0]), "fconv_b1": _features(a["ffn_conv_b_2"][1]),
           "sinks": np.broadcast_to(a["attn_sinks_2"][0][None], (P, ATT_H)),
           "eps": np.full((P, 1), EPS, np.float32), "one": np.ones((P, 1), np.float32)}
    out = np.concatenate([got[n] for n in VEC], 1)
    assert out.shape == (P, NVEC), out.shape
    return out


def _tables():
    p = np.arange(P)[:, None]
    f = np.arange(P)[None, :]
    dist = np.arange(P)[:, None] + P - np.arange(2 * P)[None, :]
    dist = np.where((dist >= 0) & (dist < P), dist, 1e30).astype(np.float32)
    levels = []
    for m in LEVELS:
        if m:
            ok = (p // (2 * m) == f // (2 * m)) & (p // m % 2 == 0) & (f // m % 2 == 1)
        else:
            ok = p == f
        levels.append(ok.astype(np.float32))
    return np.concatenate([(p <= f).astype(np.float32), dist[:, P:], dist, *levels], 1)


def kernel(**inputs):
    import concourse.bacc as bacc
    from concourse.bass_utils import run_bass_kernel_spmd

    a = {k: np.asarray(v) for k, v in inputs.items()}
    tokens = lambda x: x.reshape(-1, P, D).transpose(1, 0, 2).reshape(P, -1)
    rows = lambda v: np.broadcast_to(v[None], (P, v.size))
    arrays = {
        "x": tokens(a["x"][0]), "meta": a["meta_tokens"], "vec": _vectors(a), "tables": _tables(),
        "ident": np.eye(P, dtype=np.float32), "iota": rows(np.arange(P, dtype=np.float32)),
        "stream": _stream(a),
        "keys": a["sub_keys"][0].reshape(2 * PH, KEYS, P).transpose(2, 0, 1).reshape(P, -1),
        "g_final": rows(a["g_final"]), "final_norm": rows(a["final_norm_2"]),
        "hg_out_norm": rows(a["hg_out_norm_2"][0]),
    }
    arrays = {k: np.ascontiguousarray(v) for k, v in arrays.items()}
    nc = bacc.Bacc("TRN2", target_bir_lowering=False, num_devices=1)
    t = {k: nc.dram_tensor(f"in_{k}", v.shape, F32, kind="ExternalInput").ap() for k, v in arrays.items()}
    t["out"] = nc.dram_tensor("out", (P, TT * D), F32, kind="ExternalOutput").ap()
    for name, shape in (("h_spill", (P, TT * D)), ("act_spill", (KEYS, P, SEQ))):
        t[name] = nc.dram_tensor(name, shape, F32, kind="Internal").ap()
    build(nc, t)
    r = run_bass_kernel_spmd(nc, [{f"in_{k}": v for k, v in arrays.items()}], core_ids=[0])
    got = r.results[0]["out"]
    return got.reshape(P, TT, D).transpose(1, 0, 2).reshape(1, SEQ, D)
```
